# Optimizing a Trainium2 kernel written in Bass

```python
import math
import jax, jax.numpy as jnp
from jax import lax
import numpy as np

D_MODEL = 1024
BATCH = 1
SEQ = 512
DEPTH = 1

CHUNK = 64
ATT_HEADS = 8
ATT_KV_HEADS = 2
HEAD_DIM = 64
WINDOW = 128
WIN_CHUNKS = WINDOW // CHUNK
ATT_WIDTH = ATT_HEADS * HEAD_DIM
KV_WIDTH = ATT_KV_HEADS * HEAD_DIM
SSD_INNER = D_MODEL
SSD_HEAD_DIM = 64
SSD_HEADS = SSD_INNER // SSD_HEAD_DIM
SSD_GROUPS = 2
SSD_STATE = 64
CONV_WIDTH = 4
SSD_CONV_DIM = SSD_INNER + 2 * SSD_GROUPS * SSD_STATE
DT_MIN = 0.001
DT_MAX = 0.1
N_EXPERT_GROUPS = 4
EXPERTS_PER_GROUP = 8
N_EXPERTS = N_EXPERT_GROUPS * EXPERTS_PER_GROUP
TOP_K_INNER = 2
D_FF_EXPERT = 256
PLE_DIM = 256
LN_EPS = 1e-5
RMS_EPS = 1e-5
DN_ALPHA = (2 * DEPTH) ** 0.25
DN_BETA = (8 * DEPTH) ** -0.25
NEG_INF = -1e30
IN_PROJ_DIM = ATT_WIDTH + 2 * KV_WIDTH + SSD_INNER + SSD_CONV_DIM + SSD_HEADS + 2 * D_MODEL
IN_SPLITS = (
    ATT_WIDTH,
    ATT_WIDTH + KV_WIDTH,
    ATT_WIDTH + 2 * KV_WIDTH,
    ATT_WIDTH + 2 * KV_WIDTH + SSD_INNER,
    ATT_WIDTH + 2 * KV_WIDTH + SSD_INNER + SSD_CONV_DIM,
    ATT_WIDTH + 2 * KV_WIDTH + SSD_INNER + SSD_CONV_DIM + SSD_HEADS,
)

kernel_name = 'hybrid_swa_ssd_hmoe_deepnorm'

def _layernorm(x, w, b):
    xf = x.astype(jnp.float32)
    mu = jnp.mean(xf, axis=-1, keepdims=True)
    xc = xf - mu
    var = jnp.mean(xc * xc, axis=-1, keepdims=True)
    return (xc * lax.rsqrt(var + LN_EPS) * w.astype(jnp.float32) + b.astype(jnp.float32)).astype(x.dtype)

def _band(xc):
    nc = xc.shape[1]
    pad = jnp.zeros(xc.shape[:1] + (WIN_CHUNKS - 1,) + xc.shape[2:], xc.dtype)
    xp = jnp.concatenate([pad, xc], axis=1)
    return jnp.concatenate([xp[:, j:j + nc] for j in range(WIN_CHUNKS)], axis=2)

def _window_attention(q, k, v, sinks):
    b, s = q.shape[:2]
    nc = s // CHUNK
    grp = ATT_HEADS // ATT_KV_HEADS
    f32 = jnp.float32
    qc = q.reshape(b, nc, CHUNK, ATT_KV_HEADS, grp, HEAD_DIM).astype(f32)
    kb = _band(k.reshape(b, nc, CHUNK, ATT_KV_HEADS, HEAD_DIM)).astype(f32)
    vb = _band(v.reshape(b, nc, CHUNK, ATT_KV_HEADS, HEAD_DIM)).astype(f32)
    scores = jnp.einsum('bcqkgd,bcskd->bkgcqs', qc, kb) * (HEAD_DIM ** -0.5)
    qi = jnp.arange(CHUNK)[:, None]
    kj = jnp.arange(WIN_CHUNKS * CHUNK)[None, :]
    dist = jnp.abs(qi + (WIN_CHUNKS - 1) * CHUNK - kj).astype(f32)
    slopes = jnp.asarray(2.0 ** (-8.0 * np.arange(1, ATT_HEADS + 1) / ATT_HEADS), f32)
    slopes = slopes.reshape(ATT_KV_HEADS, grp, 1, 1, 1)
    ci = jnp.arange(nc)[:, None, None]
    valid = (ci - (WIN_CHUNKS - 1) + kj[None] // CHUNK) >= 0
    scores = jnp.where(valid, scores - slopes * dist, NEG_INF)
    sink = sinks.astype(f32).reshape(ATT_KV_HEADS, grp, 1, 1, 1)
    m = jnp.maximum(jnp.max(scores, axis=-1, keepdims=True), sink)
    e = jnp.exp(scores - m)
    probs = e / (jnp.sum(e, axis=-1, keepdims=True) + jnp.exp(sink - m))
    out = jnp.einsum('bkgcqs,bcskd->bcqkgd', probs, vb)
    return out.reshape(b, s, ATT_WIDTH).astype(q.dtype)

def _ssd(xbc, z, dt_raw, conv_w, conv_b, dt_bias, a_log, d_skip, norm_w):
    b, s = xbc.shape[:2]
    nc = s // CHUNK
    f32 = jnp.float32
    G, R, P, N = SSD_GROUPS, SSD_HEADS // SSD_GROUPS, SSD_HEAD_DIM, SSD_STATE
    conv = lax.conv_general_dilated(
        xbc.astype(f32), conv_w.astype(f32)[:, None, :], window_strides=(1,),
        padding=[(CONV_WIDTH - 1, 0)], dimension_numbers=('NWC', 'WIO', 'NWC'),
        feature_group_count=SSD_CONV_DIM)
    xbc = jax.nn.silu(conv + conv_b.astype(f32))
    xs, bm, cm = jnp.split(xbc, [SSD_INNER, SSD_INNER + G * N], axis=-1)
    xs = xs.reshape(b, nc, CHUNK, G, R, P)
    bm = bm.reshape(b, nc, CHUNK, G, N)
    cm = cm.reshape(b, nc, CHUNK, G, N)
    dt = jax.nn.softplus(dt_raw.astype(f32) + dt_bias.astype(f32)).reshape(b, nc, CHUNK, G, R)
    a = -jnp.exp(a_log.astype(f32)).reshape(G, R)
    acs = jnp.cumsum(jnp.moveaxis(dt * a, 2, -1), axis=-1)
    xdt = xs * dt[..., None]
    causal = jnp.tril(jnp.ones((CHUNK, CHUNK), dtype=bool))
    seg = acs[..., :, None] - acs[..., None, :]
    lmat = jnp.exp(jnp.where(causal, seg, -jnp.inf))
    cb = jnp.einsum('bclgn,bcsgn->bcgls', cm, bm)
    y_diag = jnp.einsum('bcgls,bcgrls,bcsgrp->bclgrp', cb, lmat, xdt)
    decay_states = jnp.exp(acs[..., -1:] - acs)
    states = jnp.einsum('bclgn,bcgrl,bclgrp->bcgrpn', bm, decay_states, xdt)
    chunk_decay = jnp.exp(acs[..., -1])

    def step(h, inp):
        st, dec = inp
        return dec[..., None, None] * h + st, h

    h0 = jnp.zeros((b, G, R, P, N), f32)
    _, prev = lax.scan(step, h0, (jnp.moveaxis(states, 1, 0), jnp.moveaxis(chunk_decay, 1, 0)))
    prev = jnp.moveaxis(prev, 0, 1)
    y_off = jnp.einsum('bclgn,bcgrpn,bcgrl->bclgrp', cm, prev, jnp.exp(acs))
    y = y_diag + y_off + xs * d_skip.astype(f32).reshape(G, R, 1)
    y = y.reshape(b, s, SSD_INNER) * jax.nn.silu(z.astype(f32))
    yg = y.reshape(b, s, G, SSD_INNER // G)
    yg = yg * lax.rsqrt(jnp.mean(yg * yg, axis=-1, keepdims=True) + RMS_EPS)
    return (yg.reshape(b, s, SSD_INNER) * norm_w.astype(f32)).astype(z.dtype)

def _hier_moe(h, w_rg, b_rg, w_re, b_re, w_gate, w_up, w_down):
    b, s, d = h.shape
    f32 = jnp.float32
    t = h.reshape(b * s, d)
    g_logits = (t @ w_rg + b_rg).astype(f32)
    g_idx = jnp.argmax(g_logits, axis=-1)
    g_w = jnp.take_along_axis(jax.nn.softmax(g_logits, axis=-1), g_idx[:, None], axis=-1)
    e_logits = (t @ w_re + b_re).astype(f32).reshape(-1, N_EXPERT_GROUPS, EXPERTS_PER_GROUP)
    e_sel = jnp.take_along_axis(e_logits, g_idx[:, None, None], axis=1)[:, 0]
    top_v, top_i = lax.top_k(e_sel, TOP_K_INNER)
    top_w = jax.nn.softmax(top_v, axis=-1) * g_w
    inner = jnp.einsum('tk,tke->te', top_w, jax.nn.one_hot(top_i, EXPERTS_PER_GROUP, dtype=f32))
    combine = jax.nn.one_hot(g_idx, N_EXPERT_GROUPS, dtype=f32)[:, :, None] * inner[:, None, :]
    out = jnp.zeros((b * s, d), f32)
    for gi in range(N_EXPERT_GROUPS):
        hg = jnp.einsum('td,edf->tef', t, w_gate[gi])
        hu = jnp.einsum('td,edf->tef', t, w_up[gi])
        act = (jax.nn.silu(hg) * hu * combine[:, gi, :, None].astype(t.dtype)).astype(t.dtype)
        out = out + jnp.einsum('tef,efd->td', act, w_down[gi]).astype(f32)
    return out.reshape(b, s, d).astype(h.dtype)

def setup_inputs(seed: int = 0) -> dict:
    key = jax.random.key(seed)
    ks = jax.random.split(key, 32)
    f32 = jnp.float32
    L = DEPTH
    D = D_MODEL

    def nrm(k, shape, scale):
        return jax.random.normal(k, shape, f32) * scale

    u = jax.random.uniform(ks[8], (L, SSD_HEADS), f32)
    dt0 = jnp.exp(u * (math.log(DT_MAX) - math.log(DT_MIN)) + math.log(DT_MIN))
    return {
        'x': nrm(ks[0], (BATCH, SEQ, D), 1.0),
        'p': nrm(ks[1], (DEPTH, BATCH, SEQ, PLE_DIM), 1.0),
        'ln0_w': 1.0 + nrm(ks[2], (D,), 0.05),
        'ln0_b': nrm(ks[3], (D,), 0.05),
        'w_in': nrm(ks[4], (L, D, IN_PROJ_DIM), D ** -0.5),
        'b_gate': nrm(ks[5], (L, 2, D), 0.1),
        'conv_w': nrm(ks[6], (L, CONV_WIDTH, SSD_CONV_DIM), CONV_WIDTH ** -0.5),
        'conv_b': nrm(ks[7], (L, SSD_CONV_DIM), 0.05),
        'dt_bias': dt0 + jnp.log(-jnp.expm1(-dt0)),
        'a_log': jnp.log(jax.random.uniform(ks[9], (L, SSD_HEADS), f32, 1.0, 16.0)),
        'd_skip': 1.0 + nrm(ks[10], (L, SSD_HEADS), 0.1),
        'ssd_norm_w': 1.0 + nrm(ks[11], (L, SSD_INNER), 0.05),
        'sinks': nrm(ks[12], (L, ATT_HEADS), 0.5),
        'w_out_attn': nrm(ks[13], (L, ATT_WIDTH, D), ATT_WIDTH ** -0.5 * DN_BETA),
        'w_out_ssd': nrm(ks[14], (L, SSD_INNER, D), SSD_INNER ** -0.5 * DN_BETA),
        'w_out': nrm(ks[15], (L, D, D), D ** -0.5 * DN_BETA),
        'ln1_w': 1.0 + nrm(ks[16], (L, D), 0.05),
        'ln1_b': nrm(ks[17], (L, D), 0.05),
        'w_router_group': nrm(ks[18], (L, D, N_EXPERT_GROUPS), D ** -0.5),
        'b_router_group': nrm(ks[19], (L, N_EXPERT_GROUPS), 0.01),
        'w_router_expert': nrm(ks[20], (L, D, N_EXPERTS), D ** -0.5),
        'b_router_expert': nrm(ks[21], (L, N_EXPERTS), 0.01),
        'w_exp_gate': nrm(ks[22], (L, N_EXPERT_GROUPS, EXPERTS_PER_GROUP, D, D_FF_EXPERT), D ** -0.5),
        'w_exp_up': nrm(ks[23], (L, N_EXPERT_GROUPS, EXPERTS_PER_GROUP, D, D_FF_EXPERT), D ** -0.5),
        'w_exp_down': nrm(ks[24], (L, N_EXPERT_GROUPS, EXPERTS_PER_GROUP, D_FF_EXPERT, D), D_FF_EXPERT ** -0.5 * DN_BETA),
        'w_ple': nrm(ks[25], (L, PLE_DIM, D), PLE_DIM ** -0.5 * DN_BETA),
        'w_ple_gate': nrm(ks[26], (L, D, D), D ** -0.5),
        'b_ple_gate': nrm(ks[27], (L, D), 0.1),
        'ln2_w': 1.0 + nrm(ks[28], (L, D), 0.05),
        'ln2_b': nrm(ks[29], (L, D), 0.05),
    }

def reference(x, p, ln0_w, ln0_b, w_in, b_gate, conv_w, conv_b, dt_bias, a_log, d_skip,
              ssd_norm_w, sinks, w_out_attn, w_out_ssd, w_out, ln1_w, ln1_b,
              w_router_group, b_router_group, w_router_expert, b_router_expert,
              w_exp_gate, w_exp_up, w_exp_down, w_ple, w_ple_gate, b_ple_gate, ln2_w, ln2_b):
    b, s, d = x.shape
    h = _layernorm(x, ln0_w, ln0_b)
    for i in range(DEPTH):
        proj = h @ w_in[i]
        q, k, v, z, xbc, dt_raw, g_logit = jnp.split(proj, IN_SPLITS, axis=-1)
        ya = _window_attention(
            q.reshape(b, s, ATT_HEADS, HEAD_DIM),
            k.reshape(b, s, ATT_KV_HEADS, HEAD_DIM),
            v.reshape(b, s, ATT_KV_HEADS, HEAD_DIM), sinks[i]) @ w_out_attn[i]
        ys = _ssd(xbc, z, dt_raw, conv_w[i], conv_b[i], dt_bias[i], a_log[i], d_skip[i],
                  ssd_norm_w[i]) @ w_out_ssd[i]
        gates = jax.nn.sigmoid(g_logit.reshape(b, s, 2, d) + b_gate[i])
        mix = (gates[:, :, 0, :] * ya + gates[:, :, 1, :] * ys) @ w_out[i]
        h1 = _layernorm(DN_ALPHA * h + mix, ln1_w[i], ln1_b[i])
        moe = _hier_moe(h1, w_router_group[i], b_router_group[i], w_router_expert[i],
                        b_router_expert[i], w_exp_gate[i], w_exp_up[i], w_exp_down[i])
        ple = jax.nn.sigmoid(h1 @ w_ple_gate[i] + b_ple_gate[i]) * (p[i] @ w_ple[i])
        h = _layernorm(DN_ALPHA * h1 + moe + ple, ln2_w[i], ln2_b[i])
    return h


_drawn_inputs = setup_inputs


def setup_inputs(seed=0):
    import zlib

    import numpy as np

    out = dict(_drawn_inputs(seed))
    spreads = {}
    factors = {'b_gate': 4.506,
     'conv_b': 4.126,
     'd_skip': 3.046,
     'ssd_norm_w': 4.647,
     'sinks': 32.8,
     'b_router_group': 22.162,
     'b_router_expert': 26.265,
     'b_ple_gate': 6.17}
    for name, (base, spread) in spreads.items():
        noise = np.random.default_rng([zlib.crc32(name.encode()), seed]).standard_normal(out[name].shape)
        drawn = base * np.exp(spread * noise) if base else spread * noise
        out[name] = __import__('jax').numpy.asarray(drawn.astype(out[name].dtype))
    for name, factor in factors.items():
        out[name] = (out[name] * factor).astype(out[name].dtype)
    return out
```

```python
from contextlib import ExitStack

import concourse.bass as bass
from concourse import mybir

ALU = mybir.AluOpType
ACT = mybir.ActivationFunctionType
F32 = mybir.dt.float32
I32 = mybir.dt.int32
U32 = mybir.dt.uint32
AX = mybir.AxisListType

P = 128
D = 1024
S = 512
NT = S // P
KD = D // P
HEADS, HD = 8, 64
SSDH, SP, SN = 16, 64, 64
CONV_W = 4
XBC = 1280
NX = XBC // P
COL_KV, COL_Z, COL_XBC, COL_DT, COL_GATE = 512, 768, 1792, 3072, 3088
NG, NPG, NE, FF = 4, 8, 32, 256
PLE = 256
ALPHA = 2.0 ** 0.25
LN_EPS = 1e-5
RMS_EPS = 1e-5
NEG = -1e30

SLOTS, SLOT = 12, 2048
CAP = 64
EXTRA = 2 * S // CAP - 1
BLOCKS = NE + EXTRA
ROWS = 3072
ZERO_DMAS = (ROWS + ROWS - NE * CAP) // P // 2
MOE_SEQ = 36


def stream_order(aps):
    w_in = aps["w_in"][0].rearrange("(k p) n -> p k n", p=P)

    def cols(c):
        return [(w_in[:, :, c:c + 256], slice(0, P), "kn", slice(0, 256))]

    out = [cols(COL_XBC + 256 * s) for s in range(5)]
    out += [cols(COL_KV)]
    for s in range(2):
        out.append([(w_in[:, :, 256 * g + 64 * (2 * s + j):][:, :, 0:64], slice(0, P), "kn",
                     slice(128 * j + 64 * g, 128 * j + 64 * g + 64)) for j in range(2) for g in range(2)])
    out += [cols(COL_Z + 256 * s) for s in range(4)]

    def gates(s):
        return [cols(COL_GATE + 256 * s), cols(COL_GATE + D + 256 * s)]

    out += gates(0)
    woa = aps["w_out_attn"][0].rearrange("(g s j d) n -> g s d j n", g=2, s=2, j=2)
    for s in range(2):
        out.append([(woa[g, s], slice(64 * g, 64 * g + 64), "kN", slice(0, D)) for g in range(2)])

    def rows(w, s):
        return [(w[256 * s:256 * s + 256, :].rearrange("(k p) n -> p k n", p=P), slice(0, P), "kN",
                 slice(0, D))]

    out += [rows(aps["w_out_ssd"][0], s) for s in range(4)]
    for s in range(1, 4):
        out += gates(s)
    out += [rows(aps["w_out"][0], s) for s in range(4)]
    out += [rows(aps["w_ple_gate"][0], s) for s in range(4)]
    out += [rows(aps["w_ple"][0], 0)]
    return out


SEQ_XBC, SEQ_KV, SEQ_Q, SEQ_Z, SEQ_WOA, SEQ_WOS, SEQ_WO, SEQ_PG, SEQ_PLE = (0, 5, 6, 8, 14, 16, 26, 30, 34)
SEQ_GATE = (12, 20, 22, 24)


def last_uses():
    out = [("pe_xbc", 2 * s + 2) for s in range(5)] + [("pe_kv", 2)] + [("pe_q", 2), ("pe_q", 4)]
    out += [("pe_z", 7), ("pe_z", 7), ("pe_z", 8), ("pe_z", 8)]
    out += [("pe_g", 3), ("pe_g", 4)] + [("pe_ya", KD)] * 2 + [("pe_ys", KD)] * 4
    for s in range(1, 4):
        out += [("pe_g", 4 * s + 3), ("pe_g", 4 * s + 4)]
    return out + [("pe_mix", 2 * NT)] * 4 + [("pe_pg", 2 * NT)] * 4 + [("pe_pp", 2 * NT)]


USED = last_uses()


def psum_plan(sems):
    units = []

    def unit(key, banks, *free):
        units.append((key, banks, [(sems[n], v) for n, v in free]))

    unit("par", 1, ("par_read", 1))
    for i in range(NT):
        for b in range(2):
            unit(("hT", i, b), 1, ("hT_read", 2 * i + b + 1))
    for n in range(NX):
        unit(("xbc", n), 1, ("conv_read", n + 1))
    unit("dt", 1, ("dt_read", 1))
    unit("k", 1, ("kv_read", 1))
    unit("v", 1, ("kv_read", 2))
    for j in range(4):
        unit(("q", j), 1, ("q_read", j + 1))

    def z(n):
        unit(("z", n), 1, ("z_read", n + 1))

    def sc(n):
        unit(("sc", n), 2, ("sc_read", n + 1))

    sc(0)
    for n in range(8):
        z(n)
        if n < 7:
            sc(n + 1)
        if n:
            unit(("av", n - 1), 1, ("av_read", n))
        unit(("pt", n), 2, ("pt_read", n + 1))
    unit(("av", 7), 1, ("av_read", 8))
    for c in range(NT):
        unit(("xt", c), 2, ("xt_read", c + 1))
        unit(("cb", c), 2, ("cb_act", c + 1), ("cb_dve", c + 1))
        for q in range(4):
            unit(("seg", c, q), 1, ("seg_read", 4 * c + q + 1))
        if c:
            unit(("yo", c), 2, ("yo_read", c))
        unit(("yd", c), 2, ("yd_read", c + 1))
        if c < NT - 1:
            unit(("st", c), 1, ("st_read", c + 1))
        unit(("yT", c), 2, ("yT_read", c + 1))
    for n in range(KD):
        unit(("gA", n), 1, ("g_read", 2 * n + 1))
        unit(("gS", n), 1, ("g_read", 2 * n + 2))
        unit(("ya", n), 1, ("ya_read", n + 1))
        unit(("ys", n), 1, ("ys_read", n + 1))
    for i in range(NT):
        for b in range(2):
            unit(("mix", i, b), 1, ("mix_read", 2 * i + b + 1))
    for kk in range(2):
        unit(("pT", kk), 1, ("pT_read", kk + 1))
    for i in range(NT):
        unit(("h1T", i), 2, ("h1T_read", i + 1))
    unit("rt", 1, ("rt_read", 1))
    for i in range(NT):
        for b in range(2):
            unit(("pg", i, b), 1, ("pg_read", 2 * i + b + 1))
            unit(("pp", i, b), 1, ("pp_read", 2 * i + b + 1))
            if i == b == 0:
                unit("rk", 1, ("rk_read", 1))
    place, holder, at = {}, [[] for _ in range(8)], 0
    for key, banks, free in units:
        if banks == 2:
            at += at % 2
        at %= 8
        need = {}
        for b in range(at, at + banks):
            for s, v in holder[b]:
                need[s.name] = (s, max(v, need.get(s.name, (s, 0))[1]))
            holder[b] = free
        place[key] = (at, list(need.values()))
        at += banks
    last = {}
    for b in range(8):
        for s, v in holder[b]:
            last[s.name] = (s, max(v, last.get(s.name, (s, 0))[1]))
    return place, list(last.values())


def block_kernel(nc, aps, out):
    with ExitStack() as ctx:
        def sem(name):
            return ctx.enter_context(nc.semaphore(name))

        arena = ctx.enter_context(nc.sbuf_tensor("arena", [P, 52880], F32))
        place = [0]

        def region(n):
            a = place[0]
            place[0] += n
            return a

        def at(base, n, parts=(0, P)):
            return arena[parts[0]:parts[0] + parts[1], base:base + n]

        def shaped(base, pattern, **k):
            n = 1
            for v in k.values():
                n *= v
            return at(base, n).rearrange(pattern, **k)

        R_RING = region(SLOTS * SLOT)
        R_H, R_T, R_Z = region(4096), region(4096), region(4096)
        R_X = region(5120)
        R_Y = region(2048)
        R_A = region(7168)
        ring = shaped(R_RING, "p (s k n) -> p s k n", s=SLOTS, k=KD, n=256)
        ringN = shaped(R_RING, "p (s k n) -> p s k n", s=SLOTS, k=2, n=D)
        h = shaped(R_H, "p (i n) -> p i n", i=NT, n=D)
        hT = shaped(R_T, "p (k t) -> p k t", k=KD, t=S)
        sz = shaped(R_Z, "p (i n) -> p i n", i=NT, n=D)
        yT = shaped(R_Z, "p (i k t) -> p i k t", i=NT, k=KD, t=P)
        xs = shaped(R_X, "p (n t) -> p n t", n=NX, t=S)
        mixT = shaped(R_X, "p (n t) -> p n t", n=KD, t=S)
        yaT = shaped(R_Y, "p (j t) -> p j t", j=4, t=S)
        qT = shaped(R_A, "p (j t) -> p j t", j=4, t=S)
        kT = at(R_A + 2048, S)
        vt = shaped(R_A + 2560, "p (i n) -> p i n", i=NT, n=P)
        bias = shaped(R_A + 3072, "p (m w) -> p m w", m=8, w=256)
        prob = shaped(R_A + 5120, "p (m w) -> p m w", m=4, w=256)
        probT = shaped(R_A + 6144, "p (m w t) -> p m w t", m=4, w=2, t=P)
        ln_w, ln_b = at(R_A + 5120, D), at(R_A + 6144, D)
        ctanh = shaped(R_Z, "p (b t) -> p b t", b=2, t=S)
        xtok = at(R_A, D)
        xdt = at(R_A + 1024, D)
        xdec = at(R_A + 2048, D)
        y = at(R_A + 3072, D)
        lmat = shaped(R_A + 4096, "p (b m t) -> p b m t", b=2, m=4, t=P)
        state = at(R_A + 5120, 512)
        btok = at(R_A + 5632, P)
        cbm = shaped(R_A + 5760, "p (g t) -> p g t", g=2, t=P)
        tmp = at(R_A + 6016, D)
        A1w, A1b = at(R_A, D), at(R_A + 1024, D)
        bple = at(R_A + 2048, D)
        gact = shaped(R_A + 3072, "p (b g t) -> p b g t", b=2, g=2, t=S)
        gtmp = shaped(R_A + 5120, "p (b t) -> p b t", b=2, t=S)
        p_in = shaped(R_A + 6144, "p (i n) -> p i n", i=NT, n=PLE)
        pT = shaped(R_X + 4096, "p (k t) -> p k t", k=2, t=S)
        pgt = shaped(R_A + 3072, "p (b t) -> p b t", b=4, t=S)
        xg = shaped(R_X, "p (b n) -> p b n", b=2, n=D)
        xgT = shaped(R_X + 2048, "p (b k t) -> p b k t", b=2, k=KD, t=P)
        eth = shaped(R_X + 4352, "p (b n) -> p b n", b=2, n=FF)[0:CAP]
        eact = shaped(R_H, "p (b n) -> p b n", b=2, n=FF)
        eactT = shaped(R_X + 4096, "p (b k t) -> p b k t", b=2, k=2, t=CAP)
        eout = shaped(R_Y, "p (b n) -> p b n", b=2, n=D)[0:CAP]
        ygat = shaped(R_T, "p (i c n) -> p i c n", i=2, c=2, n=D)
        ident, upper, ones, upstrict = (at(region(P), P) for _ in range(4))
        par_rows = at(R_A, P, (0, 74))
        par = at(region(74), 74)
        conv_w = par[:, 0:40].rearrange("p (w n) -> p w n", w=CONV_W)
        conv_b, b_gate, norm_w = par[:, 40:50], par[:, 50:66], par[:, 66:74]
        w_dt = shaped(region(KD * 16), "p (k n) -> p k n", k=KD, n=16)
        w_rt = shaped(region(KD * 36), "p (k n) -> p k n", k=KD, n=36)
        brow = region(16 * 3 + 8 + 36)
        dt_bias, a_row, dskip = (at(brow + 16 * j, 16) for j in range(3))
        sink = at(brow + 48, 8)
        rbias = at(brow + 56, 36)
        stats = at(region(12), 12)
        mv = at(region(8), 8)
        dtv = shaped(region(64), "p (i n) -> p i n", i=NT, n=16)
        dta = shaped(region(64), "p (i n) -> p i n", i=NT, n=16)
        R_SM = region(192)
        acs = shaped(R_SM, "p (a n) -> p a n", a=8, n=16)
        att = shaped(R_SM + 128, "p (b a n) -> p b a n", b=2, a=6, n=4)
        lg = shaped(region(NT * 36), "p (i n) -> p i n", i=NT, n=36)
        rw = [shaped(R_A + 5120 + NT * NE * j, "p (i n) -> p i n", i=NT, n=NE) for j in range(6)]
        rv = [at(region(NT), NT) for _ in range(12)]
        iota_e = at(region(NE), NE)
        cnt = [at(R_A + 5888 + NE * j, NE) for j in range(6)]
        ctlf = at(region(16), 16)
        rowsU = ctx.enter_context(nc.sbuf_tensor("rowsU", [P, 2 * NT], U32))
        ctl = ctx.enter_context(nc.sbuf_tensor("ctl", [P, 16], I32))
        psum = ctx.enter_context(nc.psum_tensor("psum", [P, 8, 512], F32))

        xg_dram = nc.dram_tensor("xg_rows", [ROWS, D], F32).ap()
        y_dram = nc.dram_tensor("y_rows", [ROWS, D], F32).ap()

        slot_in = [sem(f"slot_in{s}") for s in range(SLOTS)]
        s_aT_mm = sem("aT_mm")
        s_aT_sb = sem("aT_sb")
        s_acs_exp = sem("acs_exp")
        s_act_step = sem("act_step")
        s_ah_ready = sem("ah_ready")
        s_av_read = sem("av_read")
        s_base_ready = sem("base_ready")
        s_blocks_stored = sem("blocks_stored")
        s_bple_in = sem("bple_in")
        s_cb_act = sem("cb_act")
        s_cb_dve = sem("cb_dve")
        s_combined = sem("combined")
        s_consts = sem("consts")
        s_conv_read = sem("conv_read")
        s_ctanh_done = sem("ctanh_done")
        s_dist_in = sem("dist_in")
        s_dt_exp = sem("dt_exp")
        s_dt_exp_in = sem("dt_exp_in")
        s_dt_read = sem("dt_read")
        s_dta_ready = sem("dta_ready")
        s_dve_step = sem("dve_step")
        s_eact_a = sem("eact_a")
        s_eact_sb = sem("eact_sb")
        s_exp_done = sem("exp_done")
        s_fin_ready = sem("fin_ready")
        s_g_read = sem("g_read")
        s_gu_mm = sem("gu_mm")
        s_h1T_read = sem("h1T_read")
        s_h1_ready = sem("h1_ready")
        s_hT_read = sem("hT_read")
        s_h_ready = sem("h_ready")
        s_kv_read = sem("kv_read")
        s_lmat_exp = sem("lmat_exp")
        s_ln0_in = sem("ln0_in")
        s_ln1_in = sem("ln1_in")
        s_ln2_in = sem("ln2_in")
        s_m_ready = sem("m_ready")
        s_mix_read = sem("mix_read")
        s_mix_ready = sem("mix_ready")
        s_nmax_ready = sem("nmax_ready")
        s_out_st = sem("out_st")
        s_pT_read = sem("pT_read")
        s_p_in = sem("p_in")
        s_par_in = sem("par_in")
        s_par_read = sem("par_read")
        s_pe_av = sem("pe_av")
        s_pe_cb = sem("pe_cb")
        s_pe_dt = sem("pe_dt")
        s_pe_g = sem("pe_g")
        s_pe_h1T = sem("pe_h1T")
        s_pe_hT = sem("pe_hT")
        s_pe_kv = sem("pe_kv")
        s_pe_mix = sem("pe_mix")
        s_pe_pT = sem("pe_pT")
        s_pe_par = sem("pe_par")
        s_pe_pg = sem("pe_pg")
        s_pe_pp = sem("pe_pp")
        s_pe_pt = sem("pe_pt")
        s_pe_q = sem("pe_q")
        s_pe_rk = sem("pe_rk")
        s_pe_rt = sem("pe_rt")
        s_pe_sc = sem("pe_sc")
        s_pe_seg = sem("pe_seg")
        s_pe_st = sem("pe_st")
        s_pe_xbc = sem("pe_xbc")
        s_pe_xt = sem("pe_xt")
        s_pe_yT = sem("pe_yT")
        s_pe_ya = sem("pe_ya")
        s_pe_yd = sem("pe_yd")
        s_pe_yo = sem("pe_yo")
        s_pe_ys = sem("pe_ys")
        s_pe_z = sem("pe_z")
        s_pg_read = sem("pg_read")
        s_pg_tanh = sem("pg_tanh")
        s_pool_step = sem("pool_step")
        s_pp_read = sem("pp_read")
        s_prob_ready = sem("prob_ready")
        s_pt_read = sem("pt_read")
        s_q_read = sem("q_read")
        s_rk_read = sem("rk_read")
        s_rows_ready = sem("rows_ready")
        s_rt_exp = sem("rt_exp")
        s_rt_exp_in = sem("rt_exp_in")
        s_rt_read = sem("rt_read")
        s_sc_read = sem("sc_read")
        s_scattered = sem("scattered")
        s_seg_read = sem("seg_read")
        s_sel_ready = sem("sel_ready")
        s_silu_done = sem("silu_done")
        s_small_in = sem("small_in")
        s_st_read = sem("st_read")
        s_tanh_sb = sem("tanh_sb")
        s_tz_done = sem("tz_done")
        s_wsmall_in = sem("wsmall_in")
        s_xT_mm = sem("xT_mm")
        s_x_in = sem("x_in")
        s_xdec_ready = sem("xdec_ready")
        s_xdt_ready = sem("xdt_ready")
        s_xgT_sb = sem("xgT_sb")
        s_xt_read = sem("xt_read")
        s_yT_read = sem("yT_read")
        s_y_act = sem("y_act")
        s_y_dve = sem("y_dve")
        s_y_mm = sem("y_mm")
        s_y_ready = sem("y_ready")
        s_ya_read = sem("ya_read")
        s_yd_read = sem("yd_read")
        s_yo_read = sem("yo_read")
        s_ys_read = sem("ys_read")
        s_z_read = sem("z_read")
        s_zero_set = sem("zero_set")
        s_zeroed = sem("zeroed")
        sems = {x.name: x for x in (
            s_av_read, s_cb_act, s_cb_dve, s_conv_read, s_dt_read, s_g_read, s_h1T_read, s_hT_read,
            s_kv_read, s_mix_read, s_pT_read, s_par_read, s_pg_read, s_pp_read, s_pt_read, s_q_read,
            s_rk_read, s_rt_read, s_sc_read, s_seg_read, s_st_read, s_xt_read, s_yT_read, s_ya_read,
            s_yd_read, s_yo_read, s_ys_read, s_z_read, s_pe_g, s_pe_kv, s_pe_mix, s_pe_pg, s_pe_pp,
            s_pe_q, s_pe_xbc, s_pe_ya, s_pe_ys, s_pe_z)}
        xg_in = [sem(f"xg_in{b}") for b in range(2)]
        y_gath = [sem(f"y_gath{b}") for b in range(2)]
        y_st = [sem(f"y_st{b}") for b in range(2)]
        plan, plan_last = psum_plan(sems)

        def bank(key, n=512, banks=1):
            b = plan[key][0]
            flat = psum[:, b:b + banks, :].rearrange("p b n -> p (b n)")
            return flat[:, 0:n]

        loads = stream_order(aps)
        wg = aps["w_exp_gate"].rearrange("l g e d f -> (l g e) d f")
        wu = aps["w_exp_up"].rearrange("l g e d f -> (l g e) d f")
        wd = aps["w_exp_down"].rearrange("l g e f d -> (l g e) f d")
        x_v = aps["x"][0].rearrange("(i p) n -> p i n", p=P)
        p_v = aps["p"][0, 0].rearrange("(i p) n -> p i n", p=P)
        out_v = out[0].rearrange("(i p) n -> i p n", p=P)
        zview = xg_dram.rearrange("(p r) n -> p r n", p=P)

        def landings(seq):
            return sum(len(loads[q]) for q in range(seq % SLOTS, min(seq, len(loads) - 1) + 1, SLOTS))

        def arrived(eng, seq):
            eng.wait_ge(slot_in[seq % SLOTS], 16 * landings(seq))

        def expert_slot_in(eng, e4, u, w):
            s = 3 * u + w
            eng.wait_ge(slot_in[s], e4 * 16 + 16 * (landings(s + MOE_SEQ) + 1))

        block = ctx.enter_context(nc.Block())

        @block.sync
        def _(sp):
            for i in range(NT):
                sp.dma_start(h[:, i, :], x_v[:, i, :]).then_inc(s_x_in, 16)
            for seq, parts in enumerate(loads):
                if seq >= SLOTS:
                    name, value = USED[seq - SLOTS]
                    sp.wait_ge(sems[name], value)
                for src, rows, kind, columns in parts:
                    view = (ring if kind == "kn" else ringN)[rows, seq % SLOTS, :, columns]
                    sp.dma_start(view, src).then_inc(slot_in[seq % SLOTS], 16)
                if seq == 3:
                    sp.dma_start(w_dt, aps["w_in"][0].rearrange("(k p) n -> p k n", p=P)[:, :, COL_DT:COL_DT + 16])\
                        .then_inc(s_wsmall_in, 16)
                    sp.dma_start(w_rt[:, :, 0:NG], aps["w_router_group"][0].rearrange("(k p) n -> p k n", p=P))\
                        .then_inc(s_wsmall_in, 16)
                    sp.dma_start(w_rt[:, :, NG:36], aps["w_router_expert"][0].rearrange("(k p) n -> p k n", p=P))\
                        .then_inc(s_wsmall_in, 16)

            def expert(e4, u, first):
                e = e4 * 4 + u
                if first:
                    for w in range(3):
                        if 24 + 3 * u + w < len(loads):
                            name, value = USED[24 + 3 * u + w]
                            sp.wait_ge(sems[name], value)
                else:
                    sp.wait_ge(s_gu_mm, e - 3)
                for w, t in ((0, wg), (1, wu)):
                    src = t[bass.ds(e, 1)].rearrange("a (k p) f -> p (a k) f", p=P)
                    sp.dma_start(ring[:, 3 * u + w], src).then_inc(slot_in[3 * u + w], 16)
                if not first:
                    sp.wait_ge(s_y_mm, e - 3)
                src = wd[bass.ds(e, 1)].rearrange("a (k p) n -> p (a k) n", p=P)
                sp.dma_start(ringN[:, 3 * u + 2], src).then_inc(slot_in[3 * u + 2], 16)

            for u in range(4):
                expert(0, u, True)
            with sp.Fori(1, NE // 4) as e4:
                for u in range(4):
                    expert(e4, u, False)
            sp.wait_ge(s_rows_ready, 1)
            total = sp.value_load(ctl[0:1, EXTRA:EXTRA + 1], min_val=0, max_val=EXTRA)
            with sp.Fori(0, EXTRA) as j:
                with sp.If(total > j):
                    sp.wait_ge(s_y_mm, j + NE)
                    e = sp.value_load(ctl[0:1, bass.ds(j, 1)], min_val=0, max_val=NE - 1)
                    for w, t in ((0, wg), (1, wu)):
                        src = t[bass.ds(e, 1)].rearrange("a (k p) f -> p (a k) f", p=P)
                        sp.dma_start(ring[:, w], src).then_inc(slot_in[w], 16)
                    src = wd[bass.ds(e, 1)].rearrange("a (k p) n -> p (a k) n", p=P)
                    sp.dma_start(ringN[:, 2], src).then_inc(slot_in[2], 16)
                sp.nop()

        @block.gpsimd
        def _(pool):
            steps = [0]

            def link(ins):
                steps[0] += 1
                ins.then_inc(s_pool_step, 1)
                pool.wait_ge(s_pool_step, steps[0])

            g = nc.gpsimd
            pool.dma_start(ln_w, aps["ln0_w"].rearrange("(a n) -> a n", a=1).broadcast_to([P, D])).then_inc(s_ln0_in, 16)
            pool.dma_start(ln_b, aps["ln0_b"].rearrange("(a n) -> a n", a=1).broadcast_to([P, D])).then_inc(s_ln0_in, 16)
            pool.dma_start(par_rows[0:40], aps["conv_w"][0].rearrange("w (n p) -> (w n) p", p=P)).then_inc(s_par_in, 16)
            pool.dma_start(par_rows[40:50], aps["conv_b"].rearrange("l (n p) -> (l n) p", p=P)).then_inc(s_par_in, 16)
            pool.dma_start(par_rows[50:66], aps["b_gate"][0].rearrange("b (n p) -> (b n) p", p=P)).then_inc(s_par_in, 16)
            pool.dma_start(par_rows[66:74], aps["ssd_norm_w"].rearrange("l (n p) -> (l n) p", p=P)).then_inc(s_par_in, 16)
            for dst, name in ((dt_bias, "dt_bias"), (a_row, "a_log"), (dskip, "d_skip"), (sink, "sinks"),
                              (rbias[:, 0:NG], "b_router_group"), (rbias[:, NG:36], "b_router_expert")):
                pool.dma_start(dst, aps[name].broadcast_to([P, dst.shape[1]])).then_inc(s_small_in, 16)
            link(g.memset(ones, 1.0))
            g.affine_select(out=ident, in_=ones, pattern=[[1, P]], compare_op=ALU.is_equal, fill=0.0, base=0,
                            channel_multiplier=-1).then_inc(s_consts, 1)
            g.affine_select(out=upper, in_=ones, pattern=[[1, P]], compare_op=ALU.is_ge, fill=0.0, base=0,
                            channel_multiplier=-1).then_inc(s_consts, 1)
            g.affine_select(out=upstrict, in_=ones, pattern=[[1, P]], compare_op=ALU.is_gt, fill=0.0, base=0,
                            channel_multiplier=-1).then_inc(s_consts, 1)
            g.iota(iota_e, pattern=[[1, NE]], base=0, channel_multiplier=0,
                   allow_small_or_imprecise_dtypes=True).then_inc(s_consts, 1)
            dist, mask = xs[:, 8, 0:256], xs[:, 9, 0:256]
            link(g.iota(dist, pattern=[[-1, 256]], base=P, channel_multiplier=1, allow_small_or_imprecise_dtypes=True))
            link(g.memset(mask, 0.0))
            link(g.memset(mask[0:64, 0:64], NEG))
            link(g.memset(mask[0:64, 192:256], NEG))
            g.memset(mask[64:128, 0:128], NEG).then_inc(s_dist_in, 1)
            zt = shaped(R_Y, "p (r n) -> p r n", r=2, n=D)
            pool.wait_ge(s_dist_in, 1)
            g.memset(zt, 0.0).then_inc(s_zero_set, 1)
            pool.wait_ge(s_zero_set, 1)
            for r in range(0, ROWS // P, 2):
                pool.dma_start(zview[:, r:r + 2, :], zt).then_inc(s_zeroed, 16)
            zview_y = y_dram[NE * CAP:ROWS].rearrange("(p r) n -> p r n", p=P)
            for r in range(0, zview_y.shape[1], 2):
                pool.dma_start(zview_y[:, r:r + 2, :], zt).then_inc(s_zeroed, 16)
            pool.wait_ge(s_pe_hT, 2 * NT)
            for i in range(NT):
                g.tensor_scalar(h[:, i, :], h[:, i, :], ALPHA, None, ALU.mult).then_inc(s_ah_ready, 1)
            pool.wait_ge(s_pe_yT, NT)
            for dst, name, landed in ((A1w, "ln1_w", s_ln1_in), (A1b, "ln1_b", s_ln1_in), (bple, "b_ple_gate", s_bple_in)):
                pool.dma_start(dst, aps[name].broadcast_to([P, D])).then_inc(landed, 16)
            pool.dma_start(p_in, p_v).then_inc(s_p_in, 16)
            pool.wait_ge(s_h1_ready, NT)
            for dst, name in ((A1w, "ln2_w"), (A1b, "ln2_b")):
                pool.dma_start(dst, aps[name].broadcast_to([P, D])).then_inc(s_ln2_in, 16)
            pool.wait_ge(s_zeroed, 16 * ZERO_DMAS)
            pool.wait_ge(s_rows_ready, 1)
            for i in range(NT):
                for c in range(2):
                    g.indirect_dma_start(
                        out=xg_dram, out_offset=bass.IndirectOffsetOnAxis(ap=rowsU[:, 2 * i + c:2 * i + c + 1], axis=0),
                        in_=h[:, i, :], in_offset=None, bounds_check=ROWS - 1, oob_is_err=False)\
                        .then_inc(s_scattered, 16)
            pool.wait_ge(s_blocks_stored, 1)
            for i in range(NT):
                if i >= 2:
                    pool.wait_ge(s_combined, 2 * (i - 1))
                for c in range(2):
                    g.indirect_dma_start(
                        out=ygat[:, i % 2, c, :], out_offset=None, in_=y_dram,
                        in_offset=bass.IndirectOffsetOnAxis(ap=rowsU[:, 2 * i + c:2 * i + c + 1], axis=0),
                        bounds_check=ROWS - 1, oob_is_err=False).then_inc(y_gath[i % 2], 16)

        @block.tensor
        def _(pe):
            mm, tr = nc.tensor.matmul, nc.tensor.transpose

            def opened(key, n=512, banks=1):
                for s, v in plan[key][1]:
                    pe.wait_ge(s, v)
                return bank(key, n, banks)

            pe.wait_ge(s_par_in, 64)
            pe.wait_ge(s_consts, 4)
            tr(opened("par")[:, 0:74], par_rows, ident[0:74, 0:74]).then_inc(s_pe_par, 1)
            for i in range(NT):
                pe.wait_ge(s_h_ready, i + 1)
                for b in range(2):
                    o = opened(("hT", i, b))
                    for k in range(4):
                        c = (4 * b + k) * P
                        t = tr(o[:, k * P:(k + 1) * P], h[:, i, c:c + P], ident)
                    t.then_inc(s_pe_hT, 1)
            pe.wait_ge(s_hT_read, 2 * NT)

            def proj(o, weight, signal):
                for k in range(KD):
                    t = mm(o, weight(k), hT[:, k, :], start=(k == 0), stop=(k == KD - 1))
                t.then_inc(signal, 1)


            for n in range(NX):
                seq = SEQ_XBC + n // 2
                arrived(pe, seq)
                proj(opened(("xbc", n)), lambda k: ring[:, seq % SLOTS, k, (n % 2) * P:(n % 2 + 1) * P], s_pe_xbc)
            pe.wait_ge(s_wsmall_in, 16 * 3)
            o = opened("dt", 64)
            for i in range(NT):
                for k in range(KD):
                    t = mm(o[:, 16 * i:16 * i + 16], hT[:, k, i * P:(i + 1) * P], w_dt[:, k, :], start=(k == 0),
                           stop=(k == KD - 1))
            t.then_inc(s_pe_dt, 1)
            arrived(pe, SEQ_KV)
            proj(opened("k"), lambda k: ring[:, SEQ_KV, k, 0:P], s_pe_kv)
            o = opened("v")
            for i in range(NT):
                for k in range(KD):
                    t = mm(o[:, i * P:(i + 1) * P], hT[:, k, i * P:(i + 1) * P], ring[:, SEQ_KV, k, P:2 * P],
                           start=(k == 0), stop=(k == KD - 1))
            t.then_inc(s_pe_kv, 1)
            for j in range(4):
                arrived(pe, SEQ_Q + j // 2)
                proj(opened(("q", j)), lambda k: ring[:, SEQ_Q + j // 2, k, (j % 2) * P:(j % 2 + 1) * P], s_pe_q)

            def scores(n):
                i, hf = divmod(n, 2)
                w = 256 if i else P
                if n == 0:
                    pe.wait_ge(s_kv_read, 2)
                    pe.wait_ge(s_q_read, 4)
                o = opened(("sc", n), D, 2).rearrange("p (m w) -> p m w", m=4)
                for m in (0, 2, 1, 3):
                    g = (m // 2) * HD
                    t = mm(o[:, m, 0:w], qT[g:g + HD, 2 * hf + m % 2, i * P:(i + 1) * P],
                           kT[g:g + HD, (i + 1) * P - w:(i + 1) * P], start=True, stop=True)
                t.then_inc(s_pe_sc, 1)

            def zproj(n):
                i, b = divmod(n, 2)
                for s in range(2):
                    arrived(pe, SEQ_Z + 2 * b + s)
                o = opened(("z", n))
                for k in range(KD):
                    s = SEQ_Z + 2 * b
                    t = mm(o, hT[:, k, i * P:(i + 1) * P], ring[:, s:s + 2, k, :], start=(k == 0), stop=(k == KD - 1))
                t.then_inc(s_pe_z, 1)

            def probs_t(n):
                i = n // 2
                kt = 2 if i else 1
                pe.wait_ge(s_prob_ready, n + 1)
                o = opened(("pt", n), D, 2).rearrange("p (m w t) -> p m w t", m=4, w=2)
                for m in range(4):
                    for w in range(kt):
                        t = tr(o[:, m, w, :], prob[:, m, w * P:(w + 1) * P], ident)
                t.then_inc(s_pe_pt, 1)

            def attend(n):
                i, hf = divmod(n, 2)
                kt = 2 if i else 1
                pe.wait_ge(s_pt_read, n + 1)
                o = opened(("av", n), 256)
                for m in range(4):
                    g = (m // 2) * HD
                    for w in range(kt):
                        t = mm(o[g:g + HD, (m % 2) * P:(m % 2 + 1) * P], vt[:, i - kt + 1 + w, g:g + HD],
                               probT[:, m, w, :], start=(w == 0), stop=(w == kt - 1))
                t.then_inc(s_pe_av, 1)

            scores(0)
            for n in range(8):
                zproj(n)
                if n < 7:
                    scores(n + 1)
                if n:
                    attend(n - 1)
                probs_t(n)
            attend(7)

            pe.wait_ge(s_silu_done, NX)
            pe.wait_ge(s_dta_ready, 1)
            for c in range(NT):
                ts = slice(c * P, (c + 1) * P)
                o = opened(("xt", c), D, 2)
                for k in range(KD):
                    t = tr(o[:, k * P:(k + 1) * P], xs[:, k, ts], ident)
                t.then_inc(s_pe_xt, 1)
                o = opened(("cb", c), D, 2)
                tr(o[:, 0:P], xs[:, 8, ts], ident)
                for g in range(2):
                    gs = slice(64 * g, 64 * g + 64)
                    mm(o[:, P + g * 512:2 * P + g * 512], xs[gs, 8, ts], xs[gs, 9, ts], start=True, stop=True)
                mm(o[:, 256:272], upper, dta[:, c, :], start=True, stop=True)
                mm(o[:, 272:288], ones, dta[:, c, :], start=True, stop=True).then_inc(s_pe_cb, 1)

                def seg(q):
                    o = opened(("seg", c, q))
                    for m in range(4):
                        hh = 4 * q + m
                        t = mm(o[:, m * P:(m + 1) * P], dta[:, c, hh:hh + 1].broadcast_to([P, P]), upper,
                               start=True, stop=True)
                    t.then_inc(s_pe_seg, 1)

                for q in range(4):
                    seg(q)
                if c:
                    o = opened(("yo", c), D, 2)
                    pe.wait_ge(s_st_read, c)
                    for g in range(2):
                        gs = slice(64 * g, 64 * g + 64)
                        t = mm(o[:, g * 512:(g + 1) * 512], xs[gs, 9, ts], state[gs, :], start=True, stop=True)
                    t.then_inc(s_pe_yo, 1)
                o = opened(("yd", c), D, 2)
                pe.wait_ge(s_xdt_ready, c + 1)
                for q in range(4):
                    pe.wait_ge(s_m_ready, 4 * c + q + 1)
                    for m in range(4):
                        hh = 4 * q + m
                        t = mm(o[:, hh * SP:(hh + 1) * SP], lmat[:, q % 2, m, :], xdt[:, hh * SP:(hh + 1) * SP],
                               start=True, stop=True)
                    t.then_inc(s_pe_yd, 1)
                if c < NT - 1:
                    o = opened(("st", c))
                    pe.wait_ge(s_xdec_ready, c + 1)
                    pe.wait_ge(s_cb_act, c + 1)
                    for g in range(2):
                        gs = slice(64 * g, 64 * g + 64)
                        t = mm(o[gs, :], btok[:, gs], xdec[:, g * 512:(g + 1) * 512], start=True, stop=True)
                    t.then_inc(s_pe_st, 1)
                pe.wait_ge(s_y_ready, c + 1)
                o = opened(("yT", c), D, 2)
                for k in range(KD):
                    t = tr(o[:, k * P:(k + 1) * P], y[:, k * P:(k + 1) * P], ident)
                t.then_inc(s_pe_yT, 1)

            pe.wait_ge(s_av_read, 8)
            pe.wait_ge(s_yT_read, NT)
            for s in range(6):
                arrived(pe, SEQ_WOA + s)
            for n in range(KD):
                for b, nm in ((0, "gA"), (1, "gS")):
                    seq = SEQ_GATE[n // 2] + b
                    arrived(pe, seq)
                    proj(opened((nm, n)), lambda k: ring[:, seq % SLOTS, k, (n % 2) * P:(n % 2 + 1) * P], s_pe_g)
                o = opened(("ya", n))
                for j in range(4):
                    s = (SEQ_WOA + j // 2) % SLOTS
                    t = mm(o, ringN[:, s, j % 2, n * P:(n + 1) * P], yaT[:, j, :], start=(j == 0), stop=(j == 3))
                t.then_inc(s_pe_ya, 1)
                o = opened(("ys", n)).rearrange("p (i t) -> p i t", i=NT)
                for k in range(KD):
                    s = (SEQ_WOS + k // 2) % SLOTS
                    t = mm(o, ringN[:, s, k % 2, n * P:(n + 1) * P], yT[:, :, k, :], start=(k == 0), stop=(k == KD - 1))
                t.then_inc(s_pe_ys, 1)
            pe.wait_ge(s_mix_ready, KD)
            for s in range(4):
                arrived(pe, SEQ_WO + s)
            for i in range(NT):
                for b in range(2):
                    o = opened(("mix", i, b))
                    for k in range(KD):
                        s = (SEQ_WO + k // 2) % SLOTS
                        t = mm(o, mixT[:, k, i * P:(i + 1) * P], ringN[:, s, k % 2, b * 512:(b + 1) * 512],
                               start=(k == 0), stop=(k == KD - 1))
                    t.then_inc(s_pe_mix, 1)
            pe.wait_ge(s_p_in, 16)
            for kk in range(2):
                o = opened(("pT", kk))
                for i in range(NT):
                    t = tr(o[:, i * P:(i + 1) * P], p_in[:, i, kk * P:(kk + 1) * P], ident)
                t.then_inc(s_pe_pT, 1)
            for i in range(NT):
                pe.wait_ge(s_h1_ready, i + 1)
                o = opened(("h1T", i), D, 2)
                for k in range(KD):
                    t = tr(o[:, k * P:(k + 1) * P], h[:, i, k * P:(k + 1) * P], ident)
                t.then_inc(s_pe_h1T, 1)
            pe.wait_ge(s_h1T_read, NT)
            o = opened("rt", NT * 36)
            for i in range(NT):
                for k in range(KD):
                    t = mm(o[:, 36 * i:36 * i + 36], hT[:, k, i * P:(i + 1) * P], w_rt[:, k, :], start=(k == 0),
                           stop=(k == KD - 1))
            t.then_inc(s_pe_rt, 1)
            for s in range(5):
                arrived(pe, SEQ_PG + s)
            pe.wait_ge(s_pT_read, 2)
            for i in range(NT):
                for b in range(2):
                    o = opened(("pg", i, b))
                    for k in range(KD):
                        s = (SEQ_PG + k // 2) % SLOTS
                        t = mm(o, hT[:, k, i * P:(i + 1) * P], ringN[:, s, k % 2, b * 512:(b + 1) * 512],
                               start=(k == 0), stop=(k == KD - 1))
                    t.then_inc(s_pe_pg, 1)
                    o = opened(("pp", i, b))
                    for k in range(2):
                        t = mm(o, pT[:, k, i * P:(i + 1) * P], ringN[:, SEQ_PLE % SLOTS, k, b * 512:(b + 1) * 512],
                               start=(k == 0), stop=(k == 1))
                    t.then_inc(s_pe_pp, 1)
                    if i == b == 0:
                        pe.wait_ge(s_sel_ready, 1)
                        o = opened("rk", 160)
                        for a in range(NT):
                            for j in range(a + 1):
                                mm(o[:, 32 * a:32 * a + 32], upstrict if j == a else ones, rw[0][:, j, :],
                                   start=(j == 0), stop=(j == a))
                        for j in range(NT):
                            t = mm(o[:, 128:160], ones, rw[0][:, j, :], start=(j == 0), stop=(j == NT - 1))
                        t.then_inc(s_pe_rk, 1)

            for s, v in plan_last:
                pe.wait_ge(s, v)
            pe.wait_ge(s_pp_read, 2 * NT)

            def rows_t(half, buf, part, loads):
                pe.wait_ge(s_xgT_sb, half)
                pe.wait_ge(xg_in[buf], loads)
                o = psum[:, 2, :].rearrange("p (k t) -> p k t", k=4)
                for k in range(4):
                    c = (4 * part + k) * P
                    t = tr(o[:, k, :], xg[:, buf, c:c + P], ident)
                t.then_inc(s_xT_mm, 1)

            def gate_up(e, u, e4, buf, half, halves):
                expert_slot_in(pe, e4, u, 0)
                expert_slot_in(pe, e4, u, 1)
                pe.wait_ge(s_xgT_sb, halves)
                o = psum[0:CAP, u % 2, :]
                for k in range(KD):
                    t = mm(o, xgT[:, buf, k, half * CAP:(half + 1) * CAP], ring[:, 3 * u:3 * u + 2, k, :], start=(k == 0), stop=(k == KD - 1))
                t.then_inc(s_gu_mm, 1)

            def down(e, u, e4, first=False):
                expert_slot_in(pe, e4, u, 2)
                pe.wait_ge(s_aT_sb, e + 1)
                if not first:
                    pe.wait_ge(s_y_act, e - 1)
                    pe.wait_ge(s_y_dve, e - 1)
                for b in range(2):
                    o = psum[0:CAP, 4 + 2 * (u % 2) + b, :]
                    for k in range(2):
                        t = mm(o, eactT[:, u % 2, k, :], ringN[:, 3 * u + 2, k, b * 512:(b + 1) * 512],
                               start=(k == 0), stop=(k == 1))
                t.then_inc(s_y_mm, 1)

            def act_t(e, u):
                pe.wait_ge(s_eact_sb, e + 1)
                if not (isinstance(e, int) and e == 0):
                    pe.wait_ge(s_aT_sb, e)
                o = psum[:, 3, 0:256].rearrange("p (k t) -> p k t", k=2)
                for k in range(2):
                    t = tr(o[:, k, :], eact[:, u % 2, k * P:(k + 1) * P], ident)
                t.then_inc(s_aT_mm, 1)

            def step(e4, u, first=False, last=False):
                e = e4 * 4 + u
                gate_up(e, u, e4, u // 2, u % 2, e + 2 - u % 2)
                if not (first and u == 0):
                    down(e - 1, (u - 1) % 4, e4 if u else e4 - 1, first=first and u < 3)
                if not (last and u >= 2):
                    rows_t(e + 2, 1 - u // 2, u % 2, e4 * 16 + 16 * (1 + u // 2))
                act_t(e, u)

            pe.wait_ge(xg_in[0], 16)
            for part in range(2):
                if part:
                    pe.wait_ge(s_xgT_sb, 1)
                o = psum[:, 2, :].rearrange("p (k t) -> p k t", k=4)
                for k in range(4):
                    c = (4 * part + k) * P
                    t = tr(o[:, k, :], xg[:, 0, c:c + P], ident)
                t.then_inc(s_xT_mm, 1)
            for u in range(4):
                step(0, u, first=True)
            with pe.Fori(1, NE // 4 - 1) as e4:
                for u in range(4):
                    step(e4, u)
            for u in range(4):
                step(NE // 4 - 1, u, last=True)
            down(NE - 1, 3, NE // 4 - 1)
            pe.wait_ge(s_rows_ready, 1)
            total = pe.value_load(ctl[0:1, EXTRA:EXTRA + 1], min_val=0, max_val=EXTRA)
            with pe.Fori(0, EXTRA) as j:
                with pe.If(total > j):
                    for part in range(2):
                        rows_t(j * 2 + NE + part, 1, part, j * 16 + 16 * (NE // 4 + 1))
                    gate_up(j + NE, 0, j + NE // 4, 1, 0, j * 2 + NE + 2)
                    act_t(j + NE, 0)
                    pe.wait_ge(s_y_act, j + NE)
                    pe.wait_ge(s_y_dve, j + NE)
                    down(j + NE, 0, j + NE // 4, first=True)
                pe.nop()

        @block.scalar
        def _(act):
            A = nc.scalar.activation

            def copy(dst, src):
                return nc.scalar.copy(dst, src)

            for i in range(NT):
                for b in range(2):
                    act.wait_ge(s_pe_hT, 2 * i + b + 1)
                    copy(hT[:, 4 * b:4 * b + 4, i * P:(i + 1) * P],
                         bank(("hT", i, b)).rearrange("p (k t) -> p k t", k=4)).then_inc(s_hT_read, 1)
            for n in range(NX):
                act.wait_ge(s_conv_read, n + 1)
                if n >= 2:
                    act.wait_ge(s_silu_done, n - 1)
                A(ctanh[:, n % 2, :], xs[:, n, :], ACT.Tanh).then_inc(s_ctanh_done, 1)
            act.wait_ge(s_dt_exp_in, 1)
            A(dta.rearrange("p i n -> p (i n)"), dta.rearrange("p i n -> p (i n)"), ACT.Exp).then_inc(s_dt_exp, 1)
            A(a_row, a_row, ACT.Exp).then_inc(s_dt_exp, 1)
            act.wait_ge(s_pe_kv, 1)
            act.wait_ge(s_h_ready, NT)
            copy(kT, bank("k")).then_inc(s_kv_read, 1)
            act.wait_ge(s_pe_kv, 2)
            copy(vt, bank("v").rearrange("p (i n) -> p i n", i=NT)).then_inc(s_kv_read, 1)
            act.wait_ge(s_par_read, 1)
            for j in range(4):
                act.wait_ge(s_pe_q, j + 1)
                copy(qT[:, j, :], bank(("q", j))).then_inc(s_q_read, 1)

            def z_tanh(n):
                i, b = divmod(n, 2)
                act.wait_ge(s_pe_z, n + 1)
                if n == 0:
                    act.wait_ge(s_silu_done, NX)
                A(sz[:, i, b * 512:(b + 1) * 512], bank(("z", n)), ACT.Tanh, scale=0.5).then_inc(s_tz_done, 1)

            def softmax_exp(n):
                w = 256 if n >= 2 else P
                act.wait_ge(s_nmax_ready, n + 1)
                a = att[:, n % 2]
                for m in range(4):
                    A(prob[:, m, 0:w], prob[:, m, 0:w], ACT.Exp, bias=a[:, 1, m:m + 1],
                      accum_out=a[:, 3, m:m + 1]).then_inc(s_act_step, 1)
                A(a[:, 2, :], a[:, 2, :], ACT.Exp).then_inc(s_exp_done, 1)

            def probs_out(n):
                act.wait_ge(s_pe_pt, n + 1)
                if n:
                    act.wait_ge(s_pe_av, n)
                w = 2 if n >= 2 else 1
                copy(probT[:, :, 0:w, :], bank(("pt", n), D, 2).rearrange("p (m w t) -> p m w t", m=4, w=2)[:, :, 0:w, :])\
                    .then_inc(s_pt_read, 1)

            def attn_out(n):
                i, hf = divmod(n, 2)
                act.wait_ge(s_pe_av, n + 1)
                if n == 0:
                    act.wait_ge(s_zeroed, 16 * ZERO_DMAS)
                copy(yaT[:, 2 * hf:2 * hf + 2, i * P:(i + 1) * P], bank(("av", n), 256).rearrange("p (j t) -> p j t", j=2))\
                    .then_inc(s_av_read, 1)

            for n in range(8):
                softmax_exp(n)
                z_tanh(n)
                if n:
                    attn_out(n - 1)
                probs_out(n)
            attn_out(7)

            for c in range(NT):
                act.wait_ge(s_pe_xt, c + 1)
                if c:
                    act.wait_ge(s_y_ready, c)
                copy(xtok, bank(("xt", c), D, 2)).then_inc(s_xt_read, 1)
                act.wait_ge(s_cb_dve, c + 1)
                if c:
                    act.wait_ge(s_pe_st, c)
                o = bank(("cb", c), D, 2)
                copy(btok, o[:, 0:P]).then_inc(s_act_step, 1)
                A(acs[:, 1:3, :], o[:, 256:288].rearrange("p (a n) -> p a n", a=2), ACT.Exp).then_inc(s_cb_act, 1)
                A(acs[:, 3, :], acs[:, 3, :], ACT.Exp).then_inc(s_acs_exp, 1)
                for q in range(4):
                    act.wait_ge(s_seg_read, 4 * c + q + 1)
                    A(lmat[:, q % 2], lmat[:, q % 2], ACT.Exp).then_inc(s_lmat_exp, 1)

            for n in range(KD):
                for b, nm in ((0, "gA"), (1, "gS")):
                    act.wait_ge(s_pe_g, 2 * n + b + 1)
                    if n == 0 and b == 0:
                        act.wait_ge(s_yT_read, NT)
                    if n >= 2:
                        act.wait_ge((s_ya_read, s_ys_read)[b], n - 1)
                    A(gact[:, n % 2, b, :], bank((nm, n)), ACT.Tanh, scale=0.5,
                      bias=b_gate[:, 8 * b + n:8 * b + n + 1]).then_inc(s_g_read, 1)
            for kk in range(2):
                act.wait_ge(s_pe_pT, kk + 1)
                copy(pT[:, kk, :], bank(("pT", kk))).then_inc(s_pT_read, 1)
            for i in range(NT):
                act.wait_ge(s_pe_h1T, i + 1)
                copy(hT[:, :, i * P:(i + 1) * P], bank(("h1T", i), D, 2).rearrange("p (k t) -> p k t", k=KD))\
                    .then_inc(s_h1T_read, 1)
            act.wait_ge(s_rt_exp_in, 1)
            A(lg[:, :, 0:NG], lg[:, :, 0:NG], ACT.Exp).then_inc(s_act_step, 1)
            A(rv[4], rv[4], ACT.Exp).then_inc(s_rt_exp, 1)
            for i in range(2 * NT):
                act.wait_ge(s_pg_read, i + 1)
                A(pgt[:, i % 4, :], pgt[:, i % 4, :], ACT.Tanh, scale=0.5).then_inc(s_pg_tanh, 1)

            def rows_in(pair, buf, transposed):
                if transposed is not None:
                    act.wait_ge(s_xT_mm, transposed)
                act.dma_start(xg[:, buf, :], xg_dram[bass.ds(pair * 2 * CAP, 2 * CAP)]).then_inc(xg_in[buf], 16)

            def rows_copy(half, buf, part):
                act.wait_ge(s_xT_mm, half + 1)
                copy(xgT[:, buf, 4 * part:4 * part + 4, :], psum[:, 2, :].rearrange("p (k t) -> p k t", k=4))\
                    .then_inc(s_xgT_sb, 1)

            def hidden_tanh(e, u):
                act.wait_ge(s_gu_mm, e + 1)
                A(eth[:, u % 2, :], psum[0:CAP, u % 2, 0:FF], ACT.Tanh, scale=0.5).then_inc(s_tanh_sb, 1)

            def act_copy(e, u):
                act.wait_ge(s_aT_mm, e + 1)
                copy(eactT[:, u % 2], psum[:, 3, 0:256].rearrange("p (k t) -> p k t", k=2)[:, :, 0:CAP]).then_inc(s_aT_sb, 1)

            def out_copy(e, u):
                act.wait_ge(s_y_mm, e + 1)
                if not (isinstance(e, int) and e < 2):
                    act.wait_ge(y_st[u % 2], (e - u % 2) * 8 if not isinstance(e, int) else e // 2 * 16)
                copy(eout[:, u % 2, 0:512], psum[0:CAP, 4 + 2 * (u % 2), :]).then_inc(s_y_act, 1)
                act.wait_ge(s_y_act, e + 1)
                act.wait_ge(s_y_dve, e + 1)
                act.dma_start(y_dram[bass.ds(e * CAP, CAP)], eout[:, u % 2, :]).then_inc(y_st[u % 2], 16)

            def step(e4, u, first=False, last=False):
                e = e4 * 4 + u
                hidden_tanh(e, u)
                if not (first and u == 0):
                    out_copy(e - 1, (u - 1) % 4)
                if not (last and u >= 2):
                    rows_copy(e + 2, 1 - u // 2, u % 2)
                if not last and u % 2:
                    rows_in(e4 * 2 + 3 + u // 2, 1 - u // 2, e + 3)
                act_copy(e, u)

            act.wait_ge(s_scattered, 16 * 2 * NT)
            act.wait_ge(s_pT_read, 2)
            act.wait_ge(s_pe_mix, 2 * NT)
            rows_in(0, 0, None)
            rows_in(1, 1, None)
            rows_copy(0, 0, 0)
            rows_copy(1, 0, 1)
            rows_in(2, 0, 2)
            act.wait_ge(s_pe_pp, 2 * NT)
            for u in range(4):
                step(0, u, first=True)
            with act.Fori(1, NE // 4 - 1) as e4:
                for u in range(4):
                    step(e4, u)
            for u in range(4):
                step(NE // 4 - 1, u, last=True)
            out_copy(NE - 1, 3)
            total = act.value_load(ctl[0:1, EXTRA:EXTRA + 1], min_val=0, max_val=EXTRA)
            with act.Fori(0, EXTRA) as j:
                with act.If(total > j):
                    e = j + NE
                    act.dma_start(xg[:, 1, :], xg_dram[bass.ds(e * CAP, 2 * CAP)]).then_inc(xg_in[1], 16)
                    for part in range(2):
                        rows_copy(j * 2 + NE + part, 1, part)
                    hidden_tanh(e, 0)
                    act_copy(e, 0)
                    act.wait_ge(s_y_mm, e + 1)
                    act.wait_ge(y_st[0], j * 16 + NE // 2 * 16)
                    copy(eout[:, 0, 0:512], psum[0:CAP, 4, :]).then_inc(s_y_act, 1)
                    act.wait_ge(s_y_act, e + 1)
                    act.wait_ge(s_y_dve, e + 1)
                    act.dma_start(y_dram[bass.ds(e * CAP, CAP)], eout[:, 0, :]).then_inc(y_st[0], 16)
                act.nop()
            act.wait_ge(y_st[0], total * 16 + NE // 2 * 16)
            act.wait_ge(y_st[1], NE // 2 * 16)
            act.wait_ge(xg_in[0], 16 * (NE // 4 + 1))
            copy(att[0:1, 0, 5, 0:1], att[0:1, 0, 4, 0:1]).then_inc(s_blocks_stored, 1)
            for i in range(NT):
                act.wait_ge(s_fin_ready, i + 1)
                act.dma_start(out_v[i], sz[:, i, :]).then_inc(s_out_st, 16)
            act.wait_ge(s_out_st, 16 * NT)

        @block.vector
        def _(dve):
            v = nc.vector
            steps, counts = [0], {}

            def link(ins):
                steps[0] += 1
                ins.then_inc(s_dve_step, 1)
                dve.wait_ge(s_dve_step, steps[0])

            def seen(s):
                counts[s.name] = counts.get(s.name, 0) + 1
                return counts[s.name]

            def rsqrt(dst, src, t):
                link(v.tensor_scalar(dst.bitcast(I32), src.bitcast(I32), -0.5, float(0x5F3759DF), ALU.mult, ALU.add))
                for _ in range(3):
                    link(v.tensor_tensor(t, dst, dst, ALU.mult))
                    link(v.scalar_tensor_tensor(t, t, -0.5, src, ALU.mult, ALU.mult))
                    link(v.scalar_tensor_tensor(dst, t, 1.5, dst, ALU.add, ALU.mult))

            def normed(x, w, b, signal):
                for s in range(2):
                    link(v.bn_stats(stats[:, 6 * s:6 * s + 6], x[:, 512 * s:512 * s + 512]))
                link(v.bn_aggr(mv[:, 0:2], stats))
                link(v.tensor_scalar(mv[:, 2:3], mv[:, 1:2], LN_EPS, None, ALU.add))
                rsqrt(mv[:, 3:4], mv[:, 2:3], mv[:, 4:5])
                link(v.tensor_scalar(x, x, mv[:, 0:1], mv[:, 3:4], ALU.subtract, ALU.mult))
                link(v.tensor_tensor(x, x, w, ALU.mult))
                v.tensor_tensor(x, x, b, ALU.add).then_inc(signal, 1)
                dve.wait_ge(signal, seen(signal))

            dve.wait_ge(s_dist_in, 1)
            dist, mask = xs[:, 8, 0:256], xs[:, 9, 0:256]
            link(v.scalar_tensor_tensor(dist, dist, -1.0, dist, ALU.mult, ALU.max))
            for m in range(8):
                head = 2 * (m // 4) + m % 2 + 4 * (m % 4 // 2)
                link(v.scalar_tensor_tensor(bias[:, m, :], dist, -(2.0 ** -(head + 1)), mask, ALU.mult, ALU.add))
            dve.wait_ge(s_ln0_in, 32)
            for i in range(NT):
                dve.wait_ge(s_x_in, 16 * NT)
                normed(h[:, i, :], ln_w, ln_b, s_h_ready)
                if i == 0:
                    dve.wait_ge(s_pe_par, 1)
                    v.tensor_copy(par, bank("par")[:, 0:74])\
                        .then_inc(s_par_read, 1)
                    dve.wait_ge(s_par_read, seen(s_par_read))
                    link(v.tensor_scalar(par[:, 0:66], par[:, 0:66], 0.5, None, ALU.mult))

            def conv(n):
                dve.wait_ge(s_pe_xbc, n + 1)
                o, a = bank(("xbc", n)), xs[:, n, :]
                link(v.tensor_scalar(a, o, conv_w[:, 3, n:n + 1], conv_b[:, n:n + 1], ALU.mult, ALU.add))
                for w in (2, 1, 0):
                    d = 3 - w
                    ins = v.scalar_tensor_tensor(a[:, d:S], o[:, 0:S - d], conv_w[:, w, n:n + 1], a[:, d:S], ALU.mult,
                                                 ALU.add)
                    if w:
                        link(ins)
                    else:
                        ins.then_inc(s_conv_read, 1)
                        dve.wait_ge(s_conv_read, n + 1)

            def silu(n):
                dve.wait_ge(s_ctanh_done, n + 1)
                v.scalar_tensor_tensor(xs[:, n, :], ctanh[:, n % 2, :], 1.0, xs[:, n, :], ALU.add, ALU.mult)\
                    .then_inc(s_silu_done, 1)
                dve.wait_ge(s_silu_done, seen(s_silu_done))

            for n in range(NX):
                conv(n)
                if n:
                    silu(n - 1)
            silu(NX - 1)

            dve.wait_ge(s_small_in, 16 * 6)
            dve.wait_ge(s_pe_dt, 1)
            flat = lambda t: t.rearrange("p i n -> p (i n)")
            v.tensor_tensor(dtv, bank("dt", 64).rearrange("p (i n) -> p i n", i=NT),
                                 dt_bias.unsqueeze(1).broadcast_to([P, NT, 16]), ALU.add)\
                .then_inc(s_dt_read, 1)
            dve.wait_ge(s_dt_read, seen(s_dt_read))
            fv, fa = flat(dtv), flat(dta)
            v.scalar_tensor_tensor(fa, fv, -1.0, fv, ALU.mult, ALU.min)\
                .then_inc(s_dt_exp_in, 1)
            dve.wait_ge(s_dt_exp_in, seen(s_dt_exp_in))
            dve.wait_ge(s_dt_exp, 2)
            s_, q_, c_ = (at(R_Z + 1024 + 64 * j, 64) for j in range(3))
            link(v.tensor_scalar(s_, fa, 2.0, None, ALU.add))
            link(v.reciprocal(s_, s_))
            link(v.tensor_tensor(s_, s_, fa, ALU.mult))
            link(v.tensor_tensor(q_, s_, s_, ALU.mult))
            link(v.tensor_scalar(c_, q_, 1.0 / 17, None, ALU.mult))
            for k in range(7, 0, -1):
                link(v.scalar_tensor_tensor(c_, c_, 1.0 / (2 * k + 1), q_, ALU.add, ALU.mult))
            link(v.scalar_tensor_tensor(c_, c_, 1.0, s_, ALU.add, ALU.mult))
            link(v.tensor_scalar(fv, fv, 0.0, None, ALU.max))
            link(v.scalar_tensor_tensor(fv, c_, 2.0, fv, ALU.mult, ALU.add))
            v.scalar_tensor_tensor(dta, dtv, -1.0, a_row.unsqueeze(1).broadcast_to([P, NT, 16]), ALU.mult, ALU.mult)\
                .then_inc(s_dta_ready, 1)
            dve.wait_ge(s_dta_ready, seen(s_dta_ready))

            sink_v = sink.rearrange("p (g f j) -> p g f j", g=2, f=2)

            def softmax_in(n):
                i, hf = divmod(n, 2)
                w = 256 if i else P
                a = att[:, n % 2]
                dve.wait_ge(s_pe_sc, n + 1)
                if n:
                    dve.wait_ge(s_pe_pt, n)
                o = bank(("sc", n), D, 2).rearrange("p (m w) -> p m w", m=4)[:, :, 0:w]
                pr = prob[:, :, 0:w]
                v.scalar_tensor_tensor(pr, o, HD ** -0.5, bias[:, 4 * hf:4 * hf + 4, 256 - w:256], ALU.mult, ALU.add)\
                    .then_inc(s_sc_read, 1)
                dve.wait_ge(s_sc_read, seen(s_sc_read))
                link(v.tensor_reduce(a[:, 0, :], pr, AX.X, ALU.max))
                two = lambda r: a[:, r, :].rearrange("p (g j) -> p g j", g=2)
                link(v.tensor_tensor(two(0), two(0), sink_v[:, :, hf, :], ALU.max))
                link(v.tensor_tensor(two(2), sink_v[:, :, hf, :], two(0), ALU.subtract))
                v.tensor_scalar(a[:, 1, :], a[:, 0, :], -1.0, None, ALU.mult)\
                    .then_inc(s_nmax_ready, 1)
                dve.wait_ge(s_nmax_ready, seen(s_nmax_ready))

            def softmax_out(n):
                w = 256 if n >= 2 else P
                a = att[:, n % 2]
                pr = prob[:, :, 0:w]
                dve.wait_ge(s_exp_done, n + 1)
                link(v.tensor_tensor(a[:, 4, :], a[:, 2, :], a[:, 3, :], ALU.add))
                link(v.reciprocal(a[:, 5, :], a[:, 4, :]))
                v.tensor_tensor(pr, pr, a[:, 5, :].unsqueeze(2).broadcast_to([P, 4, w]), ALU.mult)\
                    .then_inc(s_prob_ready, 1)
                dve.wait_ge(s_prob_ready, seen(s_prob_ready))

            def silu_z(n):
                i, b = divmod(n, 2)
                dve.wait_ge(s_tz_done, n + 1)
                zs = sz[:, i, b * 512:(b + 1) * 512]
                v.scalar_tensor_tensor(zs, zs, 1.0, bank(("z", n)), ALU.add, ALU.mult)\
                    .then_inc(s_z_read, 1)
                dve.wait_ge(s_z_read, seen(s_z_read))

            for n in range(8):
                softmax_in(n)
                softmax_out(n)
                silu_z(n)

            heads = lambda t: t.rearrange("p (h e) -> p h e", e=SP)
            per_head = lambda r, n=16: r.unsqueeze(2).broadcast_to([r.shape[0], n, SP])

            def out_t(c):
                dve.wait_ge(s_pe_yT, c + 1)
                v.tensor_tensor(yT[:, c], bank(("yT", c), D, 2).rearrange("p (k t) -> p k t", k=KD),
                                     norm_w.unsqueeze(2).broadcast_to([P, KD, P]), ALU.mult)\
                    .then_inc(s_yT_read, 1)
                dve.wait_ge(s_yT_read, seen(s_yT_read))

            for c in range(NT):
                if c:
                    out_t(c - 1)
                dve.wait_ge(s_pe_cb, c + 1)
                o = bank(("cb", c), D, 2)
                link(v.tensor_copy(acs[:, 0, :], o[:, 256:272]))
                for g in range(2):
                    link(v.tensor_tensor(cbm[:, g, :], o[:, P + 512 * g:2 * P + 512 * g], upper, ALU.mult))
                if c:
                    dve.wait_ge(s_acs_exp, c)
                v.tensor_tensor(acs[:, 3, :], o[:, 272:288], acs[:, 0, :], ALU.subtract)\
                    .then_inc(s_cb_dve, 1)
                dve.wait_ge(s_cb_dve, seen(s_cb_dve))
                dve.wait_ge(s_xt_read, c + 1)
                v.tensor_tensor(heads(xdt), heads(xtok), per_head(dtv[:, c, :]), ALU.mult)\
                    .then_inc(s_xdt_ready, 1)
                dve.wait_ge(s_xdt_ready, seen(s_xdt_ready))

                def seg(q):
                    dve.wait_ge(s_pe_seg, 4 * c + q + 1)
                    if 4 * c + q >= 2:
                        dve.wait_ge(s_pe_yd, 4 * c + q - 1)
                    for m in range(4):
                        ins = v.tensor_scalar(lmat[:, q % 2, m, :], bank(("seg", c, q))[:, m * P:(m + 1) * P],
                                              acs[:, 0, 4 * q + m:4 * q + m + 1], 0.0, ALU.subtract, ALU.min)
                    ins.then_inc(s_seg_read, 1)
                    dve.wait_ge(s_seg_read, 4 * c + q + 1)

                def decayed(q):
                    dve.wait_ge(s_lmat_exp, 4 * c + q + 1)
                    v.tensor_tensor(lmat[:, q % 2], lmat[:, q % 2],
                                         cbm[:, q // 2, :].unsqueeze(1).broadcast_to([P, 4, P]), ALU.mult)\
                        .then_inc(s_m_ready, 1)
                    dve.wait_ge(s_m_ready, seen(s_m_ready))

                seg(0)
                seg(1)
                decayed(0)
                dve.wait_ge(s_acs_exp, c + 1)
                if c:
                    dve.wait_ge(s_pe_st, c)
                v.tensor_tensor(heads(xdec), heads(xdt), per_head(acs[:, 3, :]), ALU.mult)\
                    .then_inc(s_xdec_ready, 1)
                dve.wait_ge(s_xdec_ready, seen(s_xdec_ready))
                decayed(1)
                seg(2)
                seg(3)
                decayed(2)
                decayed(3)
                if c:
                    dve.wait_ge(s_pe_yT, c)
                    dve.wait_ge(s_pe_yo, c)
                    v.tensor_tensor(heads(y), heads(bank(("yo", c), D, 2)), per_head(acs[:, 1, :]), ALU.mult)\
                        .then_inc(s_yo_read, 1)
                    dve.wait_ge(s_yo_read, seen(s_yo_read))
                    link(v.tensor_tensor(heads(tmp), heads(xtok), per_head(dskip), ALU.mult))
                    link(v.tensor_tensor(y, y, tmp, ALU.add))
                else:
                    link(v.tensor_tensor(heads(y), heads(xtok), per_head(dskip), ALU.mult))
                dve.wait_ge(s_pe_yd, 4 * c + 4)
                v.tensor_tensor(y, bank(("yd", c), D, 2), y, ALU.add)\
                    .then_inc(s_yd_read, 1)
                dve.wait_ge(s_yd_read, seen(s_yd_read))
                if c < NT - 1:
                    dve.wait_ge(s_pe_st, c + 1)
                    if c:
                        for g in range(2):
                            gs = slice(64 * g, 64 * g + 64)
                            link(v.tensor_tensor(heads(state[gs]), heads(state[gs]),
                                                 per_head(acs[gs, 2, 8 * g:8 * g + 8], 8), ALU.mult))
                        v.tensor_tensor(state, bank(("st", c)), state, ALU.add)\
                            .then_inc(s_st_read, 1)
                        dve.wait_ge(s_st_read, seen(s_st_read))
                    else:
                        v.tensor_copy(state, bank(("st", c)))\
                            .then_inc(s_st_read, 1)
                        dve.wait_ge(s_st_read, seen(s_st_read))
                link(v.scalar_tensor_tensor(y, y, 0.5, sz[:, c, :], ALU.mult, ALU.mult))
                for g in range(2):
                    yg = y[:, 512 * g:512 * g + 512]
                    link(v.tensor_tensor_reduce(out=tmp[:, 0:512], in0=yg, in1=yg, scale=1.0 / 512, scalar=0.0,
                                                op0=ALU.mult, op1=ALU.add, accum_out=mv[:, g:g + 1]))
                link(v.tensor_scalar(mv[:, 2:4], mv[:, 0:2], RMS_EPS, None, ALU.add))
                rsqrt(mv[:, 4:6], mv[:, 2:4], mv[:, 6:8])
                v.tensor_tensor(y.rearrange("p (g n) -> p g n", g=2), y.rearrange("p (g n) -> p g n", g=2),
                                     mv[:, 4:6].unsqueeze(2).broadcast_to([P, 2, 512]), ALU.mult)\
                    .then_inc(s_y_ready, 1)
                dve.wait_ge(s_y_ready, seen(s_y_ready))
            out_t(NT - 1)

            for n in range(KD):
                dve.wait_ge(s_g_read, 2 * n + 2)
                dve.wait_ge(s_pe_ya, n + 1)
                v.scalar_tensor_tensor(mixT[:, n, :], gact[:, n % 2, 0, :], 1.0, bank(("ya", n)), ALU.add, ALU.mult)\
                    .then_inc(s_ya_read, 1)
                dve.wait_ge(s_ya_read, seen(s_ya_read))
                dve.wait_ge(s_pe_ys, n + 1)
                v.scalar_tensor_tensor(gtmp[:, n % 2, :], gact[:, n % 2, 1, :], 1.0, bank(("ys", n)), ALU.add,
                                            ALU.mult)\
                    .then_inc(s_ys_read, 1)
                dve.wait_ge(s_ys_read, seen(s_ys_read))
                v.tensor_tensor(mixT[:, n, :], mixT[:, n, :], gtmp[:, n % 2, :], ALU.add)\
                    .then_inc(s_mix_ready, 1)
                dve.wait_ge(s_mix_ready, seen(s_mix_ready))
            dve.wait_ge(s_ah_ready, NT)
            dve.wait_ge(s_ln1_in, 32)
            for i in range(NT):
                for b in range(2):
                    dve.wait_ge(s_pe_mix, 2 * i + b + 1)
                    hb = h[:, i, 512 * b:512 * b + 512]
                    v.scalar_tensor_tensor(hb, bank(("mix", i, b)), 0.5, hb, ALU.mult, ALU.add)\
                        .then_inc(s_mix_read, 1)
                    dve.wait_ge(s_mix_read, seen(s_mix_read))
                normed(h[:, i, :], A1w, A1b, s_h1_ready)

            dve.wait_ge(s_pe_rt, 1)
            v.tensor_tensor(lg, bank("rt", NT * 36).rearrange("p (i n) -> p i n", i=NT),
                                 rbias.unsqueeze(1).broadcast_to([P, NT, 36]), ALU.add)\
                .then_inc(s_rt_read, 1)
            dve.wait_ge(s_rt_read, seen(s_rt_read))
            sel, oh1, oh2, em, t4, t5 = rw
            gl = lg[:, :, 0:NG]
            along = lambda r, n: r.unsqueeze(2).broadcast_to([P, NT, n])
            iotas = lambda n: iota_e[:, 0:n].unsqueeze(1).broadcast_to([P, NT, n])

            def first_max(vals, n, top, index, onehot):
                link(v.tensor_reduce(top, vals, AX.X, ALU.max))
                link(v.tensor_tensor(t5[:, :, 0:n], vals, along(top, n), ALU.is_equal))
                link(v.scalar_tensor_tensor(t5[:, :, 0:n], t5[:, :, 0:n], -64.0, iotas(n), ALU.mult, ALU.add))
                link(v.tensor_reduce(index, t5[:, :, 0:n], AX.X, ALU.min))
                link(v.tensor_scalar(index, index, 64.0, None, ALU.add))
                link(v.tensor_tensor(onehot, iotas(n), along(index, n), ALU.is_equal))

            dve.wait_ge(s_consts, 4)
            first_max(gl, NG, rv[0], rv[1], t4[:, :, 0:NG])
            link(v.tensor_tensor(gl, gl, along(rv[0], NG), ALU.subtract))
            in_g = lambda t: t.rearrange("p i (g e) -> p i g e", g=NG)
            ohg = t4[:, :, 0:NG].unsqueeze(3).broadcast_to([P, NT, NG, NPG])
            link(v.tensor_tensor(in_g(em), in_g(lg[:, :, NG:36]), ohg, ALU.mult))
            link(v.tensor_scalar(t4[:, :, 0:NG], t4[:, :, 0:NG], -1.0, -NEG, ALU.add, ALU.mult))
            link(v.tensor_tensor(in_g(em), in_g(em), ohg, ALU.add))
            first_max(em, NE, rv[3], rv[5], oh1)
            link(v.scalar_tensor_tensor(em, oh1, -3e38, em, ALU.mult, ALU.add))
            first_max(em, NE, rv[4], rv[6], oh2)
            v.tensor_tensor(rv[4], rv[4], rv[3], ALU.subtract)\
                .then_inc(s_rt_exp_in, 1)
            dve.wait_ge(s_rt_exp_in, seen(s_rt_exp_in))
            v.tensor_tensor(sel, oh1, oh2, ALU.add)\
                .then_inc(s_sel_ready, 1)
            dve.wait_ge(s_sel_ready, seen(s_sel_ready))
            dve.wait_ge(s_rt_exp, 1)
            link(v.tensor_reduce(rv[2], gl, AX.X, ALU.add))
            link(v.scalar_tensor_tensor(rv[7], rv[4], 1.0, rv[2], ALU.add, ALU.mult))
            link(v.reciprocal(rv[7], rv[7]))
            link(v.tensor_scalar(rv[8], rv[7], 0.5, None, ALU.mult))
            link(v.tensor_tensor(rv[9], rv[8], rv[4], ALU.mult))

            def ple_sum(n):
                i, b = divmod(n, 2)
                dve.wait_ge(s_pe_pg, n + 1)
                v.tensor_tensor(pgt[:, n % 4, :], bank(("pg", i, b)), bple[:, 512 * b:512 * b + 512], ALU.add)\
                    .then_inc(s_pg_read, 1)
                dve.wait_ge(s_pg_read, seen(s_pg_read))

            def ple_out(n):
                i, b = divmod(n, 2)
                hs = slice(512 * b, 512 * b + 512)
                link(v.tensor_scalar(sz[:, i, hs], h[:, i, hs], ALPHA, None, ALU.mult))
                dve.wait_ge(s_pg_tanh, n + 1)
                dve.wait_ge(s_pe_pp, n + 1)
                v.scalar_tensor_tensor(pgt[:, n % 4, :], pgt[:, n % 4, :], 1.0, bank(("pp", i, b)), ALU.add, ALU.mult)\
                    .then_inc(s_pp_read, 1)
                dve.wait_ge(s_pp_read, seen(s_pp_read))
                v.scalar_tensor_tensor(sz[:, i, hs], pgt[:, n % 4, :], 0.5, sz[:, i, hs], ALU.mult, ALU.add)\
                    .then_inc(s_base_ready, 1)
                dve.wait_ge(s_base_ready, seen(s_base_ready))

            dve.wait_ge(s_pe_rk, 1)
            rk = bank("rk", 160)
            rank, count = t4, cnt[0]
            link(v.tensor_copy(rank, rk[:, 0:128].rearrange("p (i n) -> p i n", i=NT)))
            v.tensor_copy(count, rk[:, 128:160])\
                .then_inc(s_rk_read, 1)
            dve.wait_ge(s_rk_read, seen(s_rk_read))
            more, csum = cnt[1], [cnt[2], cnt[3]]
            link(v.tensor_scalar(more, count, float(CAP), None, ALU.is_gt))
            for b in range(2, S // CAP):
                link(v.scalar_tensor_tensor(more, count, float(CAP * b), more, ALU.is_gt, ALU.add))
            link(v.tensor_copy(csum[0], more))
            a = 0
            for d in (1, 2, 4, 8, 16):
                link(v.tensor_copy(csum[1 - a][:, 0:d], csum[a][:, 0:d]))
                link(v.tensor_tensor(csum[1 - a][:, d:NE], csum[a][:, d:NE], csum[a][:, 0:NE - d], ALU.add))
                a = 1 - a
            csum = csum[a]
            first_row, jump = cnt[4], cnt[5]
            link(v.tensor_scalar(first_row, iota_e, float(CAP), None, ALU.mult))
            link(v.tensor_tensor(jump, csum, more, ALU.subtract))
            link(v.tensor_scalar(jump, jump, float(NE - 1), float(CAP), ALU.add, ALU.mult))
            link(v.tensor_tensor(jump, jump, first_row, ALU.subtract))
            per_e = lambda r: r.unsqueeze(1).broadcast_to([P, NT, NE])
            link(v.tensor_scalar(t5, rank, float(CAP), None, ALU.is_ge))
            link(v.tensor_tensor(t5, t5, per_e(jump), ALU.mult))
            link(v.tensor_tensor(rank, rank, t5, ALU.add))
            link(v.tensor_tensor(rank, rank, per_e(first_row), ALU.add))
            rows2 = rowsU[:, :].rearrange("p (i c) -> p i c", c=2)
            for c, oh in ((0, oh1), (1, oh2)):
                link(v.tensor_tensor(t5, rank, oh, ALU.mult))
                link(v.tensor_reduce(rv[10], t5, AX.X, ALU.add))
                link(v.tensor_copy(rows2[:, :, c], rv[10]))
            for j in range(EXTRA):
                link(v.tensor_scalar(em[:, 0, :], csum, float(j), 0.0, ALU.is_le, ALU.add, accum_out=ctlf[:, j:j + 1]))
            link(v.tensor_scalar(ctlf[:, 0:EXTRA], ctlf[:, 0:EXTRA], float(NE - 1), None, ALU.min))
            link(v.tensor_copy(ctlf[:, EXTRA:EXTRA + 1], csum[:, NE - 1:NE]))
            v.tensor_copy(ctl[:, :], ctlf)\
                .then_inc(s_rows_ready, 1)
            dve.wait_ge(s_rows_ready, seen(s_rows_ready))

            dve.wait_ge(s_bple_in, 16)
            for n in range(2 * NT):
                ple_sum(n)
                if n:
                    ple_out(n - 1)
            ple_out(2 * NT - 1)

            def hidden(e, u):
                dve.wait_ge(s_tanh_sb, e + 1)
                hg, hu = psum[0:CAP, u % 2, 0:FF], psum[0:CAP, u % 2, FF:2 * FF]
                v.scalar_tensor_tensor(eact[0:CAP, u % 2, :], eth[:, u % 2, :], 1.0, hg, ALU.add, ALU.mult)\
                    .then_inc(s_eact_a, 1)
                dve.wait_ge(s_eact_a, e + 1)
                v.tensor_tensor(eact[0:CAP, u % 2, :], eact[0:CAP, u % 2, :], hu, ALU.mult).then_inc(s_eact_sb, 1)

            def out_half(e, u):
                dve.wait_ge(s_y_mm, e + 1)
                if not (isinstance(e, int) and e < 2):
                    dve.wait_ge(y_st[u % 2], (e - u % 2) * 8 if not isinstance(e, int) else e // 2 * 16)
                v.tensor_copy(eout[:, u % 2, 512:1024], psum[0:CAP, 5 + 2 * (u % 2), :]).then_inc(s_y_dve, 1)

            def step(e4, u, first=False):
                e = e4 * 4 + u
                hidden(e, u)
                if not (first and u == 0):
                    out_half(e - 1, (u - 1) % 4)

            dve.wait_ge(s_scattered, 16 * 2 * NT)
            link(v.memset(eact[CAP:P], 0.0))
            for u in range(4):
                step(0, u, first=True)
            with dve.Fori(1, NE // 4) as e4:
                for u in range(4):
                    step(e4, u)
            out_half(NE - 1, 3)
            total = dve.value_load(ctl[0:1, EXTRA:EXTRA + 1], min_val=0, max_val=EXTRA)
            with dve.Fori(0, EXTRA) as j:
                with dve.If(total > j):
                    e = j + NE
                    hidden(e, 0)
                    dve.wait_ge(s_y_mm, e + 1)
                    dve.wait_ge(y_st[0], j * 16 + NE // 2 * 16)
                    v.tensor_copy(eout[:, 0, 512:1024], psum[0:CAP, 5, :]).then_inc(s_y_dve, 1)
                dve.nop()

            dve.wait_ge(s_ln2_in, 32)
            for i in range(NT):
                dve.wait_ge(y_gath[i % 2], 32 * (i // 2 + 1))
                x = sz[:, i, :]
                for c in range(2):
                    v.scalar_tensor_tensor(x, ygat[:, i % 2, c, :], rv[8 + c][:, i:i + 1], x, ALU.mult, ALU.add)\
                        .then_inc(s_combined, 1)
                    dve.wait_ge(s_combined, 2 * i + c + 1)
                normed(x, A1w, A1b, s_fin_ready)


_INS = ["x", "p", "ln0_w", "ln0_b", "w_in", "b_gate", "conv_w", "conv_b", "dt_bias", "a_log", "d_skip", "ssd_norm_w",
        "sinks", "w_out_attn", "w_out_ssd", "w_out", "ln1_w", "ln1_b", "w_router_group", "b_router_group",
        "w_router_expert", "b_router_expert", "w_exp_gate", "w_exp_up", "w_exp_down", "w_ple", "w_ple_gate",
        "b_ple_gate", "ln2_w", "ln2_b"]


def kernel(**inputs):
    import numpy as _np
    import concourse.bacc as _bacc
    from concourse import mybir as _mybir
    from concourse.bass_utils import run_bass_kernel_spmd as _run

    nc = _bacc.Bacc("TRN2", target_bir_lowering=False, num_devices=1)
    arrays, aps = {}, {}
    for name in _INS:
        a = _np.ascontiguousarray(inputs[name])
        arrays[f"in_{name}_dram"] = a
        aps[name] = nc.dram_tensor(f"in_{name}_dram", a.shape, _mybir.dt.from_np(a.dtype), kind="ExternalInput").ap()
    out = nc.dram_tensor("out_0_dram", (1, S, D), F32, kind="ExternalOutput").ap()
    block_kernel(nc, aps, out)
    r = _run(nc, [arrays], core_ids=[0])
    return r.results[0]["out_0_dram"]
```

```python
from contextlib import ExitStack

import concourse.bass as bass
from concourse import mybir

ALU = mybir.AluOpType
ACT = mybir.ActivationFunctionType
F32 = mybir.dt.float32
I32 = mybir.dt.int32
U32 = mybir.dt.uint32
AX = mybir.AxisListType

P = 128
D = 1024
S = 512
NT = S // P
KD = D // P
HEADS, HD = 8, 64
SSDH, SP, SN = 16, 64, 64
CONV_W = 4
XBC = 1280
NX = XBC // P
COL_KV, COL_Z, COL_XBC, COL_DT, COL_GATE = 512, 768, 1792, 3072, 3088
NG, NPG, NE, FF = 4, 8, 32, 256
PLE = 256
ALPHA = 2.0 ** 0.25
LN_EPS = 1e-5
RMS_EPS = 1e-5
NEG = -1e30

SLOTS, SLOT = 12, 2048
CAP = 64
EXTRA = 2 * S // CAP - 1
PAIRS = NE // 2
MORE_PAIRS = (EXTRA + 1) // 2
ROWS = (PAIRS + MORE_PAIRS) * 2 * CAP
ZERO_DMAS = (ROWS + ROWS - NE * CAP) // P // 2
PS = 256


def stream_order(aps):
    w_in = aps["w_in"][0].rearrange("(k p) n -> p k n", p=P)

    def cols(c):
        return [(w_in[:, :, c:c + 256], slice(0, P), "kn", slice(0, 256))]

    out = [cols(COL_XBC + 256 * s) for s in range(5)]
    out += [cols(COL_KV)]
    for s in range(2):
        out.append([(w_in[:, :, 256 * g + 64 * (2 * s + j):][:, :, 0:64], slice(0, P), "kn",
                     slice(128 * j + 64 * g, 128 * j + 64 * g + 64)) for j in range(2) for g in range(2)])
    out += [cols(COL_Z + 256 * s) for s in range(4)]

    def gates(s):
        return [cols(COL_GATE + 256 * s), cols(COL_GATE + D + 256 * s)]

    for s in range(4):
        out += gates(s)
    woa = aps["w_out_attn"][0].rearrange("(g s j d) n -> g s d j n", g=2, s=2, j=2)
    for s in range(2):
        out.append([(woa[g, s], slice(64 * g, 64 * g + 64), "kN", slice(0, D)) for g in range(2)])

    def rows(w, s):
        return [(w[256 * s:256 * s + 256, :].rearrange("(k p) n -> p k n", p=P), slice(0, P), "kN",
                 slice(0, D))]

    out += [rows(aps["w_out_ssd"][0], s) for s in range(4)]
    out += [rows(aps["w_out"][0], s) for s in range(4)]
    assert len(out) == len(SLOT_OF)
    return out


SEQ_XBC, SEQ_KV, SEQ_Q, SEQ_Z, SEQ_WOA, SEQ_WOS, SEQ_WO = (0, 5, 6, 8, 20, 22, 26)
SEQ_GATE = (12, 14, 16, 18)
SLOT_OF = [*range(12), *range(8), *range(8), 8, 9]
GATE_SLOT = 8


def slot_freed():
    out = [("pe_xbc", 2 * s + 2) for s in range(5)] + [("pe_kv", 2)] + [("pe_q", 2), ("pe_q", 4)]
    for s in range(4):
        out += [("pe_g", 4 * s + 3), ("pe_g", 4 * s + 4)]
    return out + [("ys_read", 2), ("ys_read", 4)]


FREED = slot_freed()
MOE_FREED = ([("pe_ya", KD)] * 2 + [("pe_ys", KD)] * 4 + [("pe_mix", 2 * NT)] * 4 + [("ys_read", KD)] * 2)
RANKS_AFTER = 2


def psum_plan(sems):
    units = []

    def unit(key, banks, *free):
        units.append((key, banks, [(sems[n], v) for n, v in free]))

    for i in range(NT):
        for b in range(2):
            unit(("hT", i, b), 1, ("hT_read", 2 * i + b + 1))
    unit("par", 1, ("par_read", 1))
    for n in range(NX):
        unit(("xbc", n), 1, ("conv_read", n + 1))
    unit("dt", 1, ("dt_read", 1))
    unit("k", 1, ("kv_read", 1))
    unit("v", 1, ("kv_read", 2))
    for j in range(4):
        unit(("q", j), 1, ("q_read", j + 1))

    def z(n):
        unit(("z", n), 1, ("z_read", n + 1))

    def sc(n):
        unit(("sc", n), 2, ("sc_read", n + 1))

    sc(0)
    for n in range(8):
        z(n)
        if n < 7:
            sc(n + 1)
        if n:
            unit(("av", n - 1), 1, ("av_read", n))
        unit(("pt", n), 2, ("pt_read", n + 1))
    unit(("av", 7), 1, ("av_read", 8))
    gates = iter(range(2 * KD))

    def gate():
        g = next(gates)
        unit(("g", g), 1, ("g_read", g + 1))

    for c in range(NT):
        unit(("xt", c), 2, ("xt_read", c + 1))
        unit(("cb", c), 2, ("cb_act", c + 1), ("cb_dve", c + 1))
        for q in range(4):
            unit(("seg", c, q), 1, ("seg_read", 4 * c + q + 1))
        gate()
        if c:
            unit(("yo", c), 2, ("yo_read", c))
        unit(("yd", c), 2, ("yd_read", c + 1))
        gate()
        if c < NT - 1:
            unit(("st", c), 1, ("st_read", c + 1))
        gate()
        unit(("yT", c), 2, ("yT_read", c + 1))
    for g in gates:
        unit(("g", g), 1, ("g_read", g + 1))
    for n in range(KD):
        unit(("ya", n), 1, ("ya_read", n + 1))
        unit(("ys", n), 1, ("ys_read", n + 1))
    for i in range(NT):
        for b in range(2):
            unit(("mix", i, b), 1, ("mix_read", 2 * i + b + 1))
    for kk in range(2):
        unit(("pT", kk), 1, ("pT_read", kk + 1))
    for i in range(NT):
        unit(("h1T", i), 2, ("h1T_read", i + 1))
        if i == 1:
            unit("rt", 1, ("rt_read", 1))
    for n in range(4 * NT):
        unit(("pl", n), 1, ("pp_read", n + 1))
        if n == RANKS_AFTER:
            unit("rk", 1, ("rk_read", 1))
    place, holder, at = {}, [[] for _ in range(8)], 0
    for key, banks, free in units:
        if banks == 2:
            at += at % 2
        at %= 8
        need = {}
        for b in range(at, at + banks):
            for s, v in holder[b]:
                need[s.name] = (s, max(v, need.get(s.name, (s, 0))[1]))
            holder[b] = free
        place[key] = (at, list(need.values()))
        at += banks
    last = {}
    for b in range(8):
        for s, v in holder[b]:
            last[s.name] = (s, max(v, last.get(s.name, (s, 0))[1]))
    return place, list(last.values())


def block_kernel(nc, aps, out):
    with ExitStack() as ctx:
        def sem(name):
            return ctx.enter_context(nc.semaphore(name))

        arena = ctx.enter_context(nc.sbuf_tensor("arena", [P, 52896], F32))
        place = [0]

        def region(n):
            a = place[0]
            place[0] += n
            return a

        def at(base, n, parts=(0, P)):
            return arena[parts[0]:parts[0] + parts[1], base:base + n]

        def shaped(base, pattern, **k):
            n = 1
            for v in k.values():
                n *= v
            return at(base, n).rearrange(pattern, **k)

        R_RING = region(SLOTS * SLOT)
        R_H, R_T, R_Z = region(4096), region(4096), region(4096)
        R_X = region(5120)
        R_Y = region(2048)
        R_A = region(7168)
        ring = shaped(R_RING, "p (s k n) -> p s k n", s=SLOTS, k=KD, n=256)
        ringN = shaped(R_RING, "p (s k n) -> p s k n", s=SLOTS, k=2, n=D)
        h = shaped(R_H, "p (i n) -> p i n", i=NT, n=D)
        hT = shaped(R_T, "p (k t) -> p k t", k=KD, t=S)
        sz = shaped(R_Z, "p (i n) -> p i n", i=NT, n=D)
        yT = shaped(R_Z, "p (i k t) -> p i k t", i=NT, k=KD, t=P)
        xs = shaped(R_X, "p (n t) -> p n t", n=NX, t=S)
        mixT = shaped(R_X, "p (n t) -> p n t", n=KD, t=S)
        yaT = shaped(R_Y, "p (j t) -> p j t", j=4, t=S)
        qT = shaped(R_A, "p (j t) -> p j t", j=4, t=S)
        kT = at(R_A + 2048, S)
        vt = shaped(R_A + 2560, "p (i n) -> p i n", i=NT, n=P)
        bias = shaped(R_A + 3072, "p (m w) -> p m w", m=8, w=256)
        prob = shaped(R_A + 5120, "p (m w) -> p m w", m=4, w=256)
        probT = shaped(R_A + 6144, "p (m w t) -> p m w t", m=4, w=2, t=P)
        ln_w, ln_b = at(R_A + 5120, D), at(R_A + 6144, D)
        ctanh = shaped(R_Z, "p (b t) -> p b t", b=2, t=S)
        xtok = at(R_A, D)
        xdt = at(R_A + 1024, D)
        xdec = at(R_A + 2048, D)
        y = at(R_A + 3072, D)
        lmat = shaped(R_A + 4096, "p (b m t) -> p b m t", b=2, m=4, t=P)
        state = at(R_A + 5120, 512)
        btok = at(R_A + 5632, P)
        cbm = shaped(R_A + 5760, "p (g t) -> p g t", g=2, t=P)
        tmp = at(R_A + 6016, D)
        A1w, A1b = at(R_A, D), at(R_A + 1024, D)
        bple = at(R_A + 2048, D)
        gact = shaped(R_RING + GATE_SLOT * SLOT, "p (n g t) -> p n g t", n=KD, g=2, t=S)
        gtmp = shaped(R_A + 5120, "p (b t) -> p b t", b=2, t=S)
        p_in = shaped(R_A + 6144, "p (i n) -> p i n", i=NT, n=PLE)
        pT = shaped(R_X + 4096, "p (k t) -> p k t", k=2, t=S)
        pgw = [shaped(r, "p (k n) -> p k n", k=KD, n=PS) for r in (R_A + 3072, R_Y)]
        wple = shaped(R_X + 2048, "p (k n) -> p k n", k=2, n=D)
        pgt = shaped(R_A + 6144, "p (b t) -> p b t", b=4, t=PS)
        xg = shaped(R_X, "p (b n) -> p b n", b=2, n=D)
        xgT = shaped(R_X + 2048, "p (b k t) -> p b k t", b=2, k=KD, t=P)
        eact = shaped(R_H, "p (b n) -> p b n", b=2, n=FF)
        eth = shaped(R_H + 2 * FF, "p (b n) -> p b n", b=2, n=FF)
        eactT = shaped(R_H + 4 * FF, "p (b k t) -> p b k t", b=2, k=2, t=P)
        eout = shaped(R_Y, "p (b n) -> p b n", b=2, n=D)
        ygat = shaped(R_RING, "p (i c n) -> p i c n", i=NT, c=2, n=D)
        ident, upper, ones, upstrict = (at(region(P), P) for _ in range(4))
        par_rows = at(R_A, P, (0, 74))
        par = at(region(74), 74)
        conv_w = par[:, 0:40].rearrange("p (w n) -> p w n", w=CONV_W)
        conv_b, b_gate, norm_w = par[:, 40:50], par[:, 50:66], par[:, 66:74]
        w_dt = shaped(region(KD * 16), "p (k n) -> p k n", k=KD, n=16)
        w_rt = shaped(region(KD * 36), "p (k n) -> p k n", k=KD, n=36)
        brow = region(16 * 3 + 8 + 36)
        dt_bias, a_row, dskip = (at(brow + 16 * j, 16) for j in range(3))
        sink = at(brow + 48, 8)
        rbias = at(brow + 56, 36)
        stats = at(region(12), 12)
        mv = at(region(8), 8)
        dtv = shaped(region(64), "p (i n) -> p i n", i=NT, n=16)
        dta = shaped(region(64), "p (i n) -> p i n", i=NT, n=16)
        R_SM = region(192)
        acs = shaped(R_SM, "p (a n) -> p a n", a=8, n=16)
        att = shaped(R_SM + 128, "p (b a n) -> p b a n", b=2, a=6, n=4)
        lg = shaped(region(NT * 36), "p (i n) -> p i n", i=NT, n=36)
        rw = [shaped(R_A + 5120 + NT * NE * j, "p (i n) -> p i n", i=NT, n=NE) for j in range(6)]
        rv = [at(region(NT), NT) for _ in range(12)]
        iota_e = at(region(NE), NE)
        cnt = [at(R_A + 5888 + NE * j, NE) for j in range(6)]
        ctlf = at(region(EXTRA + 2), EXTRA + 2)
        mva = shaped(region(2 * NT), "p (i n) -> p i n", i=NT, n=2)
        rowsU = ctx.enter_context(nc.sbuf_tensor("rowsU", [P, 2 * NT], U32))
        ctl = ctx.enter_context(nc.sbuf_tensor("ctl", [P, EXTRA + 2], I32))
        psum = ctx.enter_context(nc.psum_tensor("psum", [P, 8, 512], F32))

        xg_dram = nc.dram_tensor("xg_rows", [ROWS, D], F32).ap()
        y_dram = nc.dram_tensor("y_rows", [ROWS, D], F32).ap()

        slot_in = [sem(f"slot_in{s}") for s in range(SLOTS)]
        s_aT_mm = sem("aT_mm")
        s_aT_sb = sem("aT_sb")
        s_acs_exp = sem("acs_exp")
        s_act_step = sem("act_step")
        s_ah_ready = sem("ah_ready")
        s_av_read = sem("av_read")
        s_ah1_ready = sem("ah1_ready")
        s_base_ready = sem("base_ready")
        s_blocks_stored = sem("blocks_stored")
        s_bple_in = sem("bple_in")
        s_cb_act = sem("cb_act")
        s_cb_dve = sem("cb_dve")
        s_combined = sem("combined")
        s_consts = sem("consts")
        s_conv_read = sem("conv_read")
        s_ctl_ready = sem("ctl_ready")
        s_ctanh_done = sem("ctanh_done")
        s_dist_in = sem("dist_in")
        s_dt_exp = sem("dt_exp")
        s_dt_exp_in = sem("dt_exp_in")
        s_dt_read = sem("dt_read")
        s_dta_ready = sem("dta_ready")
        s_dve_step = sem("dve_step")
        s_eact_a = sem("eact_a")
        s_eact_sb = sem("eact_sb")
        s_exp_done = sem("exp_done")
        s_fin_ready = sem("fin_ready")
        s_g_read = sem("g_read")
        s_gu_mm = sem("gu_mm")
        s_h1T_read = sem("h1T_read")
        s_h1_ready = sem("h1_ready")
        s_hT_read = sem("hT_read")
        s_h_ready = sem("h_ready")
        s_kv_read = sem("kv_read")
        s_lmat_exp = sem("lmat_exp")
        s_ln0_in = sem("ln0_in")
        s_ln1_in = sem("ln1_in")
        s_ln2_in = sem("ln2_in")
        s_m_ready = sem("m_ready")
        s_mix_read = sem("mix_read")
        s_mix_ready = sem("mix_ready")
        s_nmax_ready = sem("nmax_ready")
        s_out_st = sem("out_st")
        s_pT_read = sem("pT_read")
        s_p_in = sem("p_in")
        s_par_in = sem("par_in")
        s_par_read = sem("par_read")
        s_pe_av = sem("pe_av")
        s_pe_cb = sem("pe_cb")
        s_pe_dt = sem("pe_dt")
        s_pe_g = sem("pe_g")
        s_pe_h1T = sem("pe_h1T")
        s_pe_hT = sem("pe_hT")
        s_pe_kv = sem("pe_kv")
        s_pe_mix = sem("pe_mix")
        s_pe_pT = sem("pe_pT")
        s_pe_par = sem("pe_par")
        s_pe_pl = sem("pe_pl")
        s_pe_pt = sem("pe_pt")
        s_pe_q = sem("pe_q")
        s_pe_rk = sem("pe_rk")
        s_pe_rt = sem("pe_rt")
        s_pe_sc = sem("pe_sc")
        s_pe_seg = sem("pe_seg")
        s_pe_st = sem("pe_st")
        s_pe_xbc = sem("pe_xbc")
        s_pe_xt = sem("pe_xt")
        s_pe_yT = sem("pe_yT")
        s_pe_ya = sem("pe_ya")
        s_pe_yd = sem("pe_yd")
        s_pe_yo = sem("pe_yo")
        s_pe_ys = sem("pe_ys")
        s_pe_z = sem("pe_z")
        s_pg_read = sem("pg_read")
        s_pg_tanh = sem("pg_tanh")
        s_pool_step = sem("pool_step")
        s_pp_read = sem("pp_read")
        s_prob_ready = sem("prob_ready")
        s_pt_read = sem("pt_read")
        s_q_read = sem("q_read")
        s_rk_read = sem("rk_read")
        s_rows_ready = sem("rows_ready")
        s_rt_exp = sem("rt_exp")
        s_rt_exp_in = sem("rt_exp_in")
        s_rt_read = sem("rt_read")
        s_sc_read = sem("sc_read")
        s_scattered = sem("scattered")
        s_seg_read = sem("seg_read")
        s_sel_ready = sem("sel_ready")
        s_silu_done = sem("silu_done")
        s_small_in = sem("small_in")
        s_st_read = sem("st_read")
        s_tanh_sb = sem("tanh_sb")
        s_tz_done = sem("tz_done")
        s_wple_in = sem("wple_in")
        s_wsmall_in = sem("wsmall_in")
        s_xT_mm = sem("xT_mm")
        s_xdec_ready = sem("xdec_ready")
        s_xdt_ready = sem("xdt_ready")
        s_xgT_sb = sem("xgT_sb")
        s_xt_read = sem("xt_read")
        s_yT_read = sem("yT_read")
        s_y_act = sem("y_act")
        s_y_dve = sem("y_dve")
        s_y_mm = sem("y_mm")
        s_y_ready = sem("y_ready")
        s_ya_read = sem("ya_read")
        s_yd_read = sem("yd_read")
        s_yo_read = sem("yo_read")
        s_ys_read = sem("ys_read")
        s_z_read = sem("z_read")
        s_zero_set = sem("zero_set")
        s_zeroed = sem("zeroed")
        sems = {x.name: x for x in (
            s_av_read, s_cb_act, s_cb_dve, s_conv_read, s_dt_read, s_g_read, s_h1T_read, s_hT_read,
            s_kv_read, s_mix_read, s_pT_read, s_par_read, s_pg_read, s_pp_read, s_pt_read, s_q_read,
            s_rk_read, s_rt_read, s_sc_read, s_seg_read, s_st_read, s_xt_read, s_yT_read, s_ya_read,
            s_yd_read, s_yo_read, s_ys_read, s_z_read, s_pe_g, s_pe_kv, s_pe_mix, 
            s_pe_q, s_pe_xbc, s_pe_ya, s_pe_ys, s_pe_z)}
        x_in = [sem(f"x_in{i}") for i in range(NT)]
        xg_in = [sem(f"xg_in{b}") for b in range(2)]
        y_gath = [sem(f"y_gath{i}") for i in range(NT)]
        pgw_in = [sem(f"pgw_in{b}") for b in range(2)]
        y_st = [sem(f"y_st{b}") for b in range(2)]
        plan, plan_last = psum_plan(sems)

        def bank(key, n=512, banks=1):
            b = plan[key][0]
            flat = psum[:, b:b + banks, :].rearrange("p b n -> p (b n)")
            return flat[:, 0:n]

        loads = stream_order(aps)
        wg = aps["w_exp_gate"].rearrange("l g e d f -> (l g e) d f")
        wu = aps["w_exp_up"].rearrange("l g e d f -> (l g e) d f")
        wd = aps["w_exp_down"].rearrange("l g e f d -> (l g e) f d")
        x_v = aps["x"][0].rearrange("(i p) n -> p i n", p=P)
        p_v = aps["p"][0, 0].rearrange("(i p) n -> p i n", p=P)
        out_v = out[0].rearrange("(i p) n -> i p n", p=P)
        zview = xg_dram.rearrange("(p r) n -> p r n", p=P)

        def landings(slot, seq):
            return sum(len(loads[q]) for q in range(seq + 1) if SLOT_OF[q] == slot)

        def arrived(eng, seq):
            eng.wait_ge(slot_in[SLOT_OF[seq]], 16 * landings(SLOT_OF[seq], seq))

        def expert_slot(parity, half, w):
            return 6 * parity + 3 * half + w

        def expert_slot_in(eng, former, parity, half, w):
            s = expert_slot(parity, half, w)
            eng.wait_ge(slot_in[s], former * 16 + 16 * (landings(s, len(loads) - 1) + 1))

        block = ctx.enter_context(nc.Block())

        @block.sync
        def _(sp):
            for i in range(NT):
                sp.dma_start(h[:, i, :], x_v[:, i, :]).then_inc(x_in[i], 16)
            for seq, parts in enumerate(loads):
                slot = SLOT_OF[seq]
                if seq >= SLOTS:
                    name, value = FREED[seq - SLOTS]
                    sp.wait_ge(sems[name], value)
                for src, rows, kind, columns in parts:
                    view = (ring if kind == "kn" else ringN)[rows, slot, :, columns]
                    sp.dma_start(view, src).then_inc(slot_in[slot], 16)
                if seq == 3:
                    sp.dma_start(w_dt, aps["w_in"][0].rearrange("(k p) n -> p k n", p=P)[:, :, COL_DT:COL_DT + 16])\
                        .then_inc(s_wsmall_in, 16)
                    sp.dma_start(w_rt[:, :, 0:NG], aps["w_router_group"][0].rearrange("(k p) n -> p k n", p=P))\
                        .then_inc(s_wsmall_in, 16)
                    sp.dma_start(w_rt[:, :, NG:36], aps["w_router_expert"][0].rearrange("(k p) n -> p k n", p=P))\
                        .then_inc(s_wsmall_in, 16)

            w_pg = aps["w_ple_gate"][0].rearrange("(k p) n -> p k n", p=P)

            def gate_slice(s):
                sp.dma_start(pgw[s % 2], w_pg[:, :, PS * s:PS * (s + 1)]).then_inc(pgw_in[s % 2], 16)

            def experts(p, u):
                for half in range(2):
                    for w, t in ((0, wg), (1, wu)):
                        if isinstance(p, int) and p < 2:
                            name, value = MOE_FREED[6 * p + 3 * half + w]
                            sp.wait_ge(sems[name], value)
                        elif half == w == 0:
                            sp.wait_ge(s_gu_mm, p - 1)
                        src = t[bass.ds(p * 2 + half, 1)].rearrange("a (k p) f -> p (a k) f", p=P)
                        slot = expert_slot(u % 2, half, w)
                        sp.dma_start(ring[:, slot], src).then_inc(slot_in[slot], 16)
                for half in range(2):
                    if isinstance(p, int) and p < 2:
                        name, value = MOE_FREED[6 * p + 3 * half + 2]
                        sp.wait_ge(sems[name], value)
                    elif half == 0:
                        sp.wait_ge(s_y_mm, p - 1)
                    src = wd[bass.ds(p * 2 + half, 1)].rearrange("a (k p) n -> p (a k) n", p=P)
                    slot = expert_slot(u % 2, half, 2)
                    sp.dma_start(ringN[:, slot], src).then_inc(slot_in[slot], 16)

            sp.wait_ge(s_pe_ya, KD)
            gate_slice(1)
            sp.wait_ge(s_ys_read, KD)
            gate_slice(0)
            sp.wait_ge(s_pe_mix, 2 * NT)
            sp.dma_start(wple, aps["w_ple"][0].rearrange("(k p) n -> p k n", p=P)).then_inc(s_wple_in, 16)
            experts(0, 0)
            sp.wait_ge(s_pe_pl, NT)
            gate_slice(2)
            sp.wait_ge(s_pe_pl, 2 * NT)
            gate_slice(3)
            for u in range(1, 4):
                experts(u, u)
            with sp.Fori(1, PAIRS // 4) as e4:
                for u in range(4):
                    experts(e4 * 4 + u, u)
            sp.wait_ge(s_ctl_ready, 1)
            pairs = sp.value_load(ctl[0:1, EXTRA + 1:EXTRA + 2], min_val=0, max_val=MORE_PAIRS)
            with sp.Fori(0, MORE_PAIRS) as j:
                with sp.If(pairs > j):
                    sp.wait_ge(s_y_mm, j + PAIRS)
                    for half in range(2):
                        e = sp.value_load(ctl[0:1, bass.ds(j * 2 + half, 1)], min_val=0, max_val=NE - 1)
                        for w, t in ((0, wg), (1, wu)):
                            src = t[bass.ds(e, 1)].rearrange("a (k p) f -> p (a k) f", p=P)
                            slot = expert_slot(0, half, w)
                            sp.dma_start(ring[:, slot], src).then_inc(slot_in[slot], 16)
                        src = wd[bass.ds(e, 1)].rearrange("a (k p) n -> p (a k) n", p=P)
                        slot = expert_slot(0, half, 2)
                        sp.dma_start(ringN[:, slot], src).then_inc(slot_in[slot], 16)
                sp.nop()

        @block.gpsimd
        def _(pool):
            steps = [0]

            def link(ins):
                steps[0] += 1
                ins.then_inc(s_pool_step, 1)
                pool.wait_ge(s_pool_step, steps[0])

            g = nc.gpsimd
            pool.dma_start(ln_w, aps["ln0_w"].rearrange("(a n) -> a n", a=1).broadcast_to([P, D])).then_inc(s_ln0_in, 16)
            pool.dma_start(ln_b, aps["ln0_b"].rearrange("(a n) -> a n", a=1).broadcast_to([P, D])).then_inc(s_ln0_in, 16)
            link(g.memset(ones, 1.0))
            g.affine_select(out=ident, in_=ones, pattern=[[1, P]], compare_op=ALU.is_equal, fill=0.0, base=0,
                            channel_multiplier=-1).then_inc(s_consts, 1)
            g.affine_select(out=upper, in_=ones, pattern=[[1, P]], compare_op=ALU.is_ge, fill=0.0, base=0,
                            channel_multiplier=-1).then_inc(s_consts, 1)
            g.affine_select(out=upstrict, in_=ones, pattern=[[1, P]], compare_op=ALU.is_gt, fill=0.0, base=0,
                            channel_multiplier=-1).then_inc(s_consts, 1)
            g.iota(iota_e, pattern=[[1, NE]], base=0, channel_multiplier=0,
                   allow_small_or_imprecise_dtypes=True).then_inc(s_consts, 1)
            pool.dma_start(par_rows[0:40], aps["conv_w"][0].rearrange("w (n p) -> (w n) p", p=P)).then_inc(s_par_in, 16)
            pool.dma_start(par_rows[40:50], aps["conv_b"].rearrange("l (n p) -> (l n) p", p=P)).then_inc(s_par_in, 16)
            pool.dma_start(par_rows[50:66], aps["b_gate"][0].rearrange("b (n p) -> (b n) p", p=P)).then_inc(s_par_in, 16)
            pool.dma_start(par_rows[66:74], aps["ssd_norm_w"].rearrange("l (n p) -> (l n) p", p=P)).then_inc(s_par_in, 16)
            for dst, name in ((dt_bias, "dt_bias"), (a_row, "a_log"), (dskip, "d_skip"), (sink, "sinks"),
                              (rbias[:, 0:NG], "b_router_group"), (rbias[:, NG:36], "b_router_expert")):
                pool.dma_start(dst, aps[name].broadcast_to([P, dst.shape[1]])).then_inc(s_small_in, 16)
            dist, mask = xs[:, 8, 0:256], xs[:, 9, 0:256]
            link(g.iota(dist, pattern=[[-1, 256]], base=P, channel_multiplier=1, allow_small_or_imprecise_dtypes=True))
            link(g.memset(mask, 0.0))
            link(g.memset(mask[0:64, 0:64], NEG))
            link(g.memset(mask[0:64, 192:256], NEG))
            g.memset(mask[64:128, 0:128], NEG).then_inc(s_dist_in, 1)
            zt = shaped(R_Y, "p (r n) -> p r n", r=2, n=D)
            pool.wait_ge(s_dist_in, 1)
            g.memset(zt, 0.0).then_inc(s_zero_set, 1)
            pool.wait_ge(s_zero_set, 1)
            for r in range(0, ROWS // P, 2):
                pool.dma_start(zview[:, r:r + 2, :], zt).then_inc(s_zeroed, 16)
            zview_y = y_dram[NE * CAP:ROWS].rearrange("(p r) n -> p r n", p=P)
            for r in range(0, zview_y.shape[1], 2):
                pool.dma_start(zview_y[:, r:r + 2, :], zt).then_inc(s_zeroed, 16)
            pool.wait_ge(s_pe_hT, 2 * NT)
            for i in range(NT):
                g.tensor_scalar(h[:, i, :], h[:, i, :], ALPHA, None, ALU.mult).then_inc(s_ah_ready, 1)
            pool.wait_ge(s_pe_yT, NT)
            for dst, name, landed in ((A1w, "ln1_w", s_ln1_in), (A1b, "ln1_b", s_ln1_in), (bple, "b_ple_gate", s_bple_in)):
                pool.dma_start(dst, aps[name].broadcast_to([P, D])).then_inc(landed, 16)
            pool.dma_start(p_in, p_v).then_inc(s_p_in, 16)
            pool.wait_ge(s_h1_ready, NT)
            for dst, name in ((A1w, "ln2_w"), (A1b, "ln2_b")):
                pool.dma_start(dst, aps[name].broadcast_to([P, D])).then_inc(s_ln2_in, 16)
            for i in range(NT):
                g.tensor_scalar(sz[:, i, :], h[:, i, :], ALPHA, None, ALU.mult).then_inc(s_ah1_ready, 1)
            pool.wait_ge(s_zeroed, 16 * ZERO_DMAS)
            pool.wait_ge(s_rows_ready, 2)
            for i in range(NT):
                for c in range(2):
                    g.indirect_dma_start(
                        out=xg_dram, out_offset=bass.IndirectOffsetOnAxis(ap=rowsU[:, 2 * i + c:2 * i + c + 1], axis=0),
                        in_=h[:, i, :], in_offset=None, bounds_check=ROWS - 1, oob_is_err=False)\
                        .then_inc(s_scattered, 16)
            pool.wait_ge(s_blocks_stored, 1)
            for i in range(NT):
                for c in range(2):
                    g.indirect_dma_start(
                        out=ygat[:, i, c, :], out_offset=None, in_=y_dram,
                        in_offset=bass.IndirectOffsetOnAxis(ap=rowsU[:, 2 * i + c:2 * i + c + 1], axis=0),
                        bounds_check=ROWS - 1, oob_is_err=False).then_inc(y_gath[i], 16)

        @block.tensor
        def _(pe):
            mm, tr = nc.tensor.matmul, nc.tensor.transpose

            def opened(key, n=512, banks=1):
                for s, v in plan[key][1]:
                    pe.wait_ge(s, v)
                return bank(key, n, banks)

            pe.wait_ge(s_consts, 4)
            for i in range(NT):
                pe.wait_ge(s_h_ready, i + 1)
                for b in range(2):
                    o = opened(("hT", i, b))
                    for k in range(4):
                        c = (4 * b + k) * P
                        t = tr(o[:, k * P:(k + 1) * P], h[:, i, c:c + P], ident)
                    t.then_inc(s_pe_hT, 1)
            pe.wait_ge(s_par_in, 64)
            tr(opened("par")[:, 0:74], par_rows, ident[0:74, 0:74]).then_inc(s_pe_par, 1)
            pe.wait_ge(s_hT_read, 2 * NT)

            def proj(o, weight, signal):
                for k in range(KD):
                    t = mm(o, weight(k), hT[:, k, :], start=(k == 0), stop=(k == KD - 1))
                t.then_inc(signal, 1)


            for n in range(NX):
                seq = SEQ_XBC + n // 2
                arrived(pe, seq)
                proj(opened(("xbc", n)), lambda k: ring[:, SLOT_OF[seq], k, (n % 2) * P:(n % 2 + 1) * P], s_pe_xbc)
            pe.wait_ge(s_wsmall_in, 16 * 3)
            o = opened("dt", 64)
            for i in range(NT):
                for k in range(KD):
                    t = mm(o[:, 16 * i:16 * i + 16], hT[:, k, i * P:(i + 1) * P], w_dt[:, k, :], start=(k == 0),
                           stop=(k == KD - 1))
            t.then_inc(s_pe_dt, 1)
            arrived(pe, SEQ_KV)
            proj(opened("k"), lambda k: ring[:, SEQ_KV, k, 0:P], s_pe_kv)
            o = opened("v")
            for i in range(NT):
                for k in range(KD):
                    t = mm(o[:, i * P:(i + 1) * P], hT[:, k, i * P:(i + 1) * P], ring[:, SEQ_KV, k, P:2 * P],
                           start=(k == 0), stop=(k == KD - 1))
            t.then_inc(s_pe_kv, 1)
            for j in range(4):
                arrived(pe, SEQ_Q + j // 2)
                proj(opened(("q", j)), lambda k: ring[:, SEQ_Q + j // 2, k, (j % 2) * P:(j % 2 + 1) * P], s_pe_q)

            def scores(n):
                i, hf = divmod(n, 2)
                w = 256 if i else P
                if n == 0:
                    pe.wait_ge(s_kv_read, 2)
                    pe.wait_ge(s_q_read, 4)
                o = opened(("sc", n), D, 2).rearrange("p (m w) -> p m w", m=4)
                for m in (0, 2, 1, 3):
                    g = (m // 2) * HD
                    t = mm(o[:, m, 0:w], qT[g:g + HD, 2 * hf + m % 2, i * P:(i + 1) * P],
                           kT[g:g + HD, (i + 1) * P - w:(i + 1) * P], start=True, stop=True)
                t.then_inc(s_pe_sc, 1)

            def zproj(n):
                i, b = divmod(n, 2)
                for s in range(2):
                    arrived(pe, SEQ_Z + 2 * b + s)
                o = opened(("z", n))
                for k in range(KD):
                    s = SEQ_Z + 2 * b
                    t = mm(o, hT[:, k, i * P:(i + 1) * P], ring[:, s:s + 2, k, :], start=(k == 0), stop=(k == KD - 1))
                t.then_inc(s_pe_z, 1)

            def probs_t(n):
                i = n // 2
                kt = 2 if i else 1
                pe.wait_ge(s_prob_ready, n + 1)
                o = opened(("pt", n), D, 2).rearrange("p (m w t) -> p m w t", m=4, w=2)
                for m in range(4):
                    for w in range(kt):
                        t = tr(o[:, m, w, :], prob[:, m, w * P:(w + 1) * P], ident)
                t.then_inc(s_pe_pt, 1)

            def attend(n):
                i, hf = divmod(n, 2)
                kt = 2 if i else 1
                pe.wait_ge(s_pt_read, n + 1)
                o = opened(("av", n), 256)
                for m in range(4):
                    g = (m // 2) * HD
                    for w in range(kt):
                        t = mm(o[g:g + HD, (m % 2) * P:(m % 2 + 1) * P], vt[:, i - kt + 1 + w, g:g + HD],
                               probT[:, m, w, :], start=(w == 0), stop=(w == kt - 1))
                t.then_inc(s_pe_av, 1)

            gate_units = iter(range(2 * KD))

            def gate():
                g = next(gate_units)
                n, b = divmod(g, 2)
                seq = SEQ_GATE[n // 2] + b
                arrived(pe, seq)
                proj(opened(("g", g)), lambda k: ring[:, SLOT_OF[seq], k, (n % 2) * P:(n % 2 + 1) * P], s_pe_g)

            scores(0)
            for n in range(8):
                zproj(n)
                if n < 7:
                    scores(n + 1)
                if n:
                    attend(n - 1)
                probs_t(n)
            attend(7)

            pe.wait_ge(s_silu_done, NX)
            pe.wait_ge(s_dta_ready, 1)
            for c in range(NT):
                ts = slice(c * P, (c + 1) * P)
                o = opened(("xt", c), D, 2)
                for k in range(KD):
                    t = tr(o[:, k * P:(k + 1) * P], xs[:, k, ts], ident)
                t.then_inc(s_pe_xt, 1)
                o = opened(("cb", c), D, 2)
                tr(o[:, 0:P], xs[:, 8, ts], ident)
                for g in range(2):
                    gs = slice(64 * g, 64 * g + 64)
                    mm(o[:, P + g * 512:2 * P + g * 512], xs[gs, 8, ts], xs[gs, 9, ts], start=True, stop=True)
                mm(o[:, 256:272], upper, dta[:, c, :], start=True, stop=True)
                mm(o[:, 272:288], ones, dta[:, c, :], start=True, stop=True).then_inc(s_pe_cb, 1)

                def seg(q):
                    o = opened(("seg", c, q))
                    for m in range(4):
                        hh = 4 * q + m
                        t = mm(o[:, m * P:(m + 1) * P], dta[:, c, hh:hh + 1].broadcast_to([P, P]), upper,
                               start=True, stop=True)
                    t.then_inc(s_pe_seg, 1)

                for q in range(4):
                    seg(q)
                gate()
                if c:
                    o = opened(("yo", c), D, 2)
                    pe.wait_ge(s_st_read, c)
                    for g in range(2):
                        gs = slice(64 * g, 64 * g + 64)
                        t = mm(o[:, g * 512:(g + 1) * 512], xs[gs, 9, ts], state[gs, :], start=True, stop=True)
                    t.then_inc(s_pe_yo, 1)
                o = opened(("yd", c), D, 2)
                pe.wait_ge(s_xdt_ready, c + 1)
                for q in range(4):
                    pe.wait_ge(s_m_ready, 4 * c + q + 1)
                    for m in range(4):
                        hh = 4 * q + m
                        t = mm(o[:, hh * SP:(hh + 1) * SP], lmat[:, q % 2, m, :], xdt[:, hh * SP:(hh + 1) * SP],
                               start=True, stop=True)
                    t.then_inc(s_pe_yd, 1)
                    if q == 1:
                        gate()
                if c < NT - 1:
                    o = opened(("st", c))
                    pe.wait_ge(s_xdec_ready, c + 1)
                    pe.wait_ge(s_cb_act, c + 1)
                    for g in range(2):
                        gs = slice(64 * g, 64 * g + 64)
                        t = mm(o[gs, :], btok[:, gs], xdec[:, g * 512:(g + 1) * 512], start=True, stop=True)
                    t.then_inc(s_pe_st, 1)
                gate()
                pe.wait_ge(s_y_ready, c + 1)
                o = opened(("yT", c), D, 2)
                for k in range(KD):
                    t = tr(o[:, k * P:(k + 1) * P], y[:, k * P:(k + 1) * P], ident)
                t.then_inc(s_pe_yT, 1)

            for _ in range(2 * KD - 3 * NT):
                gate()
            pe.wait_ge(s_av_read, 8)
            pe.wait_ge(s_yT_read, NT)
            for s in range(6):
                arrived(pe, SEQ_WOA + s)
            for n in range(KD):
                o = opened(("ya", n))
                for j in range(4):
                    s = SLOT_OF[SEQ_WOA + j // 2]
                    t = mm(o, ringN[:, s, j % 2, n * P:(n + 1) * P], yaT[:, j, :], start=(j == 0), stop=(j == 3))
                t.then_inc(s_pe_ya, 1)
                o = opened(("ys", n)).rearrange("p (i t) -> p i t", i=NT)
                for k in range(KD):
                    s = SLOT_OF[SEQ_WOS + k // 2]
                    t = mm(o, ringN[:, s, k % 2, n * P:(n + 1) * P], yT[:, :, k, :], start=(k == 0), stop=(k == KD - 1))
                t.then_inc(s_pe_ys, 1)
            pe.wait_ge(s_mix_ready, KD)
            for s in range(4):
                arrived(pe, SEQ_WO + s)
            for i in range(NT):
                for b in range(2):
                    o = opened(("mix", i, b))
                    for k in range(KD):
                        s = SLOT_OF[SEQ_WO + k // 2]
                        t = mm(o, mixT[:, k, i * P:(i + 1) * P], ringN[:, s, k % 2, b * 512:(b + 1) * 512],
                               start=(k == 0), stop=(k == KD - 1))
                    t.then_inc(s_pe_mix, 1)
            pe.wait_ge(s_p_in, 16)
            for kk in range(2):
                o = opened(("pT", kk))
                for i in range(NT):
                    t = tr(o[:, i * P:(i + 1) * P], p_in[:, i, kk * P:(kk + 1) * P], ident)
                t.then_inc(s_pe_pT, 1)
            def route(o, i):
                pe.wait_ge(s_h1T_read, i + 1)
                for k in range(KD):
                    t = mm(o[:, 36 * i:36 * i + 36], hT[:, k, i * P:(i + 1) * P], w_rt[:, k, :], start=(k == 0),
                           stop=(k == KD - 1))
                return t

            for i in range(NT):
                pe.wait_ge(s_h1_ready, i + 1)
                o = opened(("h1T", i), D, 2)
                for k in range(KD):
                    t = tr(o[:, k * P:(k + 1) * P], h[:, i, k * P:(k + 1) * P], ident)
                t.then_inc(s_pe_h1T, 1)
                if i == 1:
                    logits = opened("rt", NT * 36)
                if i:
                    route(logits, i - 1)
            route(logits, NT - 1).then_inc(s_pe_rt, 1)

            pe.wait_ge(s_wple_in, 16)
            pe.wait_ge(s_pT_read, 2)
            for n in range(4 * NT):
                s, i = divmod(n, NT)
                pe.wait_ge(pgw_in[s % 2], 16 * (s // 2 + 1))
                o = opened(("pl", n))
                for k in range(KD):
                    mm(o[:, 0:PS], hT[:, k, i * P:(i + 1) * P], pgw[s % 2][:, k, :], start=(k == 0), stop=(k == KD - 1))
                for k in range(2):
                    t = mm(o[:, PS:2 * PS], pT[:, k, i * P:(i + 1) * P], wple[:, k, PS * s:PS * (s + 1)],
                           start=(k == 0), stop=(k == 1))
                t.then_inc(s_pe_pl, 1)
                if n == RANKS_AFTER:
                    pe.wait_ge(s_sel_ready, 1)
                    o = opened("rk", 160)
                    for a in range(NT):
                        for j in range(a + 1):
                            mm(o[:, 32 * a:32 * a + 32], upstrict if j == a else ones, rw[0][:, j, :],
                               start=(j == 0), stop=(j == a))
                    for j in range(NT):
                        t = mm(o[:, 128:160], ones, rw[0][:, j, :], start=(j == 0), stop=(j == NT - 1))
                    t.then_inc(s_pe_rk, 1)

            for s, v in plan_last:
                pe.wait_ge(s, v)
            sides = [slice(half * CAP, (half + 1) * CAP) for half in range(2)]

            def rows_t(half, buf, part, loads):
                if not (isinstance(half, int) and half < 2):
                    pe.wait_ge(s_xgT_sb, half - 1)
                pe.wait_ge(xg_in[buf], loads)
                o = psum[:, 2 + 5 * part, :].rearrange("p (k t) -> p k t", k=4)
                for k in range(4):
                    c = (4 * part + k) * P
                    t = tr(o[:, k, :], xg[:, buf, c:c + P], ident)
                t.then_inc(s_xT_mm, 1)

            def gate_up(former, u, buf, halves):
                for half in range(2):
                    expert_slot_in(pe, former, u % 2, half, 0)
                    expert_slot_in(pe, former, u % 2, half, 1)
                pe.wait_ge(s_xgT_sb, halves)
                for k in range(KD):
                    for half in range(2):
                        s = expert_slot(u % 2, half, 0)
                        t = mm(psum[sides[half], u % 2, :], xgT[:, buf, k, sides[half]], ring[:, s:s + 2, k, :],
                               start=(k == 0), stop=(k == KD - 1))
                t.then_inc(s_gu_mm, 1)

            def down(p, former, u):
                for half in range(2):
                    expert_slot_in(pe, former, u % 2, half, 2)
                pe.wait_ge(s_aT_sb, p + 1)
                if not (isinstance(p, int) and p == 0):
                    pe.wait_ge(s_y_act, p)
                    pe.wait_ge(s_y_dve, p)
                for b in range(2):
                    for k in range(2):
                        for half in range(2):
                            s = expert_slot(u % 2, half, 2)
                            t = mm(psum[sides[half], 4 + b, :], eactT[:, u % 2, k, sides[half]],
                                   ringN[:, s, k, b * 512:(b + 1) * 512], start=(k == 0), stop=(k == 1))
                t.then_inc(s_y_mm, 1)

            def act_t(p, u):
                pe.wait_ge(s_eact_sb, p + 1)
                if not (isinstance(p, int) and p == 0):
                    pe.wait_ge(s_aT_sb, p)
                o = psum[:, 3, 0:256].rearrange("p (k t) -> p k t", k=2)
                for k in range(2):
                    t = tr(o[:, k, :], eact[:, u % 2, k * P:(k + 1) * P], ident)
                t.then_inc(s_aT_mm, 1)

            def step(e4, u):
                p = e4 * 4 + u
                start = isinstance(e4, int) and u == 0
                gate_up(e4 * 2 + u // 2, u, u % 2, p * 2 + 2)
                rows_t(p * 2 + 2, 1 - u % 2, 0, e4 * 32 + 16 * ((u + 1) // 2 + 1))
                if not start:
                    down(p - 1, e4 * 2 + (u - 1) // 2, (u - 1) % 4)
                rows_t(p * 2 + 3, 1 - u % 2, 1, e4 * 32 + 16 * ((u + 1) // 2 + 1))
                act_t(p, u)

            for part in range(2):
                rows_t(part, 0, part, 16)
            for u in range(4):
                step(0, u)
            with pe.Fori(1, PAIRS // 4) as e4:
                for u in range(4):
                    step(e4, u)
            down(PAIRS - 1, PAIRS // 2 - 1, 3)
            pe.wait_ge(s_ctl_ready, 1)
            pairs = pe.value_load(ctl[0:1, EXTRA + 1:EXTRA + 2], min_val=0, max_val=MORE_PAIRS)
            with pe.Fori(0, MORE_PAIRS) as j:
                with pe.If(pairs > j):
                    for part in range(2):
                        rows_t(j * 2 + 2 * PAIRS + 2 + part, 1, part, j * 16 + 16 * (PAIRS // 2 + 2))
                    gate_up(j + PAIRS // 2, 0, 1, j * 2 + 2 * PAIRS + 4)
                    act_t(j + PAIRS, 0)
                    down(j + PAIRS, j + PAIRS // 2, 0)
                pe.nop()

        @block.scalar
        def _(act):
            A = nc.scalar.activation

            def copy(dst, src):
                return nc.scalar.copy(dst, src)

            for i in range(NT):
                for b in range(2):
                    act.wait_ge(s_pe_hT, 2 * i + b + 1)
                    copy(hT[:, 4 * b:4 * b + 4, i * P:(i + 1) * P],
                         bank(("hT", i, b)).rearrange("p (k t) -> p k t", k=4)).then_inc(s_hT_read, 1)
            for n in range(NX):
                act.wait_ge(s_conv_read, n + 1)
                if n >= 2:
                    act.wait_ge(s_silu_done, n - 1)
                A(ctanh[:, n % 2, :], xs[:, n, :], ACT.Tanh).then_inc(s_ctanh_done, 1)
            act.wait_ge(s_dt_exp_in, 1)
            A(dta.rearrange("p i n -> p (i n)"), dta.rearrange("p i n -> p (i n)"), ACT.Exp).then_inc(s_dt_exp, 1)
            A(a_row, a_row, ACT.Exp).then_inc(s_dt_exp, 1)
            act.wait_ge(s_pe_kv, 1)
            act.wait_ge(s_h_ready, NT)
            copy(kT, bank("k")).then_inc(s_kv_read, 1)
            act.wait_ge(s_pe_kv, 2)
            copy(vt, bank("v").rearrange("p (i n) -> p i n", i=NT)).then_inc(s_kv_read, 1)
            act.wait_ge(s_par_read, 1)
            for j in range(4):
                act.wait_ge(s_pe_q, j + 1)
                copy(qT[:, j, :], bank(("q", j))).then_inc(s_q_read, 1)

            def z_tanh(n):
                i, b = divmod(n, 2)
                act.wait_ge(s_pe_z, n + 1)
                if n == 0:
                    act.wait_ge(s_silu_done, NX)
                A(sz[:, i, b * 512:(b + 1) * 512], bank(("z", n)), ACT.Tanh, scale=0.5).then_inc(s_tz_done, 1)

            def softmax_exp(n):
                w = 256 if n >= 2 else P
                act.wait_ge(s_nmax_ready, n + 1)
                a = att[:, n % 2]
                for m in range(4):
                    A(prob[:, m, 0:w], prob[:, m, 0:w], ACT.Exp, bias=a[:, 1, m:m + 1],
                      accum_out=a[:, 3, m:m + 1]).then_inc(s_act_step, 1)
                A(a[:, 2, :], a[:, 2, :], ACT.Exp).then_inc(s_exp_done, 1)

            def probs_out(n):
                act.wait_ge(s_pe_pt, n + 1)
                if n:
                    act.wait_ge(s_pe_av, n)
                w = 2 if n >= 2 else 1
                copy(probT[:, :, 0:w, :], bank(("pt", n), D, 2).rearrange("p (m w t) -> p m w t", m=4, w=2)[:, :, 0:w, :])\
                    .then_inc(s_pt_read, 1)

            def attn_out(n):
                i, hf = divmod(n, 2)
                act.wait_ge(s_pe_av, n + 1)
                if n == 0:
                    act.wait_ge(s_zeroed, 16 * ZERO_DMAS)
                copy(yaT[:, 2 * hf:2 * hf + 2, i * P:(i + 1) * P], bank(("av", n), 256).rearrange("p (j t) -> p j t", j=2))\
                    .then_inc(s_av_read, 1)

            for n in range(8):
                softmax_exp(n)
                z_tanh(n)
                if n:
                    attn_out(n - 1)
                probs_out(n)
            attn_out(7)

            def gate_tanh(g):
                n, b = divmod(g, 2)
                act.wait_ge(s_pe_g, g + 1)
                if g == 0:
                    act.wait_ge(s_pe_z, 8)
                A(gact[:, n, b, :], bank(("g", g)), ACT.Tanh, scale=0.5,
                  bias=b_gate[:, 8 * b + n:8 * b + n + 1]).then_inc(s_g_read, 1)

            for c in range(NT):
                act.wait_ge(s_pe_xt, c + 1)
                if c:
                    act.wait_ge(s_y_ready, c)
                copy(xtok, bank(("xt", c), D, 2)).then_inc(s_xt_read, 1)
                act.wait_ge(s_cb_dve, c + 1)
                if c:
                    act.wait_ge(s_pe_st, c)
                o = bank(("cb", c), D, 2)
                copy(btok, o[:, 0:P]).then_inc(s_act_step, 1)
                A(acs[:, 1:3, :], o[:, 256:288].rearrange("p (a n) -> p a n", a=2), ACT.Exp).then_inc(s_cb_act, 1)
                A(acs[:, 3, :], acs[:, 3, :], ACT.Exp).then_inc(s_acs_exp, 1)
                for q in range(4):
                    act.wait_ge(s_seg_read, 4 * c + q + 1)
                    A(lmat[:, q % 2], lmat[:, q % 2], ACT.Exp).then_inc(s_lmat_exp, 1)
                    if q == 1:
                        gate_tanh(3 * c)
                gate_tanh(3 * c + 1)
                gate_tanh(3 * c + 2)
            for g in range(3 * NT, 2 * KD):
                gate_tanh(g)
            for kk in range(2):
                act.wait_ge(s_pe_pT, kk + 1)
                copy(pT[:, kk, :], bank(("pT", kk))).then_inc(s_pT_read, 1)
            for i in range(NT):
                act.wait_ge(s_pe_h1T, i + 1)
                copy(hT[:, :, i * P:(i + 1) * P], bank(("h1T", i), D, 2).rearrange("p (k t) -> p k t", k=KD))\
                    .then_inc(s_h1T_read, 1)
            act.wait_ge(s_rt_exp_in, 1)
            A(lg[:, :, 0:NG], lg[:, :, 0:NG], ACT.Exp).then_inc(s_act_step, 1)
            A(rv[4], rv[4], ACT.Exp).then_inc(s_rt_exp, 1)
            for i in range(4 * NT):
                act.wait_ge(s_pg_read, i + 1)
                A(pgt[:, i % 4, :], pgt[:, i % 4, :], ACT.Tanh, scale=0.5).then_inc(s_pg_tanh, 1)

            def rows_in(pair, buf, transposed):
                if transposed is not None:
                    act.wait_ge(s_xT_mm, transposed)
                act.dma_start(xg[:, buf, :], xg_dram[bass.ds(pair * 2 * CAP, 2 * CAP)]).then_inc(xg_in[buf], 16)

            def rows_copy(half, buf, part):
                act.wait_ge(s_xT_mm, half + 1)
                copy(xgT[:, buf, 4 * part:4 * part + 4, :], psum[:, 2 + 5 * part, :].rearrange("p (k t) -> p k t", k=4))\
                    .then_inc(s_xgT_sb, 1)

            def hidden_tanh(p, u):
                act.wait_ge(s_gu_mm, p + 1)
                A(eth[:, u % 2, :], psum[:, u % 2, 0:FF], ACT.Tanh, scale=0.5).then_inc(s_tanh_sb, 1)

            def act_copy(p, u):
                act.wait_ge(s_aT_mm, p + 1)
                copy(eactT[:, u % 2], psum[:, 3, 0:256].rearrange("p (k t) -> p k t", k=2)).then_inc(s_aT_sb, 1)

            def out_copy(p, stores, u):
                act.wait_ge(s_y_mm, p + 1)
                if not (isinstance(stores, int) and stores == 0):
                    act.wait_ge(y_st[u % 2], stores)
                copy(eout[:, u % 2, 0:512], psum[:, 4, :]).then_inc(s_y_act, 1)
                act.wait_ge(s_y_act, p + 1)
                act.wait_ge(s_y_dve, p + 1)
                act.dma_start(y_dram[bass.ds(p * 2 * CAP, 2 * CAP)], eout[:, u % 2, :]).then_inc(y_st[u % 2], 16)

            def step(e4, u):
                p = e4 * 4 + u
                hidden_tanh(p, u)
                rows_copy(p * 2 + 2, 1 - u % 2, 0)
                if not (isinstance(e4, int) and u == 0):
                    out_copy(p - 1, e4 * 32 + 16 * ((u - 1) // 2), (u - 1) % 4)
                rows_copy(p * 2 + 3, 1 - u % 2, 1)
                rows_in(p + 3, 1 - u % 2, p * 2 + 4)
                act_copy(p, u)

            act.wait_ge(s_scattered, 16 * 2 * NT)
            act.wait_ge(s_pe_mix, 2 * NT)
            act.wait_ge(s_ah1_ready, NT)
            rows_in(0, 0, None)
            rows_in(1, 1, None)
            rows_copy(0, 0, 0)
            rows_copy(1, 0, 1)
            rows_in(2, 0, 2)
            for u in range(4):
                step(0, u)
            with act.Fori(1, PAIRS // 4) as e4:
                for u in range(4):
                    step(e4, u)
            out_copy(PAIRS - 1, 16 * (PAIRS // 2 - 1), 3)
            pairs = act.value_load(ctl[0:1, EXTRA + 1:EXTRA + 2], min_val=0, max_val=MORE_PAIRS)
            with act.Fori(0, MORE_PAIRS) as j:
                with act.If(pairs > j):
                    p = j + PAIRS
                    act.wait_ge(xg_in[1], j * 16 + 16 * (PAIRS // 2 + 1))
                    rows_in(p, 1, j * 2 + 2 * PAIRS + 2)
                    for part in range(2):
                        rows_copy(j * 2 + 2 * PAIRS + 2 + part, 1, part)
                    hidden_tanh(p, 0)
                    act_copy(p, 0)
                    out_copy(p, j * 16 + 16 * (PAIRS // 2), 0)
                act.nop()
            act.wait_ge(y_st[0], pairs * 16 + 16 * (PAIRS // 2))
            act.wait_ge(y_st[1], 16 * (PAIRS // 2))
            act.wait_ge(xg_in[0], 16 * (PAIRS // 2 + 2))
            act.wait_ge(xg_in[1], 16 * (PAIRS // 2 + 1))
            copy(att[0:1, 0, 5, 0:1], att[0:1, 0, 4, 0:1]).then_inc(s_blocks_stored, 1)
            for i in range(NT):
                act.wait_ge(s_fin_ready, i + 1)
                act.dma_start(out_v[i], sz[:, i, :]).then_inc(s_out_st, 16)
            act.wait_ge(s_out_st, 16 * NT)

        @block.vector
        def _(dve):
            v = nc.vector
            steps, counts = [0], {}

            def link(ins):
                steps[0] += 1
                ins.then_inc(s_dve_step, 1)
                dve.wait_ge(s_dve_step, steps[0])

            def seen(s):
                counts[s.name] = counts.get(s.name, 0) + 1
                return counts[s.name]

            def rsqrt(dst, src, t):
                link(v.tensor_scalar(dst.bitcast(I32), src.bitcast(I32), -0.5, float(0x5F3759DF), ALU.mult, ALU.add))
                for _ in range(3):
                    link(v.tensor_tensor(t, dst, dst, ALU.mult))
                    link(v.scalar_tensor_tensor(t, t, -0.5, src, ALU.mult, ALU.mult))
                    link(v.scalar_tensor_tensor(dst, t, 1.5, dst, ALU.add, ALU.mult))

            def normed(x, w, b, signal):
                for s in range(2):
                    link(v.bn_stats(stats[:, 6 * s:6 * s + 6], x[:, 512 * s:512 * s + 512]))
                link(v.bn_aggr(mv[:, 0:2], stats))
                link(v.tensor_scalar(mv[:, 2:3], mv[:, 1:2], LN_EPS, None, ALU.add))
                rsqrt(mv[:, 3:4], mv[:, 2:3], mv[:, 4:5])
                link(v.scalar_tensor_tensor(x, x, mv[:, 0:1], w, ALU.subtract, ALU.mult))
                v.scalar_tensor_tensor(x, x, mv[:, 3:4], b, ALU.mult, ALU.add).then_inc(signal, 1)
                dve.wait_ge(signal, seen(signal))

            def tile_stats(x, i):
                for s in range(2):
                    link(v.bn_stats(stats[:, 6 * s:6 * s + 6], x[:, 512 * s:512 * s + 512]))
                link(v.bn_aggr(mva[:, i, :], stats))

            def tiles_normed(x, w, b, signal):
                link(v.tensor_scalar(rv[0], mva[:, :, 1], LN_EPS, None, ALU.add))
                rsqrt(rv[1], rv[0], rv[2])
                for i in range(NT):
                    link(v.scalar_tensor_tensor(x[:, i, :], x[:, i, :], mva[:, i, 0:1], w, ALU.subtract, ALU.mult))
                    v.scalar_tensor_tensor(x[:, i, :], x[:, i, :], rv[1][:, i:i + 1], b, ALU.mult, ALU.add)\
                        .then_inc(signal, 1)
                    dve.wait_ge(signal, seen(signal))

            for i in range(NT):
                dve.wait_ge(x_in[i], 16)
                tile_stats(h[:, i, :], i)
            dve.wait_ge(s_ln0_in, 32)
            tiles_normed(h, ln_w, ln_b, s_h_ready)
            dve.wait_ge(s_pe_par, 1)
            v.tensor_copy(par, bank("par")[:, 0:74])\
                .then_inc(s_par_read, 1)
            dve.wait_ge(s_par_read, seen(s_par_read))
            link(v.tensor_scalar(par[:, 0:66], par[:, 0:66], 0.5, None, ALU.mult))
            dve.wait_ge(s_dist_in, 1)
            dist, mask = xs[:, 8, 0:256], xs[:, 9, 0:256]
            link(v.scalar_tensor_tensor(dist, dist, -1.0, dist, ALU.mult, ALU.max))
            for m in range(8):
                head = 2 * (m // 4) + m % 2 + 4 * (m % 4 // 2)
                link(v.scalar_tensor_tensor(bias[:, m, :], dist, -(2.0 ** -(head + 1)), mask, ALU.mult, ALU.add))

            def conv(n):
                dve.wait_ge(s_pe_xbc, n + 1)
                o, a = bank(("xbc", n)), xs[:, n, :]
                link(v.tensor_scalar(a, o, conv_w[:, 3, n:n + 1], conv_b[:, n:n + 1], ALU.mult, ALU.add))
                for w in (2, 1, 0):
                    d = 3 - w
                    ins = v.scalar_tensor_tensor(a[:, d:S], o[:, 0:S - d], conv_w[:, w, n:n + 1], a[:, d:S], ALU.mult,
                                                 ALU.add)
                    if w:
                        link(ins)
                    else:
                        ins.then_inc(s_conv_read, 1)
                        dve.wait_ge(s_conv_read, n + 1)

            def silu(n):
                dve.wait_ge(s_ctanh_done, n + 1)
                v.scalar_tensor_tensor(xs[:, n, :], ctanh[:, n % 2, :], 1.0, xs[:, n, :], ALU.add, ALU.mult)\
                    .then_inc(s_silu_done, 1)
                dve.wait_ge(s_silu_done, seen(s_silu_done))

            for n in range(NX):
                conv(n)
                if n:
                    silu(n - 1)
            silu(NX - 1)

            dve.wait_ge(s_small_in, 16 * 6)
            dve.wait_ge(s_pe_dt, 1)
            flat = lambda t: t.rearrange("p i n -> p (i n)")
            v.tensor_tensor(dtv, bank("dt", 64).rearrange("p (i n) -> p i n", i=NT),
                                 dt_bias.unsqueeze(1).broadcast_to([P, NT, 16]), ALU.add)\
                .then_inc(s_dt_read, 1)
            dve.wait_ge(s_dt_read, seen(s_dt_read))
            fv, fa = flat(dtv), flat(dta)
            v.scalar_tensor_tensor(fa, fv, -1.0, fv, ALU.mult, ALU.min)\
                .then_inc(s_dt_exp_in, 1)
            dve.wait_ge(s_dt_exp_in, seen(s_dt_exp_in))
            dve.wait_ge(s_dt_exp, 2)
            s_, q_, c_ = (at(R_Z + 1024 + 64 * j, 64) for j in range(3))
            link(v.tensor_scalar(s_, fa, 2.0, None, ALU.add))
            link(v.reciprocal(s_, s_))
            link(v.tensor_tensor(s_, s_, fa, ALU.mult))
            link(v.tensor_tensor(q_, s_, s_, ALU.mult))
            link(v.tensor_scalar(c_, q_, 1.0 / 17, None, ALU.mult))
            for k in range(7, 0, -1):
                link(v.scalar_tensor_tensor(c_, c_, 1.0 / (2 * k + 1), q_, ALU.add, ALU.mult))
            link(v.scalar_tensor_tensor(c_, c_, 1.0, s_, ALU.add, ALU.mult))
            link(v.tensor_scalar(fv, fv, 0.0, None, ALU.max))
            link(v.scalar_tensor_tensor(fv, c_, 2.0, fv, ALU.mult, ALU.add))
            v.scalar_tensor_tensor(dta, dtv, -1.0, a_row.unsqueeze(1).broadcast_to([P, NT, 16]), ALU.mult, ALU.mult)\
                .then_inc(s_dta_ready, 1)
            dve.wait_ge(s_dta_ready, seen(s_dta_ready))

            sink_v = sink.rearrange("p (g f j) -> p g f j", g=2, f=2)

            def softmax_in(n):
                i, hf = divmod(n, 2)
                w = 256 if i else P
                a = att[:, n % 2]
                dve.wait_ge(s_pe_sc, n + 1)
                if n:
                    dve.wait_ge(s_pe_pt, n)
                o = bank(("sc", n), D, 2).rearrange("p (m w) -> p m w", m=4)[:, :, 0:w]
                pr = prob[:, :, 0:w]
                v.scalar_tensor_tensor(pr, o, HD ** -0.5, bias[:, 4 * hf:4 * hf + 4, 256 - w:256], ALU.mult, ALU.add)\
                    .then_inc(s_sc_read, 1)
                dve.wait_ge(s_sc_read, seen(s_sc_read))
                link(v.tensor_reduce(a[:, 0, :], pr, AX.X, ALU.max))
                two = lambda r: a[:, r, :].rearrange("p (g j) -> p g j", g=2)
                link(v.tensor_tensor(two(0), two(0), sink_v[:, :, hf, :], ALU.max))
                link(v.tensor_tensor(two(2), sink_v[:, :, hf, :], two(0), ALU.subtract))
                v.tensor_scalar(a[:, 1, :], a[:, 0, :], -1.0, None, ALU.mult)\
                    .then_inc(s_nmax_ready, 1)
                dve.wait_ge(s_nmax_ready, seen(s_nmax_ready))

            def softmax_out(n):
                w = 256 if n >= 2 else P
                a = att[:, n % 2]
                pr = prob[:, :, 0:w]
                dve.wait_ge(s_exp_done, n + 1)
                link(v.tensor_tensor(a[:, 4, :], a[:, 2, :], a[:, 3, :], ALU.add))
                link(v.reciprocal(a[:, 5, :], a[:, 4, :]))
                v.tensor_tensor(pr, pr, a[:, 5, :].unsqueeze(2).broadcast_to([P, 4, w]), ALU.mult)\
                    .then_inc(s_prob_ready, 1)
                dve.wait_ge(s_prob_ready, seen(s_prob_ready))

            def silu_z(n):
                i, b = divmod(n, 2)
                dve.wait_ge(s_tz_done, n + 1)
                zs = sz[:, i, b * 512:(b + 1) * 512]
                v.scalar_tensor_tensor(zs, zs, 1.0, bank(("z", n)), ALU.add, ALU.mult)\
                    .then_inc(s_z_read, 1)
                dve.wait_ge(s_z_read, seen(s_z_read))

            for n in range(8):
                softmax_in(n)
                softmax_out(n)
                silu_z(n)

            heads = lambda t: t.rearrange("p (h e) -> p h e", e=SP)
            per_head = lambda r, n=16: r.unsqueeze(2).broadcast_to([r.shape[0], n, SP])

            def out_t(c):
                dve.wait_ge(s_pe_yT, c + 1)
                v.tensor_tensor(yT[:, c], bank(("yT", c), D, 2).rearrange("p (k t) -> p k t", k=KD),
                                     norm_w.unsqueeze(2).broadcast_to([P, KD, P]), ALU.mult)\
                    .then_inc(s_yT_read, 1)
                dve.wait_ge(s_yT_read, seen(s_yT_read))

            for c in range(NT):
                if c:
                    out_t(c - 1)
                dve.wait_ge(s_pe_cb, c + 1)
                o = bank(("cb", c), D, 2)
                link(v.tensor_copy(acs[:, 0, :], o[:, 256:272]))
                for g in range(2):
                    link(v.tensor_tensor(cbm[:, g, :], o[:, P + 512 * g:2 * P + 512 * g], upper, ALU.mult))
                if c:
                    dve.wait_ge(s_acs_exp, c)
                v.tensor_tensor(acs[:, 3, :], o[:, 272:288], acs[:, 0, :], ALU.subtract)\
                    .then_inc(s_cb_dve, 1)
                dve.wait_ge(s_cb_dve, seen(s_cb_dve))
                dve.wait_ge(s_xt_read, c + 1)
                v.tensor_tensor(heads(xdt), heads(xtok), per_head(dtv[:, c, :]), ALU.mult)\
                    .then_inc(s_xdt_ready, 1)
                dve.wait_ge(s_xdt_ready, seen(s_xdt_ready))

                def seg(q):
                    dve.wait_ge(s_pe_seg, 4 * c + q + 1)
                    if 4 * c + q >= 2:
                        dve.wait_ge(s_pe_yd, 4 * c + q - 1)
                    for m in range(4):
                        ins = v.tensor_scalar(lmat[:, q % 2, m, :], bank(("seg", c, q))[:, m * P:(m + 1) * P],
                                              acs[:, 0, 4 * q + m:4 * q + m + 1], 0.0, ALU.subtract, ALU.min)
                    ins.then_inc(s_seg_read, 1)
                    dve.wait_ge(s_seg_read, 4 * c + q + 1)

                def decayed(q):
                    dve.wait_ge(s_lmat_exp, 4 * c + q + 1)
                    v.tensor_tensor(lmat[:, q % 2], lmat[:, q % 2],
                                         cbm[:, q // 2, :].unsqueeze(1).broadcast_to([P, 4, P]), ALU.mult)\
                        .then_inc(s_m_ready, 1)
                    dve.wait_ge(s_m_ready, seen(s_m_ready))

                seg(0)
                seg(1)
                decayed(0)
                dve.wait_ge(s_acs_exp, c + 1)
                if c:
                    dve.wait_ge(s_pe_st, c)
                v.tensor_tensor(heads(xdec), heads(xdt), per_head(acs[:, 3, :]), ALU.mult)\
                    .then_inc(s_xdec_ready, 1)
                dve.wait_ge(s_xdec_ready, seen(s_xdec_ready))
                decayed(1)
                seg(2)
                seg(3)
                decayed(2)
                decayed(3)
                if c:
                    dve.wait_ge(s_pe_yT, c)
                    dve.wait_ge(s_pe_yo, c)
                    v.tensor_tensor(heads(y), heads(bank(("yo", c), D, 2)), per_head(acs[:, 1, :]), ALU.mult)\
                        .then_inc(s_yo_read, 1)
                    dve.wait_ge(s_yo_read, seen(s_yo_read))
                    link(v.tensor_tensor(heads(tmp), heads(xtok), per_head(dskip), ALU.mult))
                    link(v.tensor_tensor(y, y, tmp, ALU.add))
                else:
                    link(v.tensor_tensor(heads(y), heads(xtok), per_head(dskip), ALU.mult))
                dve.wait_ge(s_pe_yd, 4 * c + 4)
                v.tensor_tensor(y, bank(("yd", c), D, 2), y, ALU.add)\
                    .then_inc(s_yd_read, 1)
                dve.wait_ge(s_yd_read, seen(s_yd_read))
                if c < NT - 1:
                    dve.wait_ge(s_pe_st, c + 1)
                    if c:
                        for g in range(2):
                            gs = slice(64 * g, 64 * g + 64)
                            link(v.tensor_tensor(heads(state[gs]), heads(state[gs]),
                                                 per_head(acs[gs, 2, 8 * g:8 * g + 8], 8), ALU.mult))
                        v.tensor_tensor(state, bank(("st", c)), state, ALU.add)\
                            .then_inc(s_st_read, 1)
                        dve.wait_ge(s_st_read, seen(s_st_read))
                    else:
                        v.tensor_copy(state, bank(("st", c)))\
                            .then_inc(s_st_read, 1)
                        dve.wait_ge(s_st_read, seen(s_st_read))
                link(v.scalar_tensor_tensor(y, y, 0.5, sz[:, c, :], ALU.mult, ALU.mult))
                for g in range(2):
                    yg = y[:, 512 * g:512 * g + 512]
                    link(v.tensor_tensor_reduce(out=tmp[:, 0:512], in0=yg, in1=yg, scale=1.0 / 512, scalar=0.0,
                                                op0=ALU.mult, op1=ALU.add, accum_out=mv[:, g:g + 1]))
                link(v.tensor_scalar(mv[:, 2:4], mv[:, 0:2], RMS_EPS, None, ALU.add))
                rsqrt(mv[:, 4:6], mv[:, 2:4], mv[:, 6:8])
                v.tensor_tensor(y.rearrange("p (g n) -> p g n", g=2), y.rearrange("p (g n) -> p g n", g=2),
                                     mv[:, 4:6].unsqueeze(2).broadcast_to([P, 2, 512]), ALU.mult)\
                    .then_inc(s_y_ready, 1)
                dve.wait_ge(s_y_ready, seen(s_y_ready))
            out_t(NT - 1)

            for n in range(KD):
                dve.wait_ge(s_g_read, 2 * n + 2)
                if n == 0:
                    dve.wait_ge(s_pe_yT, NT)
                dve.wait_ge(s_pe_ya, n + 1)
                v.scalar_tensor_tensor(mixT[:, n, :], gact[:, n, 0, :], 1.0, bank(("ya", n)), ALU.add, ALU.mult)\
                    .then_inc(s_ya_read, 1)
                dve.wait_ge(s_ya_read, seen(s_ya_read))
                dve.wait_ge(s_pe_ys, n + 1)
                v.scalar_tensor_tensor(gtmp[:, n % 2, :], gact[:, n, 1, :], 1.0, bank(("ys", n)), ALU.add,
                                            ALU.mult)\
                    .then_inc(s_ys_read, 1)
                dve.wait_ge(s_ys_read, seen(s_ys_read))
                v.tensor_tensor(mixT[:, n, :], mixT[:, n, :], gtmp[:, n % 2, :], ALU.add)\
                    .then_inc(s_mix_ready, 1)
                dve.wait_ge(s_mix_ready, seen(s_mix_ready))
            dve.wait_ge(s_ah_ready, NT)
            dve.wait_ge(s_ln1_in, 32)
            for i in range(NT):
                for b in range(2):
                    dve.wait_ge(s_pe_mix, 2 * i + b + 1)
                    hb = h[:, i, 512 * b:512 * b + 512]
                    v.scalar_tensor_tensor(hb, bank(("mix", i, b)), 0.5, hb, ALU.mult, ALU.add)\
                        .then_inc(s_mix_read, 1)
                    dve.wait_ge(s_mix_read, seen(s_mix_read))
                normed(h[:, i, :], A1w, A1b, s_h1_ready)

            dve.wait_ge(s_pe_rt, 1)
            v.tensor_tensor(lg, bank("rt", NT * 36).rearrange("p (i n) -> p i n", i=NT),
                                 rbias.unsqueeze(1).broadcast_to([P, NT, 36]), ALU.add)\
                .then_inc(s_rt_read, 1)
            dve.wait_ge(s_rt_read, seen(s_rt_read))
            sel, oh1, oh2, em, t4, t5 = rw
            gl = lg[:, :, 0:NG]
            along = lambda r, n: r.unsqueeze(2).broadcast_to([P, NT, n])
            iotas = lambda n: iota_e[:, 0:n].unsqueeze(1).broadcast_to([P, NT, n])

            def first_max(vals, n, top, index, onehot):
                link(v.tensor_reduce(top, vals, AX.X, ALU.max))
                link(v.tensor_tensor(t5[:, :, 0:n], vals, along(top, n), ALU.is_equal))
                link(v.scalar_tensor_tensor(t5[:, :, 0:n], t5[:, :, 0:n], -64.0, iotas(n), ALU.mult, ALU.add))
                link(v.tensor_reduce(index, t5[:, :, 0:n], AX.X, ALU.min))
                link(v.tensor_scalar(index, index, 64.0, None, ALU.add))
                link(v.tensor_tensor(onehot, iotas(n), along(index, n), ALU.is_equal))

            dve.wait_ge(s_consts, 4)
            first_max(gl, NG, rv[0], rv[1], t4[:, :, 0:NG])
            link(v.tensor_tensor(gl, gl, along(rv[0], NG), ALU.subtract))
            in_g = lambda t: t.rearrange("p i (g e) -> p i g e", g=NG)
            ohg = t4[:, :, 0:NG].unsqueeze(3).broadcast_to([P, NT, NG, NPG])
            link(v.tensor_tensor(in_g(em), in_g(lg[:, :, NG:36]), ohg, ALU.mult))
            link(v.tensor_scalar(t4[:, :, 0:NG], t4[:, :, 0:NG], -1.0, -NEG, ALU.add, ALU.mult))
            link(v.tensor_tensor(in_g(em), in_g(em), ohg, ALU.add))
            first_max(em, NE, rv[3], rv[5], oh1)
            link(v.scalar_tensor_tensor(em, oh1, -3e38, em, ALU.mult, ALU.add))
            first_max(em, NE, rv[4], rv[6], oh2)
            v.tensor_tensor(rv[4], rv[4], rv[3], ALU.subtract)\
                .then_inc(s_rt_exp_in, 1)
            dve.wait_ge(s_rt_exp_in, seen(s_rt_exp_in))
            v.tensor_tensor(sel, oh1, oh2, ALU.add)\
                .then_inc(s_sel_ready, 1)
            dve.wait_ge(s_sel_ready, seen(s_sel_ready))
            dve.wait_ge(s_rt_exp, 1)
            link(v.tensor_reduce(rv[2], gl, AX.X, ALU.add))
            link(v.scalar_tensor_tensor(rv[7], rv[4], 1.0, rv[2], ALU.add, ALU.mult))
            link(v.reciprocal(rv[7], rv[7]))
            link(v.tensor_scalar(rv[8], rv[7], 0.5, None, ALU.mult))
            link(v.tensor_tensor(rv[9], rv[8], rv[4], ALU.mult))

            def ple_sum(n):
                s = n // NT
                dve.wait_ge(s_pe_pl, n + 1)
                v.tensor_tensor(pgt[:, n % 4, :], bank(("pl", n))[:, 0:PS], bple[:, PS * s:PS * (s + 1)], ALU.add)\
                    .then_inc(s_pg_read, 1)
                dve.wait_ge(s_pg_read, seen(s_pg_read))

            def ple_out(n):
                s, i = divmod(n, NT)
                dve.wait_ge(s_pg_tanh, n + 1)
                v.scalar_tensor_tensor(pgt[:, n % 4, :], pgt[:, n % 4, :], 1.0, bank(("pl", n))[:, PS:2 * PS], ALU.add,
                                       ALU.mult).then_inc(s_pp_read, 1)
                dve.wait_ge(s_pp_read, seen(s_pp_read))
                dve.wait_ge(s_ah1_ready, i + 1)
                hs = slice(PS * s, PS * (s + 1))
                v.scalar_tensor_tensor(sz[:, i, hs], pgt[:, n % 4, :], 0.5, sz[:, i, hs], ALU.mult, ALU.add)\
                    .then_inc(s_base_ready, 1)
                dve.wait_ge(s_base_ready, seen(s_base_ready))

            dve.wait_ge(s_bple_in, 16)
            for n in range(RANKS_AFTER + 1):
                ple_sum(n)

            dve.wait_ge(s_pe_rk, 1)
            rk = bank("rk", 160)
            rank, count = t4, cnt[0]
            link(v.tensor_copy(rank, rk[:, 0:128].rearrange("p (i n) -> p i n", i=NT)))
            v.tensor_copy(count, rk[:, 128:160])\
                .then_inc(s_rk_read, 1)
            dve.wait_ge(s_rk_read, seen(s_rk_read))
            more, csum = cnt[1], [cnt[2], cnt[3]]
            link(v.tensor_scalar(more, count, float(CAP), None, ALU.is_gt))
            for b in range(2, S // CAP):
                link(v.scalar_tensor_tensor(more, count, float(CAP * b), more, ALU.is_gt, ALU.add))
            link(v.tensor_copy(csum[0], more))
            a = 0
            for d in (1, 2, 4, 8, 16):
                link(v.tensor_copy(csum[1 - a][:, 0:d], csum[a][:, 0:d]))
                link(v.tensor_tensor(csum[1 - a][:, d:NE], csum[a][:, d:NE], csum[a][:, 0:NE - d], ALU.add))
                a = 1 - a
            csum = csum[a]
            first_row, jump = cnt[4], cnt[5]
            link(v.tensor_scalar(first_row, iota_e, float(CAP), None, ALU.mult))
            link(v.tensor_tensor(jump, csum, more, ALU.subtract))
            link(v.tensor_scalar(jump, jump, float(NE - 1), float(CAP), ALU.add, ALU.mult))
            link(v.tensor_tensor(jump, jump, first_row, ALU.subtract))
            per_e = lambda r: r.unsqueeze(1).broadcast_to([P, NT, NE])
            link(v.tensor_scalar(t5, rank, float(CAP), None, ALU.is_ge))
            link(v.tensor_tensor(t5, t5, per_e(jump), ALU.mult))
            link(v.tensor_tensor(rank, rank, t5, ALU.add))
            link(v.tensor_tensor(rank, rank, per_e(first_row), ALU.add))
            rows2 = rowsU[:, :].rearrange("p (i c) -> p i c", c=2)
            for c, oh in ((0, oh1), (1, oh2)):
                link(v.tensor_tensor(t5, rank, oh, ALU.mult))
                link(v.tensor_reduce(rv[10], t5, AX.X, ALU.add))
                v.tensor_copy(rows2[:, :, c], rv[10]).then_inc(s_rows_ready, 1)
                dve.wait_ge(s_rows_ready, seen(s_rows_ready))
            for j in range(EXTRA + 1):
                link(v.tensor_scalar(em[:, 0, :], csum, float(j), 0.0, ALU.is_le, ALU.add, accum_out=ctlf[:, j:j + 1]))
            link(v.tensor_scalar(ctlf[:, 0:EXTRA + 1], ctlf[:, 0:EXTRA + 1], float(NE - 1), None, ALU.min))
            pair_of = em[:, 0, 0:MORE_PAIRS]
            link(v.tensor_scalar(pair_of, iota_e[:, 0:MORE_PAIRS], 2.0, csum[:, NE - 1:NE], ALU.mult, ALU.subtract))
            link(v.tensor_scalar(pair_of, pair_of, 0.0, 0.0, ALU.is_lt, ALU.add, accum_out=ctlf[:, EXTRA + 1:EXTRA + 2]))
            v.tensor_copy(ctl[:, :], ctlf)\
                .then_inc(s_ctl_ready, 1)
            dve.wait_ge(s_ctl_ready, seen(s_ctl_ready))

            for n in range(4 * NT):
                if RANKS_AFTER < n:
                    ple_sum(n)
                if n >= RANKS_AFTER:
                    ple_out(n - RANKS_AFTER)
            for n in range(4 * NT - RANKS_AFTER, 4 * NT):
                ple_out(n)

            def hidden(p, u):
                dve.wait_ge(s_tanh_sb, p + 1)
                hg, hu = psum[:, u % 2, 0:FF], psum[:, u % 2, FF:2 * FF]
                v.scalar_tensor_tensor(eact[:, u % 2, :], eth[:, u % 2, :], 1.0, hg, ALU.add, ALU.mult)\
                    .then_inc(s_eact_a, 1)
                dve.wait_ge(s_eact_a, p + 1)
                v.tensor_tensor(eact[:, u % 2, :], eact[:, u % 2, :], hu, ALU.mult).then_inc(s_eact_sb, 1)

            def out_half(p, stores, u):
                dve.wait_ge(s_y_mm, p + 1)
                if not (isinstance(stores, int) and stores == 0):
                    dve.wait_ge(y_st[u % 2], stores)
                v.tensor_copy(eout[:, u % 2, 512:1024], psum[:, 5, :]).then_inc(s_y_dve, 1)

            def step(e4, u):
                p = e4 * 4 + u
                hidden(p, u)
                if not (isinstance(e4, int) and u == 0):
                    out_half(p - 1, e4 * 32 + 16 * ((u - 1) // 2), (u - 1) % 4)

            for u in range(4):
                step(0, u)
            with dve.Fori(1, PAIRS // 4) as e4:
                for u in range(4):
                    step(e4, u)
            out_half(PAIRS - 1, 16 * (PAIRS // 2 - 1), 3)
            pairs = dve.value_load(ctl[0:1, EXTRA + 1:EXTRA + 2], min_val=0, max_val=MORE_PAIRS)
            with dve.Fori(0, MORE_PAIRS) as j:
                with dve.If(pairs > j):
                    hidden(j + PAIRS, 0)
                    out_half(j + PAIRS, j * 16 + 16 * (PAIRS // 2), 0)
                dve.nop()

            for i in range(NT):
                dve.wait_ge(y_gath[i], 32)
                x = sz[:, i, :]
                for c in range(2):
                    v.scalar_tensor_tensor(x, ygat[:, i, c, :], rv[8 + c][:, i:i + 1], x, ALU.mult, ALU.add)\
                        .then_inc(s_combined, 1)
                    dve.wait_ge(s_combined, 2 * i + c + 1)
                tile_stats(x, i)
            dve.wait_ge(s_ln2_in, 32)
            tiles_normed(sz, A1w, A1b, s_fin_ready)


_INS = ["x", "p", "ln0_w", "ln0_b", "w_in", "b_gate", "conv_w", "conv_b", "dt_bias", "a_log", "d_skip", "ssd_norm_w",
        "sinks", "w_out_attn", "w_out_ssd", "w_out", "ln1_w", "ln1_b", "w_router_group", "b_router_group",
        "w_router_expert", "b_router_expert", "w_exp_gate", "w_exp_up", "w_exp_down", "w_ple", "w_ple_gate",
        "b_ple_gate", "ln2_w", "ln2_b"]


def kernel(**inputs):
    import numpy as _np
    import concourse.bacc as _bacc
    from concourse import mybir as _mybir
    from concourse.bass_utils import run_bass_kernel_spmd as _run

    nc = _bacc.Bacc("TRN2", target_bir_lowering=False, num_devices=1)
    arrays, aps = {}, {}
    for name in _INS:
        a = _np.ascontiguousarray(inputs[name])
        arrays[f"in_{name}_dram"] = a
        aps[name] = nc.dram_tensor(f"in_{name}_dram", a.shape, _mybir.dt.from_np(a.dtype), kind="ExternalInput").ap()
    out = nc.dram_tensor("out_0_dram", (1, S, D), F32, kind="ExternalOutput").ap()
    block_kernel(nc, aps, out)
    r = _run(nc, [arrays], core_ids=[0])
    return r.results[0]["out_0_dram"]
```

```python
from contextlib import ExitStack

import concourse.bass as bass
from concourse import mybir

ALU = mybir.AluOpType
ACT = mybir.ActivationFunctionType
F32 = mybir.dt.float32
F32R = mybir.dt.float32r
I32 = mybir.dt.int32
U32 = mybir.dt.uint32
AX = mybir.AxisListType

P = 128
D = 1024
S = 512
NT = S // P
KD = D // P
HEADS, HD = 8, 64
SSDH, SP, SN = 16, 64, 64
CONV_W = 4
XBC = 1280
NX = XBC // P
COL_KV, COL_Z, COL_XBC, COL_DT, COL_GATE = 512, 768, 1792, 3072, 3088
NG, NPG, NE, FF = 4, 8, 32, 256
PLE = 256
ALPHA = 2.0 ** 0.25
LN_EPS = 1e-5
RMS_EPS = 1e-5
NEG = -1e30

SLOTS, SLOT = 12, 2048
CAP = 64
EXTRA = 2 * S // CAP - 1
PAIRS = NE // 2
MORE_PAIRS = (EXTRA + 1) // 2
ROWS = (PAIRS + MORE_PAIRS) * 2 * CAP
ZERO_DMAS = (ROWS - NE * CAP) // P // 2
PS = 256


def stream_order(aps):
    w_in = aps["w_in"][0].rearrange("(k p) n -> p k n", p=P)

    def cols(c):
        return [(w_in[:, :, c:c + 256], slice(0, P), "kn", slice(0, 256))]

    out = [cols(COL_XBC + 256 * s) for s in range(5)]
    out += [cols(COL_KV)]
    for s in range(2):
        out.append([(w_in[:, :, 256 * g + 64 * (2 * s + j):][:, :, 0:64], slice(0, P), "kn",
                     slice(128 * j + 64 * g, 128 * j + 64 * g + 64)) for j in range(2) for g in range(2)])
    out += [cols(COL_Z + 256 * s) for s in range(4)]

    def gates(s):
        return [cols(COL_GATE + 256 * s), cols(COL_GATE + D + 256 * s)]

    for s in range(4):
        out += gates(s)
    woa = aps["w_out_attn"][0].rearrange("(g s j d) n -> g s d j n", g=2, s=2, j=2)
    for s in range(2):
        out.append([(woa[g, s], slice(64 * g, 64 * g + 64), "kN", slice(0, D)) for g in range(2)])

    def rows(w, s):
        return [(w[256 * s:256 * s + 256, :].rearrange("(k p) n -> p k n", p=P), slice(0, P), "kN",
                 slice(0, D))]

    out += [rows(aps["w_out_ssd"][0], s) for s in range(4)]
    out += [rows(aps["w_out"][0], s) for s in range(4)]
    assert len(out) == len(SLOT_OF)
    return out


SEQ_XBC, SEQ_KV, SEQ_Q, SEQ_Z, SEQ_WOA, SEQ_WOS, SEQ_WO = (0, 5, 6, 8, 20, 22, 26)
SEQ_GATE = (12, 14, 16, 18)
PROJ = 20
HI_OF = [(4, 5, 8, 9, 10, 11)[seq % 6] if seq < 12 else 4 + seq % 2 for seq in range(PROJ)]
H_SLOT = 6
SLOT_OF = [seq % 4 for seq in range(PROJ)] + [*range(10)]
GATE_SLOT = 8


def uses():
    out = [("pe_xbc", 2 * s + 2) for s in range(5)] + [("pe_kv", 2)] + [("pe_q", 2), ("pe_q", 4)]
    return out + [("pe_z", 2 * s + 2) for s in range(4)] + [("pe_g", 2 * s + 2) for s in range(8)]


USED = uses()
FREED = USED[:PROJ - 4] + [USED[q] for q in (16, 17, 18, 19, 18, 19, 19, 19)] + [("ys_read", 2), ("ys_read", 4)]
MOE_FREED = ([("pe_ya", KD)] * 2 + [("pe_ys", KD)] * 4 + [("pe_mix", 2 * NT)] * 4 + [("ys_read", KD)] * 2)
RING = SLOTS * SLOT
ARENA = 28600
H_PARTS = 4096 + 2 * KD * 16
RANKS_AFTER = 2


def gate_of(g):
    return g // 4 * 2 + g % 2, g % 4 // 2


def psum_plan(sems):
    units = []

    def unit(key, banks, *free):
        units.append((key, banks, [(sems[n], v) for n, v in free]))

    for i in range(NT):
        for b in range(2):
            unit(("hT", i, b), 1, ("hT_read", 2 * i + b + 1))
    unit("par", 1, ("par_read", 1))
    for n in range(NX):
        unit(("xbc", n), 1, ("conv_read", n + 1))
    unit("dtT", 1, ("dtT_read", 1))
    unit("k", 1, ("kv_read", 1))
    unit("vT", 1, ("kv_read", 2))
    for j in range(4):
        if j == 2:
            unit("dt", 1, ("dt_read", 1))
        unit(("q", j), 1, ("q_read", j + 1))
    unit("v", 1, ("kv_read", 3))

    def z(n):
        unit(("z", n), 1, ("z_read", n + 1))

    def sc(n):
        unit(("sc", n), 2, ("sc_read", n + 1))

    sc(0)
    for n in range(8):
        z(n)
        if n < 7:
            sc(n + 1)
        if n:
            unit(("av", n - 1), 1, ("av_read", n))
        unit(("pt", n), 2, ("pt_read", n + 1))
    unit(("av", 7), 1, ("av_read", 8))
    gates = iter(range(2 * KD))

    def gate():
        g = next(gates)
        unit(("g", g), 1, ("g_read", g + 1))

    def chunk_in(c):
        unit(("xt", c), 2, ("xt_read", c + 1))
        unit(("cb", c), 2, ("cb_act", c + 1), ("cb_dve", c + 1))

    chunk_in(0)
    for c in range(NT):
        for q in range(4):
            unit(("seg", c, q), 1, ("seg_read", 4 * c + q + 1))
        gate()
        if c:
            unit(("yo", c), 2, ("yo_read", c))
        unit(("yd", c), 2, ("yd_read", c + 1))
        gate()
        if c < NT - 1:
            unit(("st", c), 1, ("st_read", c + 1))
        gate()
        gate()
        if c < NT - 1:
            chunk_in(c + 1)
        unit(("yT", c), 2, ("yT_read", c + 1))
    for n in range(KD):
        unit(("ya", n), 1, ("ya_read", n + 1))
    for n in range(KD):
        unit(("ys", n), 1, ("ys_read", n + 1))
    for i in range(NT):
        for b in range(2):
            unit(("mix", i, b), 1, ("mix_read", 2 * i + b + 1))
    for kk in range(2):
        unit(("pT", kk), 1, ("pT_read", kk + 1))
    for i in range(NT):
        unit(("h1T", i), 2, ("h1T_read", i + 1))
        if i == 1:
            unit("rt", 1, ("rt_read", 1))
    for n in range(4 * NT):
        unit(("pl", n), 1, ("pp_read", n + 1))
        if n == RANKS_AFTER:
            unit("rk", 1, ("rk_read", 1))
    place, holder, at = {}, [[] for _ in range(8)], 0
    for key, banks, free in units:
        if banks == 2:
            at += at % 2
        at %= 8
        need = {}
        for b in range(at, at + banks):
            for s, v in holder[b]:
                need[s.name] = (s, max(v, need.get(s.name, (s, 0))[1]))
            holder[b] = free
        place[key] = (at, list(need.values()))
        at += banks
    last = {}
    for b in range(8):
        for s, v in holder[b]:
            last[s.name] = (s, max(v, last.get(s.name, (s, 0))[1]))
    return place, list(last.values())


def block_kernel(nc, aps, out):
    with ExitStack() as ctx:
        def sem(name):
            return ctx.enter_context(nc.semaphore(name))

        with nc.sbuf_tensor("ring_r", [P, RING], F32R) as ring_r, nc.sbuf_tensor("arena_r", [P, H_PARTS], F32R) as arena_r:
            pass
        ring_words = ctx.enter_context(nc.sbuf_tensor("ring", [P, RING], F32))
        arena = ctx.enter_context(nc.sbuf_tensor("arena", [P, ARENA], F32))
        place = [0]

        def region(n):
            a = place[0]
            place[0] += n
            return a

        def at(base, n, parts=(0, P)):
            if base < RING:
                return ring_words[parts[0]:parts[0] + parts[1], base:base + n]
            return arena[parts[0]:parts[0] + parts[1], base - RING:base - RING + n]

        def shaped(base, pattern, rounded=False, **k):
            n = 1
            for v in k.values():
                n *= v
            if rounded:
                words = ring_r[:, base:base + n] if base < RING else arena_r[:, base - RING:base - RING + n]
            else:
                words = at(base, n)
            return words.rearrange(pattern, **k)

        R_RING = region(SLOTS * SLOT)
        R_T = region(4096)
        R_DT = region(2 * KD * 16)
        R_H, R_Z = region(4096), region(4096)
        R_X = region(5120)
        R_Y = region(2048)
        R_A = region(7168)
        ring = shaped(R_RING, "p (s k n) -> p s k n", s=SLOTS, k=KD, n=256)
        ringN = shaped(R_RING, "p (s k n) -> p s k n", s=SLOTS, k=2, n=D)
        h = shaped(R_H, "p (i n) -> p i n", i=NT, n=D)
        hT = shaped(R_T, "p (k t) -> p k t", k=KD, t=S)
        hT_hi = shaped(R_RING + H_SLOT * SLOT, "p (k t) -> p k t", True, k=KD, t=S)
        hT_lo = shaped(R_T, "p (k t) -> p k t", True, k=KD, t=S)
        ring_parts = shaped(R_RING, "p (s k n) -> p s k n", True, s=SLOTS, k=KD, n=256)
        sz = shaped(R_Z, "p (i n) -> p i n", i=NT, n=D)
        yT = shaped(R_Z, "p (i k t) -> p i k t", i=NT, k=KD, t=P)
        xs = shaped(R_X, "p (n t) -> p n t", n=NX, t=S)
        mixT = shaped(R_X, "p (n t) -> p n t", n=KD, t=S)
        yaT = shaped(R_Y, "p (j t) -> p j t", j=4, t=S)
        qT = shaped(R_A, "p (j t) -> p j t", j=4, t=S)
        kT = at(R_A + 2048, S)
        vt = shaped(R_A + 2560, "p (i n) -> p i n", i=NT, n=P)
        vT = at(R_A + 6144, S)
        dtT = at(R_A + 6656, S, (0, 16))
        bias = shaped(R_A + 3072, "p (m w) -> p m w", m=8, w=256)
        prob = shaped(R_A + 5120, "p (m w) -> p m w", m=4, w=256)
        probT = shaped(R_A + 6144, "p (m w t) -> p m w t", m=4, w=2, t=P)
        ln_w, ln_b = at(R_A + 5120, D), at(R_A + 6144, D)
        ctanh = shaped(R_Z, "p (b t) -> p b t", b=2, t=S)
        xtok = at(R_A, D)
        xdt = at(R_A + 1024, D)
        xdec = at(R_A + 2048, D)
        y = at(R_A + 3072, D)
        lmat = shaped(R_A + 4096, "p (b m t) -> p b m t", b=2, m=4, t=P)
        state = at(R_A + 5120, 512)
        btok = at(R_A + 5632, P)
        cbm = shaped(R_A + 5760, "p (g t) -> p g t", g=2, t=P)
        tmp = at(R_A + 6016, D)
        A1w, A1b = at(R_A, D), at(R_A + 1024, D)
        bple = at(R_A + 2048, D)
        gact = shaped(R_RING + GATE_SLOT * SLOT, "p (n g t) -> p n g t", n=KD, g=2, t=S)
        gtmp = shaped(R_A + 5120, "p (b t) -> p b t", b=2, t=S)
        p_in = shaped(R_A + 6144, "p (i n) -> p i n", i=NT, n=PLE)
        pT = shaped(R_X + 4096, "p (k t) -> p k t", k=2, t=S)
        pgw = [shaped(r, "p (k n) -> p k n", k=KD, n=PS) for r in (R_A + 3072, R_Y)]
        wple = shaped(R_X + 2048, "p (k n) -> p k n", k=2, n=D)
        pgt = shaped(R_A + 6144, "p (b t) -> p b t", b=4, t=PS)
        onehot = shaped(R_X, "p (b i r) -> p b i r", b=2, i=NT, r=P)
        eact = shaped(R_X + 1024, "p (b n) -> p b n", b=2, n=FF)
        eth = shaped(R_X + 1024 + 2 * FF, "p (b n) -> p b n", b=2, n=FF)
        xgT = shaped(R_X + 2048, "p (b k t) -> p b k t", b=2, k=KD, t=P)
        eactT = shaped(R_A + 6144, "p (b k t) -> p b k t", b=2, k=2, t=P)
        eout = shaped(R_Y, "p (b n) -> p b n", b=2, n=D)
        ygat = shaped(R_RING, "p (i c n) -> p i c n", i=NT, c=2, n=D)
        ident, upper, ones, upstrict = (at(region(P), P) for _ in range(4))
        par_rows = at(R_A, P, (0, 74))
        par = at(region(74), 74)
        conv_w = par[:, 0:40].rearrange("p (w n) -> p w n", w=CONV_W)
        conv_b, b_gate, norm_w = par[:, 40:50], par[:, 50:66], par[:, 66:74]
        w_dt = shaped(R_DT, "p (k n) -> p k n", k=KD, n=16)
        w_dt_lo, w_dt_hi = (shaped(R_DT + j * KD * 16, "p (k n) -> p k n", True, k=KD, n=16) for j in range(2))
        w_rt = shaped(region(KD * 36), "p (k n) -> p k n", k=KD, n=36)
        brow = region(16 * 3 + 8 + 36)
        dt_bias, a_row, dskip = (at(brow + 16 * j, 16) for j in range(3))
        sink = at(brow + 48, 8)
        rbias = at(brow + 56, 36)
        stats = at(region(12), 12)
        mv = at(region(8), 8)
        dtv = shaped(region(64), "p (i n) -> p i n", i=NT, n=16)
        dta = shaped(region(64), "p (i n) -> p i n", i=NT, n=16)
        R_SM = region(192)
        acs = shaped(R_SM, "p (a n) -> p a n", a=8, n=16)
        att = shaped(R_SM + 128, "p (b a n) -> p b a n", b=2, a=6, n=4)
        lg = shaped(region(NT * 36), "p (i n) -> p i n", i=NT, n=36)
        rw = [shaped(R_A + 5120 + NT * NE * j, "p (i n) -> p i n", i=NT, n=NE) for j in range(6)]
        rv = [at(region(NT), NT) for _ in range(12)]
        iota_e = at(region(NE), NE)
        cnt = [at(R_A + 5888 + NE * j, NE) for j in range(6)]
        ctlf = at(region(EXTRA + 2), EXTRA + 2)
        second = shaped(R_A + 5120, "p (i r) -> p i r", i=NT, r=P)
        iota_r = at(region(P), P)
        rowf = shaped(region(2 * NT), "p (i c) -> p i c", i=NT, c=2)
        mva = shaped(region(2 * NT), "p (i n) -> p i n", i=NT, n=2)
        sums = shaped(region(4 * NT), "p (i n) -> p i n", i=NT, n=4)
        rowsU = ctx.enter_context(nc.sbuf_tensor("rowsU", [P, 2 * NT], U32))
        ctl = ctx.enter_context(nc.sbuf_tensor("ctl", [P, EXTRA + 2], I32))
        psum = ctx.enter_context(nc.psum_tensor("psum", [P, 8, 512], F32))

        y_dram = nc.dram_tensor("y_rows", [ROWS, D], F32).ap()

        slot_in = [sem(f"slot_in{s}") for s in range(SLOTS)]
        s_aT_mm = sem("aT_mm")
        s_aT_sb = sem("aT_sb")
        s_acs_exp = sem("acs_exp")
        s_act_stats = sem("act_stats")
        s_act_sums = sem("act_sums")
        s_ah_ready = sem("ah_ready")
        s_av_read = sem("av_read")
        s_ah1_ready = sem("ah1_ready")
        s_base_ready = sem("base_ready")
        s_blocks_stored = sem("blocks_stored")
        s_bple_in = sem("bple_in")
        s_cb_act = sem("cb_act")
        s_cb_dve = sem("cb_dve")
        s_combined = sem("combined")
        s_consts = sem("consts")
        s_conv_read = sem("conv_read")
        s_ctl_ready = sem("ctl_ready")
        s_ctanh_done = sem("ctanh_done")
        s_dist_in = sem("dist_in")
        s_dt_exp = sem("dt_exp")
        s_dt_exp_in = sem("dt_exp_in")
        s_dt_read = sem("dt_read")
        s_dtT_read = sem("dtT_read")
        s_dta_ready = sem("dta_ready")
        s_dve_step = sem("dve_step")
        s_eact_a = sem("eact_a")
        s_eact_sb = sem("eact_sb")
        s_exp_done = sem("exp_done")
        s_fin_ready = sem("fin_ready")
        s_g_read = sem("g_read")
        s_gu_mm = sem("gu_mm")
        s_h1T_read = sem("h1T_read")
        s_h1_ready = sem("h1_ready")
        s_hT_read = sem("hT_read")
        s_h_ready = sem("h_ready")
        s_kv_read = sem("kv_read")
        s_lmat_exp = sem("lmat_exp")
        s_ln0_in = sem("ln0_in")
        s_ln1_in = sem("ln1_in")
        s_ln2_in = sem("ln2_in")
        s_m_ready = sem("m_ready")
        s_mix_read = sem("mix_read")
        s_mix_ready = sem("mix_ready")
        s_nmax_ready = sem("nmax_ready")
        s_onehot_a = sem("onehot_a")
        s_rowf_moved = sem("rowf_moved")
        s_onehot_ready = sem("onehot_ready")
        s_out_st = sem("out_st")
        s_pT_read = sem("pT_read")
        s_p_in = sem("p_in")
        s_par_in = sem("par_in")
        s_par_read = sem("par_read")
        s_pe_av = sem("pe_av")
        s_pe_cb = sem("pe_cb")
        s_pe_dt = sem("pe_dt")
        s_pe_g = sem("pe_g")
        s_pe_h1T = sem("pe_h1T")
        s_pe_hT = sem("pe_hT")
        s_pe_kv = sem("pe_kv")
        s_pe_mix = sem("pe_mix")
        s_pe_pT = sem("pe_pT")
        s_pe_par = sem("pe_par")
        s_pe_pl = sem("pe_pl")
        s_pe_pt = sem("pe_pt")
        s_pe_q = sem("pe_q")
        s_pe_rk = sem("pe_rk")
        s_pe_rt = sem("pe_rt")
        s_pe_sc = sem("pe_sc")
        s_pe_seg = sem("pe_seg")
        s_pe_st = sem("pe_st")
        s_pe_xbc = sem("pe_xbc")
        s_pe_xt = sem("pe_xt")
        s_pe_yT = sem("pe_yT")
        s_pe_ya = sem("pe_ya")
        s_pe_yd = sem("pe_yd")
        s_pe_yo = sem("pe_yo")
        s_pe_ys = sem("pe_ys")
        s_pe_z = sem("pe_z")
        s_pg_read = sem("pg_read")
        s_pg_tanh = sem("pg_tanh")
        s_pool_step = sem("pool_step")
        s_pp_read = sem("pp_read")
        s_prob_ready = sem("prob_ready")
        s_pt_read = sem("pt_read")
        s_q_read = sem("q_read")
        s_rk_read = sem("rk_read")
        s_roots = sem("roots")
        s_scaled = sem("scaled")
        s_last_normed = sem("last_normed")
        s_rows_ready = sem("rows_ready")
        s_rt_exp = sem("rt_exp")
        s_rt_exp_in = sem("rt_exp_in")
        s_rt_read = sem("rt_read")
        s_sc_read = sem("sc_read")
        s_seg_read = sem("seg_read")
        s_sel_ready = sem("sel_ready")
        s_silu_done = sem("silu_done")
        s_small_in = sem("small_in")
        s_st_read = sem("st_read")
        s_tanh_sb = sem("tanh_sb")
        s_tz_done = sem("tz_done")
        s_w_hi = sem("w_hi")
        s_w_lo = sem("w_lo")
        s_wdt_split = sem("wdt_split")
        s_hT_hi = sem("hT_hi")
        s_wple_in = sem("wple_in")
        s_wsmall_in = sem("wsmall_in")
        s_xT_mm = sem("xT_mm")
        s_xdec_ready = sem("xdec_ready")
        s_xdt_ready = sem("xdt_ready")
        s_xgT_sb = sem("xgT_sb")
        s_xt_read = sem("xt_read")
        s_yT_read = sem("yT_read")
        s_y_act = sem("y_act")
        s_y_dve = sem("y_dve")
        s_y_mm = sem("y_mm")
        s_y_ready = sem("y_ready")
        s_ya_read = sem("ya_read")
        s_yd_read = sem("yd_read")
        s_yo_read = sem("yo_read")
        s_ys_read = sem("ys_read")
        s_z_read = sem("z_read")
        s_zero_set = sem("zero_set")
        s_zeroed = sem("zeroed")
        sems = {x.name: x for x in (
            s_av_read, s_dtT_read, s_cb_act, s_cb_dve, s_conv_read, s_dt_read, s_g_read, s_h1T_read, s_hT_read,
            s_kv_read, s_mix_read, s_pT_read, s_par_read, s_pg_read, s_pp_read, s_pt_read, s_q_read,
            s_rk_read, s_rt_read, s_sc_read, s_seg_read, s_st_read, s_xt_read, s_yT_read, s_ya_read,
            s_yd_read, s_yo_read, s_ys_read, s_z_read, s_pe_g, s_pe_kv, s_pe_mix,
            s_pe_q, s_pe_xbc, s_pe_ya, s_pe_ys, s_pe_z)}
        x_in = [sem(f"x_in{i}") for i in range(NT)]
        y_gath = [sem(f"y_gath{i}") for i in range(NT)]
        pgw_in = [sem(f"pgw_in{b}") for b in range(2)]
        y_st = [sem(f"y_st{b}") for b in range(2)]
        plan, plan_last = psum_plan(sems)

        def bank(key, n=512, banks=1):
            b = plan[key][0]
            flat = psum[:, b:b + banks, :].rearrange("p b n -> p (b n)")
            return flat[:, 0:n]

        loads = stream_order(aps)
        wg = aps["w_exp_gate"].rearrange("l g e d f -> (l g e) d f")
        wu = aps["w_exp_up"].rearrange("l g e d f -> (l g e) d f")
        wd = aps["w_exp_down"].rearrange("l g e f d -> (l g e) f d")
        x_v = aps["x"][0].rearrange("(i p) n -> p i n", p=P)
        p_v = aps["p"][0, 0].rearrange("(i p) n -> p i n", p=P)
        out_v = out[0].rearrange("(i p) n -> i p n", p=P)

        def landings(slot, seq):
            return sum(len(loads[q]) for q in range(seq + 1) if SLOT_OF[q] == slot)

        def arrived(eng, seq):
            eng.wait_ge(slot_in[SLOT_OF[seq]], 16 * landings(SLOT_OF[seq], seq))

        def w_parts(seq):
            return ring_parts[:, HI_OF[seq]], ring_parts[:, SLOT_OF[seq]]

        def z_part(n):
            i, c = 2 * (n % 2), 256 * (n // 2)
            return sz[:, i:i + 2, c:c + 256]

        def expert_slot(parity, half, w):
            return 6 * parity + 3 * half + w

        def expert_slot_in(eng, former, parity, half, w):
            s = expert_slot(parity, half, w)
            eng.wait_ge(slot_in[s], former * 16 + 16 * (landings(s, len(loads) - 1) + 1))

        block = ctx.enter_context(nc.Block())

        @block.sync
        def _(sp):
            for i in range(NT):
                sp.dma_start(h[:, i, :], x_v[:, i, :]).then_inc(x_in[i], 16)
            for seq, parts in enumerate(loads):
                slot = SLOT_OF[seq]
                if seq >= 4:
                    name, value = FREED[seq - 4]
                    sp.wait_ge(sems[name], value)
                for src, rows, kind, columns in parts:
                    view = (ring if kind == "kn" else ringN)[rows, slot, :, columns]
                    sp.dma_start(view, src).then_inc(slot_in[slot], 16)
                if seq == 3:
                    sp.dma_start(w_dt, aps["w_in"][0].rearrange("(k p) n -> p k n", p=P)[:, :, COL_DT:COL_DT + 16])\
                        .then_inc(s_wsmall_in, 16)
                    sp.dma_start(w_rt[:, :, 0:NG], aps["w_router_group"][0].rearrange("(k p) n -> p k n", p=P))\
                        .then_inc(s_wsmall_in, 16)
                    sp.dma_start(w_rt[:, :, NG:36], aps["w_router_expert"][0].rearrange("(k p) n -> p k n", p=P))\
                        .then_inc(s_wsmall_in, 16)

            w_pg = aps["w_ple_gate"][0].rearrange("(k p) n -> p k n", p=P)

            def gate_slice(s):
                sp.dma_start(pgw[s % 2], w_pg[:, :, PS * s:PS * (s + 1)]).then_inc(pgw_in[s % 2], 16)

            def experts(p, u):
                for half in range(2):
                    for w, t in ((0, wg), (1, wu)):
                        if isinstance(p, int) and p < 2:
                            name, value = MOE_FREED[6 * p + 3 * half + w]
                            sp.wait_ge(sems[name], value)
                        elif half == w == 0:
                            sp.wait_ge(s_gu_mm, p - 1)
                        src = t[bass.ds(p * 2 + half, 1)].rearrange("a (k p) f -> p (a k) f", p=P)
                        slot = expert_slot(u % 2, half, w)
                        sp.dma_start(ring[:, slot], src).then_inc(slot_in[slot], 16)
                for half in range(2):
                    if isinstance(p, int) and p < 2:
                        name, value = MOE_FREED[6 * p + 3 * half + 2]
                        sp.wait_ge(sems[name], value)
                    elif half == 0:
                        sp.wait_ge(s_y_mm, p - 1)
                    src = wd[bass.ds(p * 2 + half, 1)].rearrange("a (k p) n -> p (a k) n", p=P)
                    slot = expert_slot(u % 2, half, 2)
                    sp.dma_start(ringN[:, slot], src).then_inc(slot_in[slot], 16)

            sp.wait_ge(s_pe_ya, KD)
            gate_slice(1)
            sp.wait_ge(s_ys_read, KD)
            gate_slice(0)
            sp.wait_ge(s_pe_mix, 2 * NT)
            sp.dma_start(wple, aps["w_ple"][0].rearrange("(k p) n -> p k n", p=P)).then_inc(s_wple_in, 16)
            experts(0, 0)
            sp.wait_ge(s_pe_pl, NT)
            gate_slice(2)
            sp.wait_ge(s_pe_pl, 2 * NT)
            gate_slice(3)
            for u in range(1, 4):
                experts(u, u)
            with sp.Fori(1, PAIRS // 4) as e4:
                for u in range(4):
                    experts(e4 * 4 + u, u)
            sp.wait_ge(s_ctl_ready, 1)
            pairs = sp.value_load(ctl[0:1, EXTRA + 1:EXTRA + 2], min_val=0, max_val=MORE_PAIRS)
            with sp.Fori(0, MORE_PAIRS) as j:
                with sp.If(pairs > j):
                    sp.wait_ge(s_y_mm, j + PAIRS)
                    for half in range(2):
                        e = sp.value_load(ctl[0:1, bass.ds(j * 2 + half, 1)], min_val=0, max_val=NE - 1)
                        for w, t in ((0, wg), (1, wu)):
                            src = t[bass.ds(e, 1)].rearrange("a (k p) f -> p (a k) f", p=P)
                            slot = expert_slot(0, half, w)
                            sp.dma_start(ring[:, slot], src).then_inc(slot_in[slot], 16)
                        src = wd[bass.ds(e, 1)].rearrange("a (k p) n -> p (a k) n", p=P)
                        slot = expert_slot(0, half, 2)
                        sp.dma_start(ringN[:, slot], src).then_inc(slot_in[slot], 16)
                sp.nop()

        @block.gpsimd
        def _(pool):
            steps = [0]

            def link(ins):
                steps[0] += 1
                ins.then_inc(s_pool_step, 1)
                pool.wait_ge(s_pool_step, steps[0])

            g = nc.gpsimd
            pool.dma_start(ln_w, aps["ln0_w"].rearrange("(a n) -> a n", a=1).broadcast_to([P, D])).then_inc(s_ln0_in, 16)
            pool.dma_start(ln_b, aps["ln0_b"].rearrange("(a n) -> a n", a=1).broadcast_to([P, D])).then_inc(s_ln0_in, 16)
            link(g.memset(ones, 1.0))
            g.affine_select(out=ident, in_=ones, pattern=[[1, P]], compare_op=ALU.is_equal, fill=0.0, base=0,
                            channel_multiplier=-1).then_inc(s_consts, 1)
            g.affine_select(out=upper, in_=ones, pattern=[[1, P]], compare_op=ALU.is_ge, fill=0.0, base=0,
                            channel_multiplier=-1).then_inc(s_consts, 1)
            g.affine_select(out=upstrict, in_=ones, pattern=[[1, P]], compare_op=ALU.is_gt, fill=0.0, base=0,
                            channel_multiplier=-1).then_inc(s_consts, 1)
            g.iota(iota_e, pattern=[[1, NE]], base=0, channel_multiplier=0,
                   allow_small_or_imprecise_dtypes=True).then_inc(s_consts, 1)
            g.iota(iota_r, pattern=[[1, P]], base=0, channel_multiplier=0,
                   allow_small_or_imprecise_dtypes=True).then_inc(s_consts, 1)
            for dst, name in ((dt_bias, "dt_bias"), (a_row, "a_log"), (dskip, "d_skip"), (sink, "sinks"),
                              (rbias[:, 0:NG], "b_router_group"), (rbias[:, NG:36], "b_router_expert")):
                pool.dma_start(dst, aps[name].broadcast_to([P, dst.shape[1]])).then_inc(s_small_in, 16)
            dist, mask = xs[:, 8, 0:256], xs[:, 9, 0:256]
            link(g.iota(dist, pattern=[[-1, 256]], base=P, channel_multiplier=1, allow_small_or_imprecise_dtypes=True))
            link(g.memset(mask, 0.0))
            link(g.memset(mask[0:64, 0:64], NEG))
            link(g.memset(mask[0:64, 192:256], NEG))
            g.memset(mask[64:128, 0:128], NEG).then_inc(s_dist_in, 1)
            zt = shaped(R_Y, "p (r n) -> p r n", r=2, n=D)
            pool.wait_ge(s_dist_in, 1)
            g.memset(zt, 0.0).then_inc(s_zero_set, 1)
            pool.wait_ge(s_zero_set, 1)

            def last_normed(x, w, b, norms):
                pool.wait_ge(s_scaled, norms)
                link(g.tensor_tensor(x, x, w, ALU.mult))
                g.tensor_tensor(x, x, b, ALU.add).then_inc(s_last_normed, 1)

            pool.wait_ge(s_ln0_in, 32)
            last_normed(h[:, NT - 1, :], ln_w, ln_b, 1)

            def rest(seq):
                hi, lo = w_parts(seq)
                pool.wait_ge(s_w_hi, seq + 1)
                g.tensor_tensor(lo, ring[:, SLOT_OF[seq]], hi.bitcast(F32), ALU.subtract).then_inc(s_w_lo, 1)

            for seq in range(2):
                rest(seq)
            zview_y = y_dram[NE * CAP:ROWS].rearrange("(p r) n -> p r n", p=P)
            for r in range(0, zview_y.shape[1], 2):
                pool.dma_start(zview_y[:, r:r + 2, :], zt).then_inc(s_zeroed, 16)
            for seq in range(2, 8):
                rest(seq)
            pool.wait_ge(s_pe_hT, 2 * NT)
            for i in range(NT):
                g.tensor_scalar(h[:, i, :], h[:, i, :], ALPHA, None, ALU.mult).then_inc(s_ah_ready, 1)
            for seq in range(8, PROJ):
                rest(seq)
            pool.wait_ge(s_pe_yT, NT)
            for dst, name, landed in ((A1w, "ln1_w", s_ln1_in), (A1b, "ln1_b", s_ln1_in), (bple, "b_ple_gate", s_bple_in)):
                pool.dma_start(dst, aps[name].broadcast_to([P, D])).then_inc(landed, 16)
            pool.dma_start(p_in, p_v).then_inc(s_p_in, 16)
            pool.wait_ge(s_h1_ready, NT)
            for dst, name in ((A1w, "ln2_w"), (A1b, "ln2_b")):
                pool.dma_start(dst, aps[name].broadcast_to([P, D])).then_inc(s_ln2_in, 16)
            for i in range(NT):
                g.tensor_scalar(sz[:, i, :], h[:, i, :], ALPHA, None, ALU.mult).then_inc(s_ah1_ready, 1)
            pool.wait_ge(s_rows_ready, 2)
            pool.wait_ge(s_blocks_stored, 1)
            for i in range(NT):
                for c in range(2):
                    g.indirect_dma_start(
                        out=ygat[:, i, c, :], out_offset=None, in_=y_dram,
                        in_offset=bass.IndirectOffsetOnAxis(ap=rowsU[:, 2 * i + c:2 * i + c + 1], axis=0),
                        bounds_check=ROWS - 1, oob_is_err=False).then_inc(y_gath[i], 16)
            pool.wait_ge(s_ln2_in, 32)
            last_normed(sz[:, NT - 1, :], A1w, A1b, 2)

        @block.tensor
        def _(pe):
            mm, tr = nc.tensor.matmul, nc.tensor.transpose

            def opened(key, n=512, banks=1):
                for s, v in plan[key][1]:
                    pe.wait_ge(s, v)
                return bank(key, n, banks)

            pe.wait_ge(s_consts, 5)
            for i in range(NT):
                if i < NT - 1:
                    pe.wait_ge(s_h_ready, i + 1)
                else:
                    pe.wait_ge(s_last_normed, 1)
                for b in range(2):
                    o = opened(("hT", i, b))
                    for k in range(4):
                        c = (4 * b + k) * P
                        t = tr(o[:, k * P:(k + 1) * P], h[:, i, c:c + P], ident)
                    t.then_inc(s_pe_hT, 1)
            pe.wait_ge(s_par_in, 64)
            tr(opened("par")[:, 0:74], par_rows, ident[0:74, 0:74]).then_inc(s_pe_par, 1)
            pe.wait_ge(s_hT_read, 2 * NT)

            def thrice(o, w_hi, w_lo, h_hi, h_lo, first, last, h_stationary=False):
                for j, (a, b) in enumerate(((w_hi, h_hi), (w_hi, h_lo), (w_lo, h_hi)) if not h_stationary else
                                           ((h_hi, w_hi), (h_hi, w_lo), (h_lo, w_hi))):
                    t = mm(o, a, b, start=(first and j == 0), stop=(last and j == 2))
                return t

            def proj(o, seq, columns, signal):
                pe.wait_ge(s_w_lo, seq + 1)
                w_hi, w_lo = w_parts(seq)
                for k in range(KD):
                    t = thrice(o, w_hi[:, k, columns], w_lo[:, k, columns], hT_hi[:, k, :], hT_lo[:, k, :],
                               k == 0, k == KD - 1)
                t.then_inc(signal, 1)

            def proj_tokens(o, seq, columns, i):
                pe.wait_ge(s_w_lo, seq + 1)
                w_hi, w_lo = w_parts(seq)
                ts = slice(i * P, (i + 1) * P)
                for k in range(KD):
                    t = thrice(o, w_hi[:, k, columns], w_lo[:, k, columns], hT_hi[:, k, ts], hT_lo[:, k, ts],
                               k == 0, k == KD - 1, h_stationary=True)
                return t

            def tile_of(n):
                return slice((n % 2) * P, (n % 2 + 1) * P)

            for n in range(NX):
                proj(opened(("xbc", n)), SEQ_XBC + n // 2, tile_of(n), s_pe_xbc)
            pe.wait_ge(s_wdt_split, 2)
            o = opened("dtT")
            for k in range(KD):
                t = thrice(o[0:16], w_dt_hi[:, k, :], w_dt_lo[:, k, :], hT_hi[:, k, :], hT_lo[:, k, :],
                           k == 0, k == KD - 1)
            t.then_inc(s_pe_dt, 1)
            proj(opened("k"), SEQ_KV, tile_of(0), s_pe_kv)
            proj(opened("vT"), SEQ_KV, tile_of(1), s_pe_kv)
            for j in range(4):
                if j == 2:
                    o = opened("dt", 64)
                    pe.wait_ge(s_dtT_read, 1)
                    for i in range(NT):
                        t = tr(o[:, 16 * i:16 * i + 16], dtT[:, i * P:(i + 1) * P], ident[0:16, 0:16])
                    t.then_inc(s_pe_dt, 1)
                proj(opened(("q", j)), SEQ_Q + j // 2, tile_of(j), s_pe_q)
            o = opened("v")
            pe.wait_ge(s_kv_read, 2)
            for i in range(NT):
                t = tr(o[:, i * P:(i + 1) * P], vT[:, i * P:(i + 1) * P], ident)
            t.then_inc(s_pe_kv, 1)

            def scores(n):
                i, hf = divmod(n, 2)
                w = 256 if i else P
                if n == 0:
                    pe.wait_ge(s_kv_read, 2)
                    pe.wait_ge(s_q_read, 4)
                o = opened(("sc", n), D, 2).rearrange("p (m w) -> p m w", m=4)
                for m in (0, 2, 1, 3):
                    g = (m // 2) * HD
                    t = mm(o[:, m, 0:w], qT[g:g + HD, 2 * hf + m % 2, i * P:(i + 1) * P],
                           kT[g:g + HD, (i + 1) * P - w:(i + 1) * P], start=True, stop=True)
                t.then_inc(s_pe_sc, 1)

            def zproj(n):
                o = opened(("z", n))
                for j in range(2):
                    t = proj_tokens(o[:, 256 * j:256 * (j + 1)], SEQ_Z + n // 2, slice(0, 256), 2 * (n % 2) + j)
                t.then_inc(s_pe_z, 1)

            def probs_t(n):
                i = n // 2
                kt = 2 if i else 1
                pe.wait_ge(s_prob_ready, n + 1)
                o = opened(("pt", n), D, 2).rearrange("p (m w t) -> p m w t", m=4, w=2)
                for m in range(4):
                    for w in range(kt):
                        t = tr(o[:, m, w, :], prob[:, m, w * P:(w + 1) * P], ident)
                t.then_inc(s_pe_pt, 1)

            def attend(n):
                i, hf = divmod(n, 2)
                kt = 2 if i else 1
                pe.wait_ge(s_pt_read, n + 1)
                if n == 0:
                    pe.wait_ge(s_kv_read, 3)
                o = opened(("av", n), 256)
                for m in range(4):
                    g = (m // 2) * HD
                    for w in range(kt):
                        t = mm(o[g:g + HD, (m % 2) * P:(m % 2 + 1) * P], vt[:, i - kt + 1 + w, g:g + HD],
                               probT[:, m, w, :], start=(w == 0), stop=(w == kt - 1))
                t.then_inc(s_pe_av, 1)

            gate_units = iter(range(2 * KD))

            def gate():
                g = next(gate_units)
                n, b = gate_of(g)
                proj(opened(("g", g)), SEQ_GATE[n // 2] + b, tile_of(n), s_pe_g)

            scores(0)
            for n in range(8):
                zproj(n)
                if n < 7:
                    scores(n + 1)
                if n:
                    attend(n - 1)
                probs_t(n)
            attend(7)

            pe.wait_ge(s_silu_done, NX)
            pe.wait_ge(s_dta_ready, 1)

            def chunk_in(c):
                ts = slice(c * P, (c + 1) * P)
                o = opened(("xt", c), D, 2)
                for k in range(KD):
                    t = tr(o[:, k * P:(k + 1) * P], xs[:, k, ts], ident)
                t.then_inc(s_pe_xt, 1)
                o = opened(("cb", c), D, 2)
                tr(o[:, 0:P], xs[:, 8, ts], ident)
                for g in range(2):
                    gs = slice(64 * g, 64 * g + 64)
                    mm(o[:, P + g * 512:2 * P + g * 512], xs[gs, 8, ts], xs[gs, 9, ts], start=True, stop=True)
                mm(o[:, 256:272], upper, dta[:, c, :], start=True, stop=True)
                mm(o[:, 272:288], ones, dta[:, c, :], start=True, stop=True).then_inc(s_pe_cb, 1)

            chunk_in(0)
            for c in range(NT):
                ts = slice(c * P, (c + 1) * P)

                def seg(q):
                    o = opened(("seg", c, q))
                    for m in range(4):
                        hh = 4 * q + m
                        t = mm(o[:, m * P:(m + 1) * P], dta[:, c, hh:hh + 1].broadcast_to([P, P]), upper,
                               start=True, stop=True)
                    t.then_inc(s_pe_seg, 1)

                for q in range(4):
                    seg(q)
                gate()
                if c:
                    o = opened(("yo", c), D, 2)
                    pe.wait_ge(s_st_read, c)
                    for g in range(2):
                        gs = slice(64 * g, 64 * g + 64)
                        t = mm(o[:, g * 512:(g + 1) * 512], xs[gs, 9, ts], state[gs, :], start=True, stop=True)
                    t.then_inc(s_pe_yo, 1)
                o = opened(("yd", c), D, 2)
                pe.wait_ge(s_xdt_ready, c + 1)
                for q in range(4):
                    pe.wait_ge(s_m_ready, 4 * c + q + 1)
                    for m in range(4):
                        hh = 4 * q + m
                        t = mm(o[:, hh * SP:(hh + 1) * SP], lmat[:, q % 2, m, :], xdt[:, hh * SP:(hh + 1) * SP],
                               start=True, stop=True)
                    t.then_inc(s_pe_yd, 1)
                    if q == 1:
                        gate()
                if c < NT - 1:
                    o = opened(("st", c))
                    pe.wait_ge(s_xdec_ready, c + 1)
                    pe.wait_ge(s_cb_act, c + 1)
                    for g in range(2):
                        gs = slice(64 * g, 64 * g + 64)
                        t = mm(o[gs, :], btok[:, gs], xdec[:, g * 512:(g + 1) * 512], start=True, stop=True)
                    t.then_inc(s_pe_st, 1)
                gate()
                gate()
                if c < NT - 1:
                    chunk_in(c + 1)
                pe.wait_ge(s_y_ready, c + 1)
                o = opened(("yT", c), D, 2)
                for k in range(KD):
                    t = tr(o[:, k * P:(k + 1) * P], y[:, k * P:(k + 1) * P], ident)
                t.then_inc(s_pe_yT, 1)

            pe.wait_ge(s_av_read, 8)
            for s in range(2):
                arrived(pe, SEQ_WOA + s)
            for n in range(KD):
                o = opened(("ya", n))
                for j in range(4):
                    s = SLOT_OF[SEQ_WOA + j // 2]
                    t = mm(o, ringN[:, s, j % 2, n * P:(n + 1) * P], yaT[:, j, :], start=(j == 0), stop=(j == 3))
                t.then_inc(s_pe_ya, 1)
            pe.wait_ge(s_yT_read, NT)
            for s in range(4):
                arrived(pe, SEQ_WOS + s)
            for n in range(KD):
                o = opened(("ys", n)).rearrange("p (i t) -> p i t", i=NT)
                for k in range(KD):
                    s = SLOT_OF[SEQ_WOS + k // 2]
                    t = mm(o, ringN[:, s, k % 2, n * P:(n + 1) * P], yT[:, :, k, :], start=(k == 0), stop=(k == KD - 1))
                t.then_inc(s_pe_ys, 1)
            pe.wait_ge(s_mix_ready, KD)
            for s in range(4):
                arrived(pe, SEQ_WO + s)
            for i in range(NT):
                for b in range(2):
                    o = opened(("mix", i, b))
                    for k in range(KD):
                        s = SLOT_OF[SEQ_WO + k // 2]
                        t = mm(o, mixT[:, k, i * P:(i + 1) * P], ringN[:, s, k % 2, b * 512:(b + 1) * 512],
                               start=(k == 0), stop=(k == KD - 1))
                    t.then_inc(s_pe_mix, 1)
            pe.wait_ge(s_p_in, 16)
            for kk in range(2):
                o = opened(("pT", kk))
                for i in range(NT):
                    t = tr(o[:, i * P:(i + 1) * P], p_in[:, i, kk * P:(kk + 1) * P], ident)
                t.then_inc(s_pe_pT, 1)

            def route(o, i):
                pe.wait_ge(s_wsmall_in, 16 * 3)
                pe.wait_ge(s_h1T_read, i + 1)
                for k in range(KD):
                    t = mm(o[:, 36 * i:36 * i + 36], hT[:, k, i * P:(i + 1) * P], w_rt[:, k, :], start=(k == 0),
                           stop=(k == KD - 1))
                return t

            for i in range(NT):
                pe.wait_ge(s_h1_ready, i + 1)
                o = opened(("h1T", i), D, 2)
                for k in range(KD):
                    t = tr(o[:, k * P:(k + 1) * P], h[:, i, k * P:(k + 1) * P], ident)
                t.then_inc(s_pe_h1T, 1)
                if i == 1:
                    logits = opened("rt", NT * 36)
                if i:
                    route(logits, i - 1)
            route(logits, NT - 1).then_inc(s_pe_rt, 1)

            pe.wait_ge(s_wple_in, 16)
            pe.wait_ge(s_pT_read, 2)
            for n in range(4 * NT):
                s, i = divmod(n, NT)
                pe.wait_ge(pgw_in[s % 2], 16 * (s // 2 + 1))
                o = opened(("pl", n))
                for k in range(KD):
                    mm(o[:, 0:PS], hT[:, k, i * P:(i + 1) * P], pgw[s % 2][:, k, :], start=(k == 0), stop=(k == KD - 1))
                for k in range(2):
                    t = mm(o[:, PS:2 * PS], pT[:, k, i * P:(i + 1) * P], wple[:, k, PS * s:PS * (s + 1)],
                           start=(k == 0), stop=(k == 1))
                t.then_inc(s_pe_pl, 1)
                if n == RANKS_AFTER:
                    pe.wait_ge(s_sel_ready, 1)
                    o = opened("rk", 160)
                    for a in range(NT):
                        for j in range(a + 1):
                            mm(o[:, 32 * a:32 * a + 32], upstrict if j == a else ones, rw[0][:, j, :],
                               start=(j == 0), stop=(j == a))
                    for j in range(NT):
                        t = mm(o[:, 128:160], ones, rw[0][:, j, :], start=(j == 0), stop=(j == NT - 1))
                    t.then_inc(s_pe_rk, 1)

            for s, v in plan_last:
                pe.wait_ge(s, v)
            sides = [slice(half * CAP, (half + 1) * CAP) for half in range(2)]

            def fetch(half, buf, part):
                if not (isinstance(half, int) and half < 2):
                    pe.wait_ge(s_xgT_sb, half - 1)
                o = psum[:, 2 + 5 * part, :].rearrange("p (k t) -> p k t", k=4)
                for k in range(4):
                    c = (4 * part + k) * P
                    for i in range(NT):
                        t = mm(o[:, k, :], h[:, i, c:c + P], onehot[:, buf, i, :], start=(i == 0), stop=(i == NT - 1))
                t.then_inc(s_xT_mm, 1)

            def gate_up(former, u, buf, halves):
                for half in range(2):
                    expert_slot_in(pe, former, u % 2, half, 0)
                    expert_slot_in(pe, former, u % 2, half, 1)
                pe.wait_ge(s_xgT_sb, halves)
                for k in range(KD):
                    for half in range(2):
                        s = expert_slot(u % 2, half, 0)
                        t = mm(psum[sides[half], u % 2, :], xgT[:, buf, k, sides[half]], ring[:, s:s + 2, k, :],
                               start=(k == 0), stop=(k == KD - 1))
                t.then_inc(s_gu_mm, 1)

            def down(p, former, u):
                for half in range(2):
                    expert_slot_in(pe, former, u % 2, half, 2)
                pe.wait_ge(s_aT_sb, p + 1)
                if not (isinstance(p, int) and p == 0):
                    pe.wait_ge(s_y_act, p)
                    pe.wait_ge(s_y_dve, p)
                for b in range(2):
                    for k in range(2):
                        for half in range(2):
                            s = expert_slot(u % 2, half, 2)
                            t = mm(psum[sides[half], 4 + b, :], eactT[:, u % 2, k, sides[half]],
                                   ringN[:, s, k, b * 512:(b + 1) * 512], start=(k == 0), stop=(k == 1))
                t.then_inc(s_y_mm, 1)

            def act_t(p, u):
                pe.wait_ge(s_eact_sb, p + 1)
                if not (isinstance(p, int) and p == 0):
                    pe.wait_ge(s_aT_sb, p)
                o = psum[:, 3, 0:256].rearrange("p (k t) -> p k t", k=2)
                for k in range(2):
                    t = tr(o[:, k, :], eact[:, u % 2, k * P:(k + 1) * P], ident)
                t.then_inc(s_aT_mm, 1)

            def step(e4, u):
                p = e4 * 4 + u
                start = isinstance(e4, int) and u == 0
                gate_up(e4 * 2 + u // 2, u, u % 2, p * 2 + 2)
                pe.wait_ge(s_onehot_ready, p + 2)
                fetch(p * 2 + 2, 1 - u % 2, 0)
                if not start:
                    down(p - 1, e4 * 2 + (u - 1) // 2, (u - 1) % 4)
                fetch(p * 2 + 3, 1 - u % 2, 1)
                act_t(p, u)

            pe.wait_ge(s_onehot_ready, 1)
            for part in range(2):
                fetch(part, 0, part)
            for u in range(4):
                step(0, u)
            with pe.Fori(1, PAIRS // 4) as e4:
                for u in range(4):
                    step(e4, u)
            down(PAIRS - 1, PAIRS // 2 - 1, 3)
            pe.wait_ge(s_ctl_ready, 1)
            pairs = pe.value_load(ctl[0:1, EXTRA + 1:EXTRA + 2], min_val=0, max_val=MORE_PAIRS)
            with pe.Fori(0, MORE_PAIRS) as j:
                with pe.If(pairs > j):
                    pe.wait_ge(s_onehot_ready, j + PAIRS + 3)
                    for part in range(2):
                        fetch(j * 2 + 2 * PAIRS + 2 + part, 0, part)
                    gate_up(j + PAIRS // 2, 0, 0, j * 2 + 2 * PAIRS + 4)
                    act_t(j + PAIRS, 0)
                    down(j + PAIRS, j + PAIRS // 2, 0)
                pe.nop()

        @block.scalar
        def _(act):
            A = nc.scalar.activation

            def copy(dst, src):
                return nc.scalar.copy(dst, src)

            sums_made = [0]

            def summed(ins):
                sums_made[0] += 1
                ins.then_inc(s_act_sums, 1)
                act.wait_ge(s_act_sums, sums_made[0])

            def tile_stats(x, i, scratch):
                total, minus_mean, squares = (sums[:, i, j:j + 1] for j in range(3))
                summed(A(scratch, x, ACT.Copy, accum_out=total))
                A(mva[:, i, 0:1], total, ACT.Copy, scale=1.0 / D)
                summed(A(minus_mean, total, ACT.Copy, scale=-1.0 / D))
                summed(A(scratch, x, ACT.Square, bias=minus_mean, accum_out=squares))
                A(mva[:, i, 1:2], squares, ACT.Copy, scale=1.0 / D).then_inc(s_act_stats, 1)

            def scaled(x, norms):
                act.wait_ge(s_roots, norms)
                A(x, x, ACT.Identity, scale=rv[1][:, NT - 1:NT], bias=rv[3][:, NT - 1:NT]).then_inc(s_scaled, 1)

            act.dma_start(par_rows[0:40], aps["conv_w"][0].rearrange("w (n p) -> (w n) p", p=P)).then_inc(s_par_in, 16)
            act.dma_start(par_rows[40:50], aps["conv_b"].rearrange("l (n p) -> (l n) p", p=P)).then_inc(s_par_in, 16)
            act.dma_start(par_rows[50:66], aps["b_gate"][0].rearrange("b (n p) -> (b n) p", p=P)).then_inc(s_par_in, 16)
            act.dma_start(par_rows[66:74], aps["ssd_norm_w"].rearrange("l (n p) -> (l n) p", p=P)).then_inc(s_par_in, 16)
            act.wait_ge(x_in[1], 16)
            tile_stats(h[:, 1, :], 1, sz[:, 1, :])
            scaled(h[:, NT - 1, :], 1)

            def part(seq):
                arrived(act, seq)
                if seq >= 6:
                    name, value = USED[seq - 6 if seq < 14 else seq - 2]
                    act.wait_ge(sems[name], value)
                copy(w_parts(seq)[0], ring[:, SLOT_OF[seq]]).then_inc(s_w_hi, 1)

            part(0)
            part(1)
            for i in range(NT):
                for b in range(2):
                    act.wait_ge(s_pe_hT, 2 * i + b + 1)
                    copy(hT_hi[:, 4 * b:4 * b + 4, i * P:(i + 1) * P],
                         bank(("hT", i, b)).rearrange("p (k t) -> p k t", k=4)).then_inc(s_hT_hi, 1)
            part(2)
            act.wait_ge(s_wsmall_in, 16 * 3)
            copy(w_dt_hi, w_dt).then_inc(s_wdt_split, 1)
            for n in range(NX):
                if n % 2:
                    part(3 + n // 2)
                act.wait_ge(s_conv_read, n + 1)
                if n >= 2:
                    act.wait_ge(s_silu_done, n - 1)
                A(ctanh[:, n % 2, :], xs[:, n, :], ACT.Tanh).then_inc(s_ctanh_done, 1)
            act.wait_ge(s_h_ready, NT - 1)
            act.wait_ge(s_last_normed, 1)
            act.wait_ge(s_pe_dt, 1)
            copy(dtT, bank("dtT")[0:16]).then_inc(s_dtT_read, 1)
            part(8)
            act.wait_ge(s_pe_kv, 1)
            copy(kT, bank("k")).then_inc(s_kv_read, 1)
            act.wait_ge(s_pe_kv, 2)
            copy(vT, bank("vT")).then_inc(s_kv_read, 1)
            part(9)
            act.wait_ge(s_par_read, 1)
            for j in range(4):
                act.wait_ge(s_pe_q, j + 1)
                copy(qT[:, j, :], bank(("q", j))).then_inc(s_q_read, 1)
                if j % 2:
                    part(10 + j // 2)
                if j == 1:
                    act.wait_ge(s_dt_exp_in, 1)
                    A(dta.rearrange("p i n -> p (i n)"), dta.rearrange("p i n -> p (i n)"), ACT.Exp)\
                        .then_inc(s_dt_exp, 1)
                    A(a_row, a_row, ACT.Exp).then_inc(s_dt_exp, 1)
            act.wait_ge(s_pe_kv, 3)
            copy(vt, bank("v").rearrange("p (i n) -> p i n", i=NT)).then_inc(s_kv_read, 1)

            def z_tanh(n):
                act.wait_ge(s_pe_z, n + 1)
                if n == 0:
                    act.wait_ge(s_silu_done, NX)
                A(z_part(n), bank(("z", n)).rearrange("p (i n) -> p i n", i=2), ACT.Tanh, scale=0.5)\
                    .then_inc(s_tz_done, 1)
                if n in (1, 3):
                    part(12 + n // 2)

            def softmax_exp(n):
                w = 256 if n >= 2 else P
                act.wait_ge(s_nmax_ready, n + 1)
                a = att[:, n % 2]
                for m in range(4):
                    A(prob[:, m, 0:w], prob[:, m, 0:w], ACT.Exp, bias=a[:, 1, m:m + 1],
                      accum_out=a[:, 3, m:m + 1])
                A(a[:, 2, :], a[:, 2, :], ACT.Exp).then_inc(s_exp_done, 1)

            def probs_out(n):
                act.wait_ge(s_pe_pt, n + 1)
                if n:
                    act.wait_ge(s_pe_av, n)
                w = 2 if n >= 2 else 1
                copy(probT[:, :, 0:w, :], bank(("pt", n), D, 2).rearrange("p (m w t) -> p m w t", m=4, w=2)[:, :, 0:w, :])\
                    .then_inc(s_pt_read, 1)

            def attn_out(n):
                i, hf = divmod(n, 2)
                act.wait_ge(s_pe_av, n + 1)
                if n == 0:
                    act.wait_ge(s_zeroed, 16 * ZERO_DMAS)
                copy(yaT[:, 2 * hf:2 * hf + 2, i * P:(i + 1) * P], bank(("av", n), 256).rearrange("p (j t) -> p j t", j=2))\
                    .then_inc(s_av_read, 1)

            for n in range(8):
                softmax_exp(n)
                z_tanh(n)
                if n:
                    attn_out(n - 1)
                probs_out(n)
            attn_out(7)

            def gate_tanh(g):
                n, b = gate_of(g)
                act.wait_ge(s_pe_g, g + 1)
                if g == 0:
                    act.wait_ge(s_pe_z, 8)
                A(gact[:, n, b, :], bank(("g", g)), ACT.Tanh, scale=0.5,
                  bias=b_gate[:, 8 * b + n:8 * b + n + 1]).then_inc(s_g_read, 1)
                if g % 2 and 14 + g // 2 < PROJ:
                    part(14 + g // 2)

            for c in range(NT):
                act.wait_ge(s_pe_xt, c + 1)
                if c:
                    act.wait_ge(s_y_ready, c)
                copy(xtok, bank(("xt", c), D, 2)).then_inc(s_xt_read, 1)
                act.wait_ge(s_cb_dve, c + 1)
                if c:
                    act.wait_ge(s_pe_st, c)
                o = bank(("cb", c), D, 2)
                copy(btok, o[:, 0:P])
                A(acs[:, 1:3, :], o[:, 256:288].rearrange("p (a n) -> p a n", a=2), ACT.Exp).then_inc(s_cb_act, 1)
                A(acs[:, 3, :], acs[:, 3, :], ACT.Exp).then_inc(s_acs_exp, 1)
                for q in range(4):
                    act.wait_ge(s_seg_read, 4 * c + q + 1)
                    A(lmat[:, q % 2], lmat[:, q % 2], ACT.Exp).then_inc(s_lmat_exp, 1)
                    if q == 1:
                        gate_tanh(4 * c)
                for j in range(1, 4):
                    gate_tanh(4 * c + j)
            for kk in range(2):
                act.wait_ge(s_pe_pT, kk + 1)
                copy(pT[:, kk, :], bank(("pT", kk))).then_inc(s_pT_read, 1)
            for i in range(NT):
                act.wait_ge(s_pe_h1T, i + 1)
                copy(hT[:, :, i * P:(i + 1) * P], bank(("h1T", i), D, 2).rearrange("p (k t) -> p k t", k=KD))\
                    .then_inc(s_h1T_read, 1)
            act.wait_ge(s_rt_exp_in, 1)
            A(lg[:, :, 0:NG], lg[:, :, 0:NG], ACT.Exp)
            A(rv[4], rv[4], ACT.Exp).then_inc(s_rt_exp, 1)
            for i in range(4 * NT):
                act.wait_ge(s_pg_read, i + 1)
                A(pgt[:, i % 4, :], pgt[:, i % 4, :], ACT.Tanh, scale=0.5).then_inc(s_pg_tanh, 1)

            def rows_copy(half, buf, part):
                act.wait_ge(s_xT_mm, half + 1)
                copy(xgT[:, buf, 4 * part:4 * part + 4, :], psum[:, 2 + 5 * part, :].rearrange("p (k t) -> p k t", k=4))\
                    .then_inc(s_xgT_sb, 1)

            def hidden_tanh(p, u):
                act.wait_ge(s_gu_mm, p + 1)
                A(eth[:, u % 2, :], psum[:, u % 2, 0:FF], ACT.Tanh, scale=0.5).then_inc(s_tanh_sb, 1)

            def act_copy(p, u):
                act.wait_ge(s_aT_mm, p + 1)
                copy(eactT[:, u % 2], psum[:, 3, 0:256].rearrange("p (k t) -> p k t", k=2)).then_inc(s_aT_sb, 1)

            def out_copy(p, stores, u):
                act.wait_ge(s_y_mm, p + 1)
                if not (isinstance(stores, int) and stores == 0):
                    act.wait_ge(y_st[u % 2], stores)
                copy(eout[:, u % 2, 0:512], psum[:, 4, :]).then_inc(s_y_act, 1)
                act.wait_ge(s_y_act, p + 1)
                act.wait_ge(s_y_dve, p + 1)
                act.dma_start(y_dram[bass.ds(p * 2 * CAP, 2 * CAP)], eout[:, u % 2, :]).then_inc(y_st[u % 2], 16)

            def step(e4, u):
                p = e4 * 4 + u
                hidden_tanh(p, u)
                rows_copy(p * 2 + 2, 1 - u % 2, 0)
                if not (isinstance(e4, int) and u == 0):
                    out_copy(p - 1, e4 * 32 + 16 * ((u - 1) // 2), (u - 1) % 4)
                rows_copy(p * 2 + 3, 1 - u % 2, 1)
                act_copy(p, u)

            act.wait_ge(s_pe_mix, 2 * NT)
            rows_copy(0, 0, 0)
            rows_copy(1, 0, 1)
            for u in range(4):
                step(0, u)
            with act.Fori(1, PAIRS // 4) as e4:
                for u in range(4):
                    step(e4, u)
            out_copy(PAIRS - 1, 16 * (PAIRS // 2 - 1), 3)
            pairs = act.value_load(ctl[0:1, EXTRA + 1:EXTRA + 2], min_val=0, max_val=MORE_PAIRS)
            with act.Fori(0, MORE_PAIRS) as j:
                with act.If(pairs > j):
                    p = j + PAIRS
                    for part in range(2):
                        rows_copy(j * 2 + 2 * PAIRS + 2 + part, 0, part)
                    hidden_tanh(p, 0)
                    act_copy(p, 0)
                    out_copy(p, j * 16 + 16 * (PAIRS // 2), 0)
                act.nop()
            act.wait_ge(y_st[0], pairs * 16 + 16 * (PAIRS // 2))
            act.wait_ge(y_st[1], 16 * (PAIRS // 2))
            copy(att[0:1, 0, 5, 0:1], att[0:1, 0, 4, 0:1]).then_inc(s_blocks_stored, 1)
            for i in range(NT - 1):
                act.wait_ge(s_combined, 2 * i + 2)
                tile_stats(sz[:, i, :], i, h[:, i, :])
            scaled(sz[:, NT - 1, :], 2)
            for i in (0, 1, 3, 2):
                if i < NT - 1:
                    act.wait_ge(s_fin_ready, i + 1)
                else:
                    act.wait_ge(s_last_normed, 2)
                act.dma_start(out_v[i], sz[:, i, :]).then_inc(s_out_st, 16)
            act.wait_ge(s_out_st, 16 * NT)

        @block.vector
        def _(dve):
            v = nc.vector
            steps, counts = [0], {}

            def link(ins):
                steps[0] += 1
                ins.then_inc(s_dve_step, 1)
                dve.wait_ge(s_dve_step, steps[0])

            def seen(s):
                counts[s.name] = counts.get(s.name, 0) + 1
                return counts[s.name]

            def rsqrt(dst, src, t):
                link(v.tensor_scalar(dst.bitcast(I32), src.bitcast(I32), -0.5, float(0x5F3759DF), ALU.mult, ALU.add))
                for _ in range(3):
                    link(v.tensor_tensor(t, dst, dst, ALU.mult))
                    link(v.scalar_tensor_tensor(t, t, -0.5, src, ALU.mult, ALU.mult))
                    link(v.scalar_tensor_tensor(dst, t, 1.5, dst, ALU.add, ALU.mult))

            def normed(x, w, b, signal):
                for s in range(2):
                    link(v.bn_stats(stats[:, 6 * s:6 * s + 6], x[:, 512 * s:512 * s + 512]))
                link(v.bn_aggr(mv[:, 0:2], stats))
                link(v.tensor_scalar(mv[:, 2:3], mv[:, 1:2], LN_EPS, None, ALU.add))
                rsqrt(mv[:, 3:4], mv[:, 2:3], mv[:, 4:5])
                link(v.scalar_tensor_tensor(x, x, mv[:, 0:1], w, ALU.subtract, ALU.mult))
                v.scalar_tensor_tensor(x, x, mv[:, 3:4], b, ALU.mult, ALU.add).then_inc(signal, 1)
                dve.wait_ge(signal, seen(signal))

            def tile_stats(x, i):
                for s in range(2):
                    link(v.bn_stats(stats[:, 6 * s:6 * s + 6], x[:, 512 * s:512 * s + 512]))
                link(v.bn_aggr(mva[:, i, :], stats))

            def tiles_normed(x, w, b, signal, then=lambda i: None):
                link(v.tensor_scalar(rv[0], mva[:, :, 1], LN_EPS, None, ALU.add))
                rsqrt(rv[1], rv[0], rv[2])
                v.scalar_tensor_tensor(rv[3], mva[:, :, 0], -1.0, rv[1], ALU.mult, ALU.mult).then_inc(s_roots, 1)
                for i in range(NT - 1):
                    link(v.scalar_tensor_tensor(x[:, i, :], x[:, i, :], mva[:, i, 0:1], w, ALU.subtract, ALU.mult))
                    v.scalar_tensor_tensor(x[:, i, :], x[:, i, :], rv[1][:, i:i + 1], b, ALU.mult, ALU.add)\
                        .then_inc(signal, 1)
                    dve.wait_ge(signal, seen(signal))
                    then(i)

            def h_rest(i):
                for b in range(2):
                    dve.wait_ge(s_hT_hi, 2 * i + b + 1)
                    o = (slice(None), slice(4 * b, 4 * b + 4), slice(i * P, (i + 1) * P))
                    v.tensor_tensor(hT_lo[o], bank(("hT", i, b)).rearrange("p (k t) -> p k t", k=4),
                                    hT_hi[o].bitcast(F32), ALU.subtract).then_inc(s_hT_read, 1)

            for i in (0, 2, 3):
                dve.wait_ge(x_in[i], 16)
                tile_stats(h[:, i, :], i)
            dve.wait_ge(s_act_stats, 1)
            dve.wait_ge(s_ln0_in, 32)
            tiles_normed(h, ln_w, ln_b, s_h_ready, lambda i: h_rest(i - 1) if i else None)
            for i in (NT - 2, NT - 1):
                h_rest(i)
            dve.wait_ge(s_pe_par, 1)
            v.tensor_copy(par, bank("par")[:, 0:74])\
                .then_inc(s_par_read, 1)
            dve.wait_ge(s_par_read, seen(s_par_read))
            link(v.tensor_scalar(par[:, 0:66], par[:, 0:66], 0.5, None, ALU.mult))
            dve.wait_ge(s_wdt_split, 1)
            v.tensor_tensor(w_dt_lo, w_dt, w_dt_hi.bitcast(F32), ALU.subtract).then_inc(s_wdt_split, 1)
            dve.wait_ge(s_dist_in, 1)
            dist, mask = xs[:, 8, 0:256], xs[:, 9, 0:256]
            link(v.scalar_tensor_tensor(dist, dist, -1.0, dist, ALU.mult, ALU.max))
            for m in range(8):
                head = 2 * (m // 4) + m % 2 + 4 * (m % 4 // 2)
                link(v.scalar_tensor_tensor(bias[:, m, :], dist, -(2.0 ** -(head + 1)), mask, ALU.mult, ALU.add))

            def conv(n):
                dve.wait_ge(s_pe_xbc, n + 1)
                o, a = bank(("xbc", n)), xs[:, n, :]
                link(v.tensor_scalar(a, o, conv_w[:, 3, n:n + 1], conv_b[:, n:n + 1], ALU.mult, ALU.add))
                for w in (2, 1, 0):
                    d = 3 - w
                    ins = v.scalar_tensor_tensor(a[:, d:S], o[:, 0:S - d], conv_w[:, w, n:n + 1], a[:, d:S], ALU.mult,
                                                 ALU.add)
                    if w:
                        link(ins)
                    else:
                        ins.then_inc(s_conv_read, 1)
                        dve.wait_ge(s_conv_read, n + 1)

            def silu(n):
                dve.wait_ge(s_ctanh_done, n + 1)
                v.scalar_tensor_tensor(xs[:, n, :], ctanh[:, n % 2, :], 1.0, xs[:, n, :], ALU.add, ALU.mult)\
                    .then_inc(s_silu_done, 1)
                dve.wait_ge(s_silu_done, seen(s_silu_done))

            for n in range(NX):
                conv(n)
                if n:
                    silu(n - 1)
            silu(NX - 1)

            dve.wait_ge(s_small_in, 16 * 6)
            dve.wait_ge(s_pe_dt, 2)
            flat = lambda t: t.rearrange("p i n -> p (i n)")
            v.tensor_tensor(dtv, bank("dt", 64).rearrange("p (i n) -> p i n", i=NT),
                                 dt_bias.unsqueeze(1).broadcast_to([P, NT, 16]), ALU.add)\
                .then_inc(s_dt_read, 1)
            dve.wait_ge(s_dt_read, seen(s_dt_read))
            fv, fa = flat(dtv), flat(dta)
            v.scalar_tensor_tensor(fa, fv, -1.0, fv, ALU.mult, ALU.min)\
                .then_inc(s_dt_exp_in, 1)
            dve.wait_ge(s_dt_exp_in, seen(s_dt_exp_in))
            dve.wait_ge(s_dt_exp, 2)
            s_, q_, c_ = (at(R_Z + 1024 + 64 * j, 64) for j in range(3))
            link(v.tensor_scalar(s_, fa, 2.0, None, ALU.add))
            link(v.reciprocal(s_, s_))
            link(v.tensor_tensor(s_, s_, fa, ALU.mult))
            link(v.tensor_tensor(q_, s_, s_, ALU.mult))
            link(v.tensor_scalar(c_, q_, 1.0 / 17, None, ALU.mult))
            for k in range(7, 0, -1):
                link(v.scalar_tensor_tensor(c_, c_, 1.0 / (2 * k + 1), q_, ALU.add, ALU.mult))
            link(v.scalar_tensor_tensor(c_, c_, 1.0, s_, ALU.add, ALU.mult))
            link(v.tensor_scalar(fv, fv, 0.0, None, ALU.max))
            link(v.scalar_tensor_tensor(fv, c_, 2.0, fv, ALU.mult, ALU.add))
            v.scalar_tensor_tensor(dta, dtv, -1.0, a_row.unsqueeze(1).broadcast_to([P, NT, 16]), ALU.mult, ALU.mult)\
                .then_inc(s_dta_ready, 1)
            dve.wait_ge(s_dta_ready, seen(s_dta_ready))

            sink_v = sink.rearrange("p (g f j) -> p g f j", g=2, f=2)

            def softmax_in(n):
                i, hf = divmod(n, 2)
                w = 256 if i else P
                a = att[:, n % 2]
                dve.wait_ge(s_pe_sc, n + 1)
                if n:
                    dve.wait_ge(s_pe_pt, n)
                o = bank(("sc", n), D, 2).rearrange("p (m w) -> p m w", m=4)[:, :, 0:w]
                pr = prob[:, :, 0:w]
                v.scalar_tensor_tensor(pr, o, HD ** -0.5, bias[:, 4 * hf:4 * hf + 4, 256 - w:256], ALU.mult, ALU.add)\
                    .then_inc(s_sc_read, 1)
                dve.wait_ge(s_sc_read, seen(s_sc_read))
                link(v.tensor_reduce(a[:, 0, :], pr, AX.X, ALU.max))
                two = lambda r: a[:, r, :].rearrange("p (g j) -> p g j", g=2)
                link(v.tensor_tensor(two(0), two(0), sink_v[:, :, hf, :], ALU.max))
                link(v.tensor_tensor(two(2), sink_v[:, :, hf, :], two(0), ALU.subtract))
                v.tensor_scalar(a[:, 1, :], a[:, 0, :], -1.0, None, ALU.mult)\
                    .then_inc(s_nmax_ready, 1)
                dve.wait_ge(s_nmax_ready, seen(s_nmax_ready))

            def softmax_out(n):
                w = 256 if n >= 2 else P
                a = att[:, n % 2]
                pr = prob[:, :, 0:w]
                dve.wait_ge(s_exp_done, n + 1)
                link(v.tensor_tensor(a[:, 4, :], a[:, 2, :], a[:, 3, :], ALU.add))
                link(v.reciprocal(a[:, 5, :], a[:, 4, :]))
                v.tensor_tensor(pr, pr, a[:, 5, :].unsqueeze(2).broadcast_to([P, 4, w]), ALU.mult)\
                    .then_inc(s_prob_ready, 1)
                dve.wait_ge(s_prob_ready, seen(s_prob_ready))

            def silu_z(n):
                dve.wait_ge(s_tz_done, n + 1)
                v.scalar_tensor_tensor(z_part(n), z_part(n), 1.0, bank(("z", n)).rearrange("p (i n) -> p i n", i=2),
                                       ALU.add, ALU.mult).then_inc(s_z_read, 1)
                dve.wait_ge(s_z_read, seen(s_z_read))

            for n in range(8):
                softmax_in(n)
                softmax_out(n)
                silu_z(n)

            heads = lambda t: t.rearrange("p (h e) -> p h e", e=SP)
            per_head = lambda r, n=16: r.unsqueeze(2).broadcast_to([r.shape[0], n, SP])

            def out_t(c):
                dve.wait_ge(s_pe_yT, c + 1)
                v.tensor_tensor(yT[:, c], bank(("yT", c), D, 2).rearrange("p (k t) -> p k t", k=KD),
                                     norm_w.unsqueeze(2).broadcast_to([P, KD, P]), ALU.mult)\
                    .then_inc(s_yT_read, 1)
                dve.wait_ge(s_yT_read, seen(s_yT_read))

            for c in range(NT):
                if c:
                    out_t(c - 1)
                dve.wait_ge(s_pe_cb, c + 1)
                o = bank(("cb", c), D, 2)
                link(v.tensor_copy(acs[:, 0, :], o[:, 256:272]))
                for g in range(2):
                    link(v.tensor_tensor(cbm[:, g, :], o[:, P + 512 * g:2 * P + 512 * g], upper, ALU.mult))
                if c:
                    dve.wait_ge(s_acs_exp, c)
                v.tensor_tensor(acs[:, 3, :], o[:, 272:288], acs[:, 0, :], ALU.subtract)\
                    .then_inc(s_cb_dve, 1)
                dve.wait_ge(s_cb_dve, seen(s_cb_dve))
                dve.wait_ge(s_xt_read, c + 1)
                v.tensor_tensor(heads(xdt), heads(xtok), per_head(dtv[:, c, :]), ALU.mult)\
                    .then_inc(s_xdt_ready, 1)
                dve.wait_ge(s_xdt_ready, seen(s_xdt_ready))

                def seg(q):
                    dve.wait_ge(s_pe_seg, 4 * c + q + 1)
                    if 4 * c + q >= 2:
                        dve.wait_ge(s_pe_yd, 4 * c + q - 1)
                    for m in range(4):
                        ins = v.tensor_scalar(lmat[:, q % 2, m, :], bank(("seg", c, q))[:, m * P:(m + 1) * P],
                                              acs[:, 0, 4 * q + m:4 * q + m + 1], 0.0, ALU.subtract, ALU.min)
                    ins.then_inc(s_seg_read, 1)
                    dve.wait_ge(s_seg_read, 4 * c + q + 1)

                def decayed(q):
                    dve.wait_ge(s_lmat_exp, 4 * c + q + 1)
                    v.tensor_tensor(lmat[:, q % 2], lmat[:, q % 2],
                                         cbm[:, q // 2, :].unsqueeze(1).broadcast_to([P, 4, P]), ALU.mult)\
                        .then_inc(s_m_ready, 1)
                    dve.wait_ge(s_m_ready, seen(s_m_ready))

                seg(0)
                seg(1)
                decayed(0)
                dve.wait_ge(s_acs_exp, c + 1)
                if c:
                    dve.wait_ge(s_pe_st, c)
                v.tensor_tensor(heads(xdec), heads(xdt), per_head(acs[:, 3, :]), ALU.mult)\
                    .then_inc(s_xdec_ready, 1)
                dve.wait_ge(s_xdec_ready, seen(s_xdec_ready))
                decayed(1)
                seg(2)
                seg(3)
                decayed(2)
                decayed(3)
                if c:
                    dve.wait_ge(s_pe_yT, c)
                    dve.wait_ge(s_pe_yo, c)
                    v.tensor_tensor(heads(y), heads(bank(("yo", c), D, 2)), per_head(acs[:, 1, :]), ALU.mult)\
                        .then_inc(s_yo_read, 1)
                    dve.wait_ge(s_yo_read, seen(s_yo_read))
                    link(v.tensor_tensor(heads(tmp), heads(xtok), per_head(dskip), ALU.mult))
                    link(v.tensor_tensor(y, y, tmp, ALU.add))
                else:
                    link(v.tensor_tensor(heads(y), heads(xtok), per_head(dskip), ALU.mult))
                dve.wait_ge(s_pe_yd, 4 * c + 4)
                v.tensor_tensor(y, bank(("yd", c), D, 2), y, ALU.add)\
                    .then_inc(s_yd_read, 1)
                dve.wait_ge(s_yd_read, seen(s_yd_read))
                if c < NT - 1:
                    dve.wait_ge(s_pe_st, c + 1)
                    if c:
                        for g in range(2):
                            gs = slice(64 * g, 64 * g + 64)
                            link(v.tensor_tensor(heads(state[gs]), heads(state[gs]),
                                                 per_head(acs[gs, 2, 8 * g:8 * g + 8], 8), ALU.mult))
                        v.tensor_tensor(state, bank(("st", c)), state, ALU.add)\
                            .then_inc(s_st_read, 1)
                        dve.wait_ge(s_st_read, seen(s_st_read))
                    else:
                        v.tensor_copy(state, bank(("st", c)))\
                            .then_inc(s_st_read, 1)
                        dve.wait_ge(s_st_read, seen(s_st_read))
                link(v.scalar_tensor_tensor(y, y, 0.5, sz[:, c, :], ALU.mult, ALU.mult))
                for g in range(2):
                    yg = y[:, 512 * g:512 * g + 512]
                    link(v.tensor_tensor_reduce(out=tmp[:, 0:512], in0=yg, in1=yg, scale=1.0 / 512, scalar=0.0,
                                                op0=ALU.mult, op1=ALU.add, accum_out=mv[:, g:g + 1]))
                link(v.tensor_scalar(mv[:, 2:4], mv[:, 0:2], RMS_EPS, None, ALU.add))
                rsqrt(mv[:, 4:6], mv[:, 2:4], mv[:, 6:8])
                v.tensor_tensor(y.rearrange("p (g n) -> p g n", g=2), y.rearrange("p (g n) -> p g n", g=2),
                                     mv[:, 4:6].unsqueeze(2).broadcast_to([P, 2, 512]), ALU.mult)\
                    .then_inc(s_y_ready, 1)
                dve.wait_ge(s_y_ready, seen(s_y_ready))
            out_t(NT - 1)

            dve.wait_ge(s_g_read, 2 * KD)
            dve.wait_ge(s_pe_yT, NT)
            for n in range(KD):
                dve.wait_ge(s_pe_ya, n + 1)
                v.scalar_tensor_tensor(mixT[:, n, :], gact[:, n, 0, :], 1.0, bank(("ya", n)), ALU.add, ALU.mult)\
                    .then_inc(s_ya_read, 1)
            for n in range(KD):
                dve.wait_ge(s_ya_read, n + 1)
                dve.wait_ge(s_pe_ys, n + 1)
                if n:
                    dve.wait_ge(s_mix_ready, n)
                v.scalar_tensor_tensor(gtmp[:, n % 2, :], gact[:, n, 1, :], 1.0, bank(("ys", n)), ALU.add,
                                            ALU.mult)\
                    .then_inc(s_ys_read, 1)
                dve.wait_ge(s_ys_read, n + 1)
                v.tensor_tensor(mixT[:, n, :], mixT[:, n, :], gtmp[:, n % 2, :], ALU.add)\
                    .then_inc(s_mix_ready, 1)
            dve.wait_ge(s_mix_ready, KD)
            dve.wait_ge(s_ah_ready, NT)
            dve.wait_ge(s_ln1_in, 32)
            for i in range(NT):
                for b in range(2):
                    dve.wait_ge(s_pe_mix, 2 * i + b + 1)
                    hb = h[:, i, 512 * b:512 * b + 512]
                    v.scalar_tensor_tensor(hb, bank(("mix", i, b)), 0.5, hb, ALU.mult, ALU.add)\
                        .then_inc(s_mix_read, 1)
                    dve.wait_ge(s_mix_read, seen(s_mix_read))
                normed(h[:, i, :], A1w, A1b, s_h1_ready)

            dve.wait_ge(s_pe_rt, 1)
            v.tensor_tensor(lg, bank("rt", NT * 36).rearrange("p (i n) -> p i n", i=NT),
                                 rbias.unsqueeze(1).broadcast_to([P, NT, 36]), ALU.add)\
                .then_inc(s_rt_read, 1)
            dve.wait_ge(s_rt_read, seen(s_rt_read))
            sel, oh1, oh2, em, t4, t5 = rw
            gl = lg[:, :, 0:NG]
            along = lambda r, n: r.unsqueeze(2).broadcast_to([P, NT, n])
            iotas = lambda n: iota_e[:, 0:n].unsqueeze(1).broadcast_to([P, NT, n])

            def first_max(vals, n, top, index, onehot):
                link(v.tensor_reduce(top, vals, AX.X, ALU.max))
                link(v.tensor_tensor(t5[:, :, 0:n], vals, along(top, n), ALU.is_equal))
                link(v.scalar_tensor_tensor(t5[:, :, 0:n], t5[:, :, 0:n], -64.0, iotas(n), ALU.mult, ALU.add))
                link(v.tensor_reduce(index, t5[:, :, 0:n], AX.X, ALU.min))
                link(v.tensor_scalar(index, index, 64.0, None, ALU.add))
                link(v.tensor_tensor(onehot, iotas(n), along(index, n), ALU.is_equal))

            dve.wait_ge(s_consts, 5)
            first_max(gl, NG, rv[0], rv[1], t4[:, :, 0:NG])
            link(v.tensor_tensor(gl, gl, along(rv[0], NG), ALU.subtract))
            in_g = lambda t: t.rearrange("p i (g e) -> p i g e", g=NG)
            ohg = t4[:, :, 0:NG].unsqueeze(3).broadcast_to([P, NT, NG, NPG])
            link(v.tensor_tensor(in_g(em), in_g(lg[:, :, NG:36]), ohg, ALU.mult))
            link(v.tensor_scalar(t4[:, :, 0:NG], t4[:, :, 0:NG], -1.0, -NEG, ALU.add, ALU.mult))
            link(v.tensor_tensor(in_g(em), in_g(em), ohg, ALU.add))
            first_max(em, NE, rv[3], rv[5], oh1)
            link(v.scalar_tensor_tensor(em, oh1, -3e38, em, ALU.mult, ALU.add))
            first_max(em, NE, rv[4], rv[6], oh2)
            v.tensor_tensor(rv[4], rv[4], rv[3], ALU.subtract)\
                .then_inc(s_rt_exp_in, 1)
            dve.wait_ge(s_rt_exp_in, seen(s_rt_exp_in))
            v.tensor_tensor(sel, oh1, oh2, ALU.add)\
                .then_inc(s_sel_ready, 1)
            dve.wait_ge(s_sel_ready, seen(s_sel_ready))
            dve.wait_ge(s_rt_exp, 1)
            link(v.tensor_reduce(rv[2], gl, AX.X, ALU.add))
            link(v.scalar_tensor_tensor(rv[7], rv[4], 1.0, rv[2], ALU.add, ALU.mult))
            link(v.reciprocal(rv[7], rv[7]))
            link(v.tensor_scalar(rv[8], rv[7], 0.5, None, ALU.mult))
            link(v.tensor_tensor(rv[9], rv[8], rv[4], ALU.mult))

            def ple_sum(n):
                s = n // NT
                dve.wait_ge(s_pe_pl, n + 1)
                v.tensor_tensor(pgt[:, n % 4, :], bank(("pl", n))[:, 0:PS], bple[:, PS * s:PS * (s + 1)], ALU.add)\
                    .then_inc(s_pg_read, 1)
                dve.wait_ge(s_pg_read, seen(s_pg_read))

            def ple_out(n):
                s, i = divmod(n, NT)
                dve.wait_ge(s_pg_tanh, n + 1)
                v.scalar_tensor_tensor(pgt[:, n % 4, :], pgt[:, n % 4, :], 1.0, bank(("pl", n))[:, PS:2 * PS], ALU.add,
                                       ALU.mult).then_inc(s_pp_read, 1)
                dve.wait_ge(s_pp_read, seen(s_pp_read))
                dve.wait_ge(s_ah1_ready, i + 1)
                hs = slice(PS * s, PS * (s + 1))
                v.scalar_tensor_tensor(sz[:, i, hs], pgt[:, n % 4, :], 0.5, sz[:, i, hs], ALU.mult, ALU.add)\
                    .then_inc(s_base_ready, 1)
                dve.wait_ge(s_base_ready, seen(s_base_ready))

            dve.wait_ge(s_bple_in, 16)
            for n in range(RANKS_AFTER + 1):
                ple_sum(n)

            dve.wait_ge(s_pe_rk, 1)
            rk = bank("rk", 160)
            rank, count = t4, cnt[0]
            link(v.tensor_copy(rank, rk[:, 0:128].rearrange("p (i n) -> p i n", i=NT)))
            v.tensor_copy(count, rk[:, 128:160])\
                .then_inc(s_rk_read, 1)
            dve.wait_ge(s_rk_read, seen(s_rk_read))
            more, csum = cnt[1], [cnt[2], cnt[3]]
            link(v.tensor_scalar(more, count, float(CAP), None, ALU.is_gt))
            for b in range(2, S // CAP):
                link(v.scalar_tensor_tensor(more, count, float(CAP * b), more, ALU.is_gt, ALU.add))
            link(v.tensor_copy(csum[0], more))
            a = 0
            for d in (1, 2, 4, 8, 16):
                link(v.tensor_copy(csum[1 - a][:, 0:d], csum[a][:, 0:d]))
                link(v.tensor_tensor(csum[1 - a][:, d:NE], csum[a][:, d:NE], csum[a][:, 0:NE - d], ALU.add))
                a = 1 - a
            csum = csum[a]
            first_row, jump = cnt[4], cnt[5]
            link(v.tensor_scalar(first_row, iota_e, float(CAP), None, ALU.mult))
            link(v.tensor_tensor(jump, csum, more, ALU.subtract))
            link(v.tensor_scalar(jump, jump, float(NE - 1), float(CAP), ALU.add, ALU.mult))
            link(v.tensor_tensor(jump, jump, first_row, ALU.subtract))
            per_e = lambda r: r.unsqueeze(1).broadcast_to([P, NT, NE])
            link(v.tensor_scalar(t5, rank, float(CAP), None, ALU.is_ge))
            link(v.tensor_tensor(t5, t5, per_e(jump), ALU.mult))
            link(v.tensor_tensor(rank, rank, t5, ALU.add))
            link(v.tensor_tensor(rank, rank, per_e(first_row), ALU.add))
            rows2 = rowsU[:, :].rearrange("p (i c) -> p i c", c=2)
            for c, oh in ((0, oh1), (1, oh2)):
                link(v.tensor_tensor(t5, rank, oh, ALU.mult))
                link(v.tensor_reduce(rowf[:, :, c], t5, AX.X, ALU.add))
                v.tensor_copy(rows2[:, :, c], rowf[:, :, c]).then_inc(s_rows_ready, 1)
                dve.wait_ge(s_rows_ready, seen(s_rows_ready))
            for j in range(EXTRA + 1):
                link(v.tensor_scalar(em[:, 0, :], csum, float(j), 0.0, ALU.is_le, ALU.add, accum_out=ctlf[:, j:j + 1]))
            link(v.tensor_scalar(ctlf[:, 0:EXTRA + 1], ctlf[:, 0:EXTRA + 1], float(NE - 1), None, ALU.min))
            pair_of = em[:, 0, 0:MORE_PAIRS]
            link(v.tensor_scalar(pair_of, iota_e[:, 0:MORE_PAIRS], 2.0, csum[:, NE - 1:NE], ALU.mult, ALU.subtract))
            link(v.tensor_scalar(pair_of, pair_of, 0.0, 0.0, ALU.is_lt, ALU.add, accum_out=ctlf[:, EXTRA + 1:EXTRA + 2]))
            v.tensor_copy(ctl[:, :], ctlf)\
                .then_inc(s_ctl_ready, 1)
            dve.wait_ge(s_ctl_ready, seen(s_ctl_ready))

            columns = iota_r.unsqueeze(1).broadcast_to([P, NT, P])
            rows_of = lambda c: rowf[:, :, c:c + 1].broadcast_to([P, NT, P])

            def tokens_rows(q, buf, fetched, rebased):
                if fetched is not None:
                    dve.wait_ge(s_xT_mm, fetched)
                if rebased is not None:
                    dve.wait_ge(s_rowf_moved, rebased)
                    dve.wait_ge(s_onehot_ready, q)
                o = onehot[:, buf]
                v.tensor_tensor(o, columns, rows_of(0), ALU.is_equal).then_inc(s_onehot_a, 1)
                v.tensor_tensor(second, columns, rows_of(1), ALU.is_equal).then_inc(s_onehot_a, 1)
                dve.wait_ge(s_onehot_a, q * 2 + 2)
                v.tensor_tensor(o, o, second, ALU.add).then_inc(s_onehot_ready, 1)
                v.tensor_scalar(rowf, rowf, -2.0 * CAP, None, ALU.add).then_inc(s_rowf_moved, 1)

            tokens_rows(0, 0, None, None)
            tokens_rows(1, 1, None, 1)
            for n in range(4 * NT):
                if RANKS_AFTER < n:
                    ple_sum(n)
                if n >= RANKS_AFTER:
                    ple_out(n - RANKS_AFTER)
            for n in range(4 * NT - RANKS_AFTER, 4 * NT):
                ple_out(n)

            def hidden(p, u):
                dve.wait_ge(s_tanh_sb, p + 1)
                hg, hu = psum[:, u % 2, 0:FF], psum[:, u % 2, FF:2 * FF]
                v.scalar_tensor_tensor(eact[:, u % 2, :], eth[:, u % 2, :], 1.0, hg, ALU.add, ALU.mult)\
                    .then_inc(s_eact_a, 1)
                dve.wait_ge(s_eact_a, p + 1)
                v.tensor_tensor(eact[:, u % 2, :], eact[:, u % 2, :], hu, ALU.mult).then_inc(s_eact_sb, 1)

            def out_half(p, stores, u):
                dve.wait_ge(s_y_mm, p + 1)
                if not (isinstance(stores, int) and stores == 0):
                    dve.wait_ge(y_st[u % 2], stores)
                v.tensor_copy(eout[:, u % 2, 512:1024], psum[:, 5, :]).then_inc(s_y_dve, 1)

            def step(e4, u):
                p = e4 * 4 + u
                hidden(p, u)
                tokens_rows(p + 2, u % 2, p * 2 + 2, p + 2)
                if not (isinstance(e4, int) and u == 0):
                    out_half(p - 1, e4 * 32 + 16 * ((u - 1) // 2), (u - 1) % 4)

            for u in range(4):
                step(0, u)
            with dve.Fori(1, PAIRS // 4) as e4:
                for u in range(4):
                    step(e4, u)
            out_half(PAIRS - 1, 16 * (PAIRS // 2 - 1), 3)
            dve.wait_ge(s_rowf_moved, PAIRS + 2)
            v.tensor_scalar(rowf, rowf, 4.0 * CAP, None, ALU.add).then_inc(s_rowf_moved, 1)
            pairs = dve.value_load(ctl[0:1, EXTRA + 1:EXTRA + 2], min_val=0, max_val=MORE_PAIRS)
            with dve.Fori(0, MORE_PAIRS) as j:
                with dve.If(pairs > j):
                    tokens_rows(j + PAIRS + 2, 0, j * 2 + 2 * PAIRS + 2, j + PAIRS + 3)
                    hidden(j + PAIRS, 0)
                    out_half(j + PAIRS, j * 16 + 16 * (PAIRS // 2), 0)
                dve.nop()

            for i in range(NT):
                dve.wait_ge(y_gath[i], 32)
                x = sz[:, i, :]
                for c in range(2):
                    v.scalar_tensor_tensor(x, ygat[:, i, c, :], rv[8 + c][:, i:i + 1], x, ALU.mult, ALU.add)\
                        .then_inc(s_combined, 1)
                    dve.wait_ge(s_combined, 2 * i + c + 1)
                if i == NT - 1:
                    tile_stats(x, i)
            dve.wait_ge(s_act_stats, 1 + NT - 1)
            dve.wait_ge(s_ln2_in, 32)
            tiles_normed(sz, A1w, A1b, s_fin_ready)


_INS = ["x", "p", "ln0_w", "ln0_b", "w_in", "b_gate", "conv_w", "conv_b", "dt_bias", "a_log", "d_skip", "ssd_norm_w",
        "sinks", "w_out_attn", "w_out_ssd", "w_out", "ln1_w", "ln1_b", "w_router_group", "b_router_group",
        "w_router_expert", "b_router_expert", "w_exp_gate", "w_exp_up", "w_exp_down", "w_ple", "w_ple_gate",
        "b_ple_gate", "ln2_w", "ln2_b"]


def kernel(**inputs):
    import numpy as _np
    import concourse.bacc as _bacc
    from concourse import mybir as _mybir
    from concourse.bass_utils import run_bass_kernel_spmd as _run

    nc = _bacc.Bacc("TRN2", target_bir_lowering=False, num_devices=1)
    arrays, aps = {}, {}
    for name in _INS:
        a = _np.ascontiguousarray(inputs[name])
        arrays[f"in_{name}_dram"] = a
        aps[name] = nc.dram_tensor(f"in_{name}_dram", a.shape, _mybir.dt.from_np(a.dtype), kind="ExternalInput").ap()
    out = nc.dram_tensor("out_0_dram", (1, S, D), F32, kind="ExternalOutput").ap()
    block_kernel(nc, aps, out)
    r = _run(nc, [arrays], core_ids=[0])
    return r.results[0]["out_0_dram"]
```
